# Optimizing a Trainium2 kernel written in Bass

```python
import math
import jax, jax.numpy as jnp
from jax import lax
import numpy as np

D_MODEL = 1024
BATCH = 1
SEQ = 256
DEPTH = 1

CHUNK = 64
D_MIX = D_MODEL
D_SSM = D_MIX // 2
SSM_GROUP = 16
N_SSM_GROUPS = D_SSM // SSM_GROUP
SSM_STATE = 64
D_ATT = D_MIX - D_SSM
HEAD_DIM = 64
N_HEADS = D_ATT // HEAD_DIM
Q_BLOCK = 128
N_EXPERTS = 64
TOP_K = 8
N_EXPERT_GROUPS = 8
TOPK_GROUPS = 4
D_EXPERT = 256
D_SHARED = 256
ROUTED_SCALE = 2.5
TOKEN_BLOCK = 128
EPS = 1e-6
DT_MIN = 1e-3
DT_MAX = 1e-1
LAMBDA_RE_MAX = -1e-4

kernel_name = "hymba_s5_stickbreak_moe_block"

def rms_norm(x, g):
    xf = x.astype(jnp.float32)
    y = xf * lax.rsqrt(jnp.mean(xf * xf, axis=-1, keepdims=True) + EPS)
    return (y * g.astype(jnp.float32)).astype(x.dtype)

def s5_mixer(u, lam_re, lam_im, b_re, b_im, c_re, c_im, d_skip, log_step, w_glu, b_glu):
    f32 = jnp.float32
    bsz, seq, _ = u.shape
    uf = u.astype(f32)
    lam = lax.complex(jnp.minimum(lam_re.astype(f32), LAMBDA_RE_MAX), lam_im.astype(f32))
    step = jnp.exp(log_step.astype(f32))[:, None]
    lam_bar = jnp.exp(lam * step)
    b_mat = lax.complex(b_re.astype(f32), b_im.astype(f32))
    b_bar = ((lam_bar - 1.0) / lam)[..., None] * b_mat
    c_mat = lax.complex(c_re.astype(f32), c_im.astype(f32))

    n_chunks = seq // CHUNK
    u_c = uf.reshape(bsz, n_chunks, CHUNK, N_SSM_GROUPS, SSM_GROUP).transpose(1, 2, 0, 3, 4)
    a_chunk = jnp.broadcast_to(lam_bar, (CHUNK, bsz, N_SSM_GROUPS, SSM_STATE))

    def combine(left, right):
        a_l, b_l = left
        a_r, b_r = right
        return a_r * a_l, a_r * b_l + b_r

    def chunk_step(h0, u_blk):
        bu = jnp.einsum('cbgh,gph->cbgp', u_blk.astype(jnp.complex64), b_bar)
        bu = bu.at[0].add(lam_bar * h0)
        _, states = lax.associative_scan(combine, (a_chunk, bu), axis=0)
        y = jnp.einsum('cbgp,ghp->cbgh', states, c_mat).real
        return states[-1], y

    h0 = jnp.zeros((bsz, N_SSM_GROUPS, SSM_STATE), jnp.complex64)
    _, y = lax.scan(chunk_step, h0, u_c)
    y = y.transpose(2, 0, 1, 3, 4).reshape(bsz, seq, D_SSM)
    y = jax.nn.gelu(y + d_skip.astype(f32) * uf)
    y = y * jax.nn.sigmoid(y @ w_glu.astype(f32) + b_glu.astype(f32))
    return y.astype(u.dtype)

def stick_breaking_attention(q, k, v):
    f32 = jnp.float32
    bsz, seq, _, _ = q.shape
    qh = q.astype(f32).transpose(0, 2, 1, 3)
    kh = k.astype(f32).transpose(0, 2, 1, 3)
    vh = v.astype(f32).transpose(0, 2, 1, 3)
    scale = 1.0 / math.sqrt(HEAD_DIM)
    outs = []
    for blk in range(seq // Q_BLOCK):
        start = blk * Q_BLOCK
        end = start + Q_BLOCK
        qb = qh[:, :, start:end]
        kp = kh[:, :, :end]
        vp = vh[:, :, :end]
        z = jnp.einsum('bhqd,bhkd->bhqk', qb, kp) * scale
        t_pos = start + jnp.arange(Q_BLOCK)[:, None]
        s_pos = jnp.arange(end)[None, :]
        mask = s_pos < t_pos
        log_1m = jnp.where(mask, jax.nn.log_sigmoid(-z), 0.0)
        after = lax.cumsum(log_1m, axis=3, reverse=True) - log_1m
        w = jnp.where(mask, jnp.exp(jax.nn.log_sigmoid(z) + after), 0.0)
        outs.append(jnp.einsum('bhqk,bhkd->bhqd', w, vp))
    o = jnp.concatenate(outs, axis=2)
    return o.transpose(0, 2, 1, 3).reshape(bsz, seq, D_ATT)

def swiglu(h, w1, w3, w2):
    return (jax.nn.silu(h @ w1) * (h @ w3)) @ w2

def moe_ffn(h, w_router, router_bias, e_w1, e_w3, e_w2, s_w1, s_w3, s_w2):
    f32 = jnp.float32
    bsz, seq, d = h.shape
    ht = h.reshape(-1, d)
    n_tok = ht.shape[0]
    scores = jax.nn.sigmoid((ht @ w_router).astype(f32))
    biased = scores + router_bias.astype(f32)
    grp = biased.reshape(n_tok, N_EXPERT_GROUPS, N_EXPERTS // N_EXPERT_GROUPS)
    grp_score = jnp.sum(lax.top_k(grp, 2)[0], axis=-1)
    _, grp_idx = lax.top_k(grp_score, TOPK_GROUPS)
    grp_mask = jnp.sum(jax.nn.one_hot(grp_idx, N_EXPERT_GROUPS, dtype=f32), axis=1)
    expert_mask = jnp.repeat(grp_mask, N_EXPERTS // N_EXPERT_GROUPS, axis=1)
    sel = jnp.where(expert_mask > 0, biased, -jnp.inf)
    _, idx = lax.top_k(sel, TOP_K)
    w = jnp.take_along_axis(scores, idx, axis=1)
    w = w / jnp.sum(w, axis=-1, keepdims=True) * ROUTED_SCALE
    gate = jnp.sum(jax.nn.one_hot(idx, N_EXPERTS, dtype=f32) * w[..., None], axis=1)

    def expert_block(args):
        xb, gb = args
        a = jnp.einsum('td,edf->tef', xb, e_w1)
        b = jnp.einsum('td,edf->tef', xb, e_w3)
        act = jax.nn.silu(a) * b * gb.astype(xb.dtype)[..., None]
        return jnp.einsum('tef,efd->td', act, e_w2)

    routed = lax.map(expert_block, (ht.reshape(-1, TOKEN_BLOCK, d),
                                    gate.reshape(-1, TOKEN_BLOCK, N_EXPERTS)))
    routed = routed.reshape(n_tok, d)
    shared = swiglu(ht, s_w1, s_w3, s_w2)
    return (routed + shared).reshape(bsz, seq, d)

def setup_inputs(seed: int = 0) -> dict:
    key = jax.random.key(seed)
    ks = jax.random.split(key, 32)
    f32 = jnp.float32
    L, G, P, H = DEPTH, N_SSM_GROUPS, SSM_STATE, SSM_GROUP
    nrm = lambda k, shape, s: jax.random.normal(k, shape, f32) * s
    gain = lambda k, shape: 1.0 + 0.01 * jax.random.normal(k, shape, f32)
    d_in = D_SSM + 3 * D_ATT
    return {
        "x": jax.random.normal(ks[0], (BATCH, SEQ, D_MODEL), f32),
        "g_mix": gain(ks[1], (L, D_MODEL)),
        "w_in": nrm(ks[2], (L, D_MODEL, d_in), D_MODEL ** -0.5),
        "lam_re": -0.5 + 0.01 * jax.random.normal(ks[3], (L, G, P), f32),
        "lam_im": jnp.pi * jnp.arange(P, dtype=f32)[None, None, :]
                  + 0.01 * jax.random.normal(ks[4], (L, G, P), f32),
        "b_re": nrm(ks[5], (L, G, P, H), (2.0 * H) ** -0.5),
        "b_im": nrm(ks[6], (L, G, P, H), (2.0 * H) ** -0.5),
        "c_re": nrm(ks[7], (L, G, H, P), (2.0 * P) ** -0.5),
        "c_im": nrm(ks[8], (L, G, H, P), (2.0 * P) ** -0.5),
        "d_skip": jax.random.normal(ks[9], (L, D_SSM), f32),
        "log_step": jax.random.uniform(ks[10], (L, G), f32, math.log(DT_MIN), math.log(DT_MAX)),
        "w_glu": nrm(ks[11], (L, D_SSM, D_SSM), D_SSM ** -0.5),
        "b_glu": nrm(ks[12], (L, D_SSM), 0.01),
        "g_q": gain(ks[13], (L, HEAD_DIM)),
        "g_k": gain(ks[14], (L, HEAD_DIM)),
        "g_out_ssm": gain(ks[15], (L, D_SSM)),
        "g_out_att": gain(ks[16], (L, D_ATT)),
        "w_out": nrm(ks[17], (L, D_MIX, D_MODEL), D_MIX ** -0.5),
        "g_ffn": gain(ks[18], (L, D_MODEL)),
        "w_router": nrm(ks[19], (L, D_MODEL, N_EXPERTS), D_MODEL ** -0.5),
        "router_bias": nrm(ks[20], (L, N_EXPERTS), 0.01),
        "e_w1": nrm(ks[21], (L, N_EXPERTS, D_MODEL, D_EXPERT), D_MODEL ** -0.5),
        "e_w3": nrm(ks[22], (L, N_EXPERTS, D_MODEL, D_EXPERT), D_MODEL ** -0.5),
        "e_w2": nrm(ks[23], (L, N_EXPERTS, D_EXPERT, D_MODEL), D_EXPERT ** -0.5),
        "s_w1": nrm(ks[24], (L, D_MODEL, D_SHARED), D_MODEL ** -0.5),
        "s_w3": nrm(ks[25], (L, D_MODEL, D_SHARED), D_MODEL ** -0.5),
        "s_w2": nrm(ks[26], (L, D_SHARED, D_MODEL), D_SHARED ** -0.5),
    }

def reference(x, g_mix, w_in, lam_re, lam_im, b_re, b_im, c_re, c_im, d_skip, log_step,
              w_glu, b_glu, g_q, g_k, g_out_ssm, g_out_att, w_out, g_ffn, w_router,
              router_bias, e_w1, e_w3, e_w2, s_w1, s_w3, s_w2):
    bsz, seq, _ = x.shape
    h = x
    for l in range(DEPTH):
        hn = rms_norm(h, g_mix[l])
        proj = hn @ w_in[l]
        u, q, k, v = jnp.split(proj, [D_SSM, D_SSM + D_ATT, D_SSM + 2 * D_ATT], axis=-1)
        y_ssm = s5_mixer(u, lam_re[l], lam_im[l], b_re[l], b_im[l], c_re[l], c_im[l],
                         d_skip[l], log_step[l], w_glu[l], b_glu[l])
        q = rms_norm(q.reshape(bsz, seq, N_HEADS, HEAD_DIM), g_q[l])
        k = rms_norm(k.reshape(bsz, seq, N_HEADS, HEAD_DIM), g_k[l])
        v = v.reshape(bsz, seq, N_HEADS, HEAD_DIM)
        y_att = stick_breaking_attention(q, k, v).astype(h.dtype)
        mixed = jnp.concatenate([rms_norm(y_ssm, g_out_ssm[l]),
                                 rms_norm(y_att, g_out_att[l])], axis=-1)
        h = h + mixed @ w_out[l]
        h = h + moe_ffn(rms_norm(h, g_ffn[l]), w_router[l], router_bias[l], e_w1[l],
                        e_w3[l], e_w2[l], s_w1[l], s_w3[l], s_w2[l])
    return h


_drawn_inputs = setup_inputs


def setup_inputs(seed=0):
    import zlib

    import numpy as np

    out = dict(_drawn_inputs(seed))
    spreads = {}
    factors = {}
    for name, (base, spread) in spreads.items():
        noise = np.random.default_rng([zlib.crc32(name.encode()), seed]).standard_normal(out[name].shape)
        drawn = base * np.exp(spread * noise) if base else spread * noise
        out[name] = __import__('jax').numpy.asarray(drawn.astype(out[name].dtype))
    for name, factor in factors.items():
        out[name] = (out[name] * factor).astype(out[name].dtype)
    return out
```

```python
from contextlib import ExitStack

import numpy as np

import concourse.bass as bass
from concourse import mybir

FP32 = mybir.dt.float32
BF16 = mybir.dt.bfloat16
I32 = mybir.dt.int32
ALU = mybir.AluOpType
ACT = mybir.ActivationFunctionType
AX = mybir.AxisListType

D = 1024
T = 256
DS = 512
KT = D // 128
G, P, H = 32, 64, 16
PR = G // 2
L = 8
C = T // L
NH, DH = 8, 64
E, TOPK, NG, GE, TOPG = 64, 8, 8, 8, 4
F = 256
SLOTS = 64
EB = 8
NB = E // EB
NPAIR = EB // 2
EPS = 1e-6
ROUTED_SCALE = 2.5
BIG = 3.0e38
TWO_PI = 2 * np.pi
PI_DOWN = 3.1415925
ROUND_MAGIC = 12582912.0
RSQRT_MAGIC = 1597463007.0


def two_pi_parts():
    parts, rest = [], TWO_PI
    for bits in (10, 10, 24):
        scale = 2.0 ** (bits - 1 - np.floor(np.log2(abs(rest))))
        part = float(np.round(rest * scale) / scale)
        parts.append(float(np.float32(part)))
        rest -= parts[-1]
    return parts


def build(nc, I, out):
    ctx = ExitStack()
    with ctx:
        def sb(name, words, dt=FP32, parts=128):
            return ctx.enter_context(nc.sbuf_tensor(name, [parts, words], dt))

        def sem(name):
            return ctx.enter_context(nc.semaphore(name))

        SLOT_W = 3 * 2048
        ring = sb("ring", 4 * SLOT_W)
        wreg = sb("wreg", 16384)
        acc = sb("acc", 2048)
        reg_a = sb("reg_a", 2048)
        reg_b = sb("reg_b", 2048)
        reg_c = sb("reg_c", 3072)
        reg_d = sb("reg_d", 2304)
        ident = sb("ident", 128)
        small = sb("small", 600)
        ps = [ctx.enter_context(nc.psum_tensor(f"bank{i}", [128, 512], FP32)) for i in range(8)]

        taken = {}

        def piece(region, words, size):
            at = taken.get(words, 0)
            taken[words] = at + size
            assert at + size <= region.shape[1], (words, at + size)
            return region[:, at:at + size]

        Et = [piece(ring, "s5", 2048) for _ in range(2)]
        EtV = [e.rearrange("p (r j h) -> p r j h", r=PR, j=L) for e in Et]
        Gm = [piece(ring, "s5", PR * 9 * H) for _ in range(2)]
        GmV = [g.rearrange("p (r j h) -> p r j h", r=PR, j=9) for g in Gm]
        Tm = piece(ring, "s5", G * 128)
        TmV = Tm.rearrange("p (g n) -> p g n", g=G)
        Em = piece(ring, "s5", PR * 2 * 128)
        EmV = Em.rearrange("p (r i s) -> p r i s", r=PR, i=2)
        U = piece(ring, "s5", G * C)
        UV = U.rearrange("p (g c) -> p g c", g=G)
        uev = piece(ring, "s5", 1024)
        par = lambda n: piece(ring, "s5", n)
        lr, li, ls, mag, th, cosv, sinv, lbr, lbi, t1, t2, t3, t4, cor, coi, den, e8r, e8i, rho = (
            par(PR) for _ in range(19))
        PW = [par(9 * PR).rearrange("p (k r) -> p k r", k=9) for _ in range(2)]
        Braw = [par(PR * H).rearrange("p (r h) -> p r h", r=PR) for _ in range(2)]
        Bbar = [par(PR * H).rearrange("p (r h) -> p r h", r=PR) for _ in range(2)]
        Ct = [par(PR * H).rearrange("p (r h) -> p r h", r=PR) for _ in range(2)]
        rot = [par(33 * PR).rearrange("p (c r) -> p c r", c=33) for _ in range(2)]
        dT = par(G)
        negtri = par(128)
        negones = par(128)
        prm = par(128)
        prm2 = par(128)
        prm3 = par(128)
        ls2 = par(2)
        dS = par(H)
        Craw = [Em[:, 512 * i:512 * i + 512].rearrange("p (b n) -> p b n", b=4) for i in range(2)]
        Kv = ring[0:H, 0:4096].rearrange("p (g n) -> p g n", g=G)
        Kdiag = par(G * H)[0:H, :].rearrange("p (g h) -> p g h", g=G)
        scan_t = [Em[:, 512 * i:512 * i + 512] for i in range(8)]
        rtmp = [uev[:, 256 * i:256 * i + 256] for i in range(4)]
        ygel = reg_d[:, 0:1024]
        ytok = reg_d[:, 1024:2048]

        hnT = reg_a[:, :].rearrange("p (k t) -> p k t", k=KT)
        hnC = reg_d[:, 0:2048].rearrange("p (k t) -> p k t", k=KT)
        mixT = hnT
        hn2T = hnT
        xs = reg_b[:, :].rearrange("p (a d) -> p a d", a=2)
        qk = reg_b[:, :].rearrange("p (a n) -> p a n", a=2)
        hs = reg_b[:, :].rearrange("p (a k m) -> p a k m", a=2, k=KT)
        v = reg_c[:, 0:1024].rearrange("p (a n) -> p a n", a=2)
        qT = reg_c[:, 1024:2048].rearrange("p (m t) -> p m t", m=4)
        kT = reg_c[:, 2048:3072].rearrange("p (m t) -> p m t", m=4)
        parts = [reg_c[:, 1024 * i:1024 * i + 1024].bitcast(BF16).rearrange("p (a k m) -> p a k m", a=2, k=KT)
                 for i in range(3)]
        sqa = reg_b[:, 0:1024].rearrange("p (m t) -> p m t", m=4)
        sqs = reg_b[:, 1024:2048].rearrange("p (m t) -> p m t", m=4)
        sigt = reg_c[:, 0:1024].rearrange("p (m t) -> p m t", m=4)
        attE = [reg_d[:, 1152 * i:1152 * i + 384] for i in range(2)]
        attL = [reg_d[:, 1152 * i + 384:1152 * i + 768] for i in range(2)]
        attW = [reg_d[:, 1152 * i + 768:1152 * i + 1152] for i in range(2)]
        sqtmp = reg_d[:, 0:2048]
        rest = reg_d[:, 0:2048].rearrange("p (a k m) -> p a k m", a=2, k=KT)
        Pm = reg_d[:, 0:512].bitcast(BF16).rearrange("p (a e s) -> p a e s", a=2, e=EB)
        PG = reg_d[:, 512:1536].rearrange("p (a e s) -> p a e s", a=2, e=EB)
        GmT = reg_a[:, 0:1024].rearrange("p (n a t) -> p n a t", n=NPAIR, a=2)
        silu_o = [reg_b[:, 256 * i:256 * i + 256] for i in range(2)]
        act_o = [reg_b[:, 512 + 256 * i:768 + 256 * i] for i in range(2)]
        actT = [reg_b[:, 1024 + 256 * i:1280 + 256 * i].rearrange("p (j s) -> p j s", j=2) for i in range(2)]

        w_in = wreg[:, :].rearrange("p (n k c) -> p n k c", n=4, k=KT)
        w_out = wreg[:, 0:8192].rearrange("p (k n) -> p k n", k=KT)
        w_glu = wreg[:, 8192:10240].rearrange("p (k n) -> p k n", k=4)
        sh13 = wreg[:, 10240:14336].rearrange("p (w k f) -> p w k f", w=2, k=KT)
        sh2 = wreg[:, 14336:16384].rearrange("p (j n) -> p j n", j=2)
        xTg = wreg[:, 0:4096].rearrange("p (k s) -> p k s", k=KT)
        ysb = wreg[:, 4096:8192].rearrange("p (n d) -> p n d", n=NPAIR)
        ringV = ring[:, :].rearrange("p (s w) -> p s w", s=4)
        slot13 = [ringV[:, s, 0:4096].rearrange("p (w k f) -> p w k f", w=2, k=KT) for s in range(4)]
        slot2 = [ringV[:, s, 4096:6144].rearrange("p (j n) -> p j n", j=2) for s in range(4)]

        rt = lambda n: piece(rt_region, "rt", n)
        rt_region = wreg[:, 8192:10240]
        w_rt = rt(KT * E).rearrange("p (k e) -> p k e", k=KT)
        two = lambda w: w.rearrange("p (a e) -> p a e", a=2)
        scores, biased, sel, repl, mask, gate_r = (two(rt(2 * E)) for _ in range(6))
        m8 = rt(2 * NG * 8).rearrange("p (a g x) -> p a g x", a=2, g=NG)
        gs = two(rt(2 * NG))
        gt_c = rt(2 * NG * NG).rearrange("p (a i j) -> p a i j", a=2, i=NG)
        eq_c = rt(2 * NG * NG).rearrange("p (a i j) -> p a i j", a=2, i=NG)
        rk1, gmask = two(rt(2 * NG)), two(rt(2 * NG))
        top8 = two(rt(16))
        mask_b = rt(E).bitcast(BF16).rearrange("p (a e) -> p a e", a=2)
        tri_b = rt(64).bitcast(BF16)
        ones_b = rt(64).bitcast(BF16)
        bias_bc = rt(E)
        lower = rt(64).rearrange("p (i j) -> p i j", i=NG)

        sm = lambda n: piece(small, "small", n)
        g_mix, g_ffn = sm(KT), sm(KT)
        gq, gk = sm(1), sm(1)
        g_os, g_oa, b_glu = sm(4), sm(4), sm(4)
        ones_col = sm(1)
        ssx, nm, ny, nt, nh = sm(2), sm(32), sm(32), sm(32), sm(32)
        ssqk = sm(32)
        sso = sm(4)
        rso = sm(4)
        iota = sm(SLOTS)
        PADE = E + EB
        pos = sm(2 * PADE).rearrange("p (a e) -> p a e", a=2)
        gate = sm(2 * PADE).rearrange("p (a e) -> p a e", a=2)
        passes = small[:, taken["small"]:taken["small"] + 1].bitcast(I32)
        taken["small"] += 1
        mx = sm(2)
        gsum = sm(2)
        pos_b, gate_b = sm(2 * EB), sm(2 * EB)
        pos_b, gate_b = (w.rearrange("p (a e) -> p a e", a=2) for w in (pos_b, gate_b))

        names = """x_in gm_in params_in gains_in b_in c_in wu_in wq_in wk_in wv_in wo_in glu_in sh_in wr_in bias_in
        ident_ready negtri_ready iota_ready trib_ready onesb_ready lower_ready
        ones_ready ssx_ready xs_ready xT_even xT_odd xt_done spread_ready par_t_done par_evac ct_evac
        step_ready a_ready th_ready exps_ready u_done u_evac U_ready qk_done qk_evac qk_normed
        v_done v_evac gq_ready qkT_done qkT_act qkT_dve
        Et_ready Bbar_ready G_ready E_done E_act E_dve K_done K_evac diag_ready T_zero T_dma V_done S_ready
        z_done zc_ready e_ready ln_ready sp_ready L_ready zi_done w_ready wm_ready pv_done pv_act
        y5_done y5_gelu ytok_ready yT_done yT_act yT_dve zg_done sig_ready sqs_ready ys_ready sso_done sso_evac
        opa_done ops_done h_ready ssh_ready hs_ready hT_done hT_act hT_dve p1_ready rest_ready p2_ready
        parts_ready lg_done scores_ready mask_ready pos_done route_ready pbuilt
        slots_chain pos_moved dve_chain pool_chain sh_up sh_silu sh_act sh_T sh_actT shd_done shared_added
        gath_done xa xd gt_done gm_act gm_dve up_done silu_done act_ready t_done actT_ready down_done ya yd
        comb_mm comb_done out_done""".split()
        S = {n: sem(n) for n in names}
        w13_in = [sem(f"w13_in{s}") for s in range(4)]
        w2_in = [sem(f"w2_in{s}") for s in range(4)]

        def chunked(ap):
            return ap.rearrange("p (c q a) -> p a q c", q=4, a=2)

        block = ctx.enter_context(nc.Block())

        @block.sync
        def _(sp):
            xv = I["x"].rearrange("o (c q a) d -> q c (o a d)", q=4, a=2)
            for q in range(4):
                sp.dma_start(acc[32 * q:32 * q + 32, :], xv[q]).then_inc(S["x_in"], 16)
            sp.dma_start(g_mix, I["g_mix"].rearrange("o (p k) -> (o p) k", k=KT)).then_inc(S["gm_in"], 16)
            wi = I["w_in"].rearrange("o (p k) (n c) -> n (o p) k c", k=KT, n=4)
            sp.dma_start(w_in[:, 0], wi[0]).then_inc(S["wu_in"], 16)
            lam = "o (r i) p -> (o r) (i p)"
            sp.dma_start(prm[0:PR, :], I["lam_re"].rearrange(lam, i=2)).then_inc(S["params_in"], 16)
            sp.dma_start(prm2[0:PR, :], I["lam_im"].rearrange(lam, i=2)).then_inc(S["params_in"], 16)
            sp.dma_start(ls2[0:PR, :], I["log_step"].rearrange("o (r i) -> (o r) i", i=2)).then_inc(S["params_in"], 16)
            sp.dma_start(dS[0:G, :], I["d_skip"].rearrange("o (g h) -> (o g) h", h=H)).then_inc(S["params_in"], 16)
            for i, n in enumerate(("c_re", "c_im")):
                cv = I[n].rearrange("o (b g) h p -> (o g h) b p", b=4)
                for half in range(2):
                    sp.dma_start(Craw[i][:, :, 64 * half:64 * half + 64], cv).then_inc(S["c_in"], 16)
            for i, n in enumerate(("b_re", "b_im")):
                bv = I[n].rearrange("o (r i) p h -> (o i p) r h", i=2)
                sp.dma_start(Braw[i], bv).then_inc(S["b_in"], 16)
            for n in (1, 2, 3):
                sp.dma_start(w_in[:, n], wi[n]).then_inc(S[("", "wq_in", "wk_in", "wv_in")[n]], 16)
            for t, n in ((gq, "g_q"), (gk, "g_k")):
                for i in range(2):
                    sp.dma_start(t[64 * i:64 * i + 64, :], I[n].rearrange("o (d i) -> (o d) i", i=1)).then_inc(S["gains_in"], 16)
            with nc.allow_non_contiguous_dma(reason="three vectors of 512 values"):
                for t, n in ((g_os, "g_out_ssm"), (g_oa, "g_out_att"), (b_glu, "b_glu")):
                    sp.dma_start(t, I[n].rearrange("o (k p) -> p (o k)", p=128)).then_inc(S["gains_in"], 16)
            sp.dma_start(g_ffn, I["g_ffn"].rearrange("o (p k) -> (o p) k", k=KT)).then_inc(S["gains_in"], 16)
            sp.wait_ge(S["qk_done"], 2)
            sp.dma_start(w_out, I["w_out"].rearrange("o (k p) n -> p (o k) n", k=KT)).then_inc(S["wo_in"], 16)
            sp.wait_ge(S["qk_done"], 4)
            sp.dma_start(w_glu, I["w_glu"].rearrange("o (k p) n -> p (o k) n", k=4)).then_inc(S["glu_in"], 16)
            sp.wait_ge(S["T_zero"], 1)
            sp.wait_ge(S["diag_ready"], 1)
            for j in range(L):
                sp.dma_start(TmV[16 * j:16 * j + 16, :, 16 * j:128], Kv[:, :, 0:128 - 16 * j]).then_inc(S["T_dma"], 16)
            sp.wait_ge(S["v_done"], 2)
            for w, n in enumerate(("s_w1", "s_w3")):
                sp.dma_start(sh13[:, w], I[n].rearrange("o (p k) f -> (o p) k f", k=KT)).then_inc(S["sh_in"], 16)
            sp.dma_start(sh2, I["s_w2"].rearrange("o (p j) n -> (o p) j n", j=2)).then_inc(S["sh_in"], 16)

            w1v = I["e_w1"].rearrange("o e (p k) f -> (o e) p k f", k=KT)
            w3v = I["e_w3"].rearrange("o e (p k) f -> (o e) p k f", k=KT)
            w2v = I["e_w2"].rearrange("o e (p j) n -> (o e) p j n", j=2)

            def load_pair(b, p, n=None):
                if n is not None:
                    sp.wait_ge(S["up_done"], n - 1)
                for i in range(2):
                    s = 2 * (p % 2) + i
                    e = b * EB + (2 * p + i)
                    sp.dma_start(slot13[s][:, 0], w1v[bass.ds(e, 1)].rearrange("o p k f -> (o p) k f")).then_inc(w13_in[s], 16)
                    sp.dma_start(slot13[s][:, 1], w3v[bass.ds(e, 1)].rearrange("o p k f -> (o p) k f")).then_inc(w13_in[s], 16)
                if n is not None:
                    sp.wait_ge(S["down_done"], n - 1)
                for i in range(2):
                    s = 2 * (p % 2) + i
                    e = b * EB + (2 * p + i)
                    sp.dma_start(slot2[s], w2v[bass.ds(e, 1)].rearrange("o p j n -> (o p) j n")).then_inc(w2_in[s], 16)

            sp.wait_ge(S["y5_done"], 2)
            load_pair(0, 0)
            load_pair(0, 1)
            sp.wait_ge(S["zg_done"], 4)
            sp.dma_start(w_rt, I["w_router"].rearrange("o (p k) e -> (o p) k e", k=KT)).then_inc(S["wr_in"], 16)
            sp.dma_start(bias_bc, I["router_bias"].to_broadcast([128, E])).then_inc(S["bias_in"], 16)
            with sp.Fori(0, NB - 1) as b:
                for p, nb in ((2, b), (3, b), (0, b + 1), (1, b + 1)):
                    load_pair(nb, p, nb * NPAIR + p)
            for p in (2, 3):
                load_pair(NB - 1, p, (NB - 1) * NPAIR + p)
            sp.wait_ge(S["route_ready"], 1)
            n_pass = sp.value_load(passes[0:1, :], min_val=1, max_val=4)
            with sp.If(n_pass > 1):
                with sp.Fori(1, n_pass) as r:
                    with sp.Fori(0, NB) as b:
                        for p in range(NPAIR):
                            load_pair(b, p, (r * NB + b) * NPAIR + p)
            sp.wait_ge(S["comb_done"], n_pass * (NB * 4))
            ov = out.rearrange("o (c q a) d -> q c (o a d)", q=4, a=2)
            for q in range(4):
                sp.dma_start(ov[q], acc[32 * q:32 * q + 32, :]).then_inc(S["out_done"], 16)
            sp.wait_ge(S["out_done"], 64)

        @block.gpsimd
        def _(pool):
            n = [0]

            def step(ins):
                n[0] += 1
                ins.then_inc(S["pool_chain"], 1)
                pool.wait_ge(S["pool_chain"], n[0])

            step(nc.gpsimd.memset(ident[:, :], 0.0))
            nc.gpsimd.affine_select(out=ident[:, :], in_=ident[:, :], compare_op=ALU.not_equal, fill=1.0,
                                    base=0, pattern=[[-1, 128]], channel_multiplier=1).then_inc(S["ident_ready"], 1)
            nc.gpsimd.memset(Tm, 0.0).then_inc(S["T_zero"], 1)
            step(nc.gpsimd.memset(negtri[:, :], -1.0))
            nc.gpsimd.affine_select(out=negtri[:, :], in_=negtri[:, :], compare_op=ALU.is_ge, fill=0.0,
                                    base=0, pattern=[[-1, 128]], channel_multiplier=1).then_inc(S["negtri_ready"], 1)
            nc.gpsimd.iota(iota, pattern=[[1, SLOTS]], base=0, channel_multiplier=0,
                           allow_small_or_imprecise_dtypes=True).then_inc(S["iota_ready"], 1)

            def causal(buf, done):
                d = buf.rearrange("p (b t) -> p b t", b=3)[:, 0::2, :]
                nc.gpsimd.affine_select(out=d, in_=d, compare_op=ALU.is_gt, fill=0.0, base=0,
                                        pattern=[[0, 2], [1, 128]], channel_multiplier=-1).then_inc(S[done], 1)

            for i in range(NH + 1):
                if i < NH:
                    pool.wait_ge(S["sp_ready"], i + 1)
                    causal(attL[i % 2], "L_ready")
                if i >= 1:
                    pool.wait_ge(S["w_ready"], i)
                    causal(attW[(i - 1) % 2], "wm_ready")
            pool.wait_ge(S["zg_done"], 4)
            step(nc.gpsimd.memset(tri_b, 1.0))
            nc.gpsimd.affine_select(out=tri_b, in_=tri_b, compare_op=ALU.is_gt, fill=0.0, base=0,
                                    pattern=[[1, 128]], channel_multiplier=-1).then_inc(S["trib_ready"], 1)
            nc.gpsimd.memset(ones_b, 1.0).then_inc(S["onesb_ready"], 1)
            step(nc.gpsimd.memset(lower, 1.0))
            nc.gpsimd.affine_select(out=lower, in_=lower, compare_op=ALU.is_gt, fill=0.0, base=0,
                                    pattern=[[1, NG], [-1, NG]], channel_multiplier=0).then_inc(S["lower_ready"], 1)
            pool.wait_ge(S["p2_ready"], 1)
            pool.wait_ge(S["rest_ready"], 1)
            nc.gpsimd.tensor_tensor(parts[2], rest, parts[1], ALU.subtract).then_inc(S["parts_ready"], 1)

        @block.tensor
        def _(pe):
            def mm(out_, lhsT, rhs, start=True, stop=True, **kw):
                return nc.tensor.matmul(out_, lhsT, rhs, start=start, stop=stop, **kw)

            pe.wait_ge(S["ident_ready"], 1)
            pe.wait_ge(S["xs_ready"], 2)
            xsv = xs.rearrange("p a (m k) -> p a k m", k=KT)
            for k in range(KT):
                for a in range(2):
                    last = nc.tensor.transpose(ps[k][:, 128 * a:128 * a + 128], xsv[:, a, k, :], ident[:, :])
                last.then_inc(S["xt_done"], 1)
            pe.wait_ge(S["params_in"], 16 * 4)
            pe.wait_ge(S["spread_ready"], 1)
            pe.wait_ge(S["xT_odd"], 4)
            for n, t in enumerate((prm, prm2, prm3)):
                nc.tensor.transpose(ps[7][:, 16 * n:16 * n + 16], t[0:PR, :], ident[0:PR, 0:PR])
            nc.tensor.transpose(ps[7][0:16, 64:96], dS[0:G, :], ident[0:G, 0:G]).then_inc(S["par_t_done"], 1)
            pe.wait_ge(S["c_in"], 16 * 4)
            pe.wait_ge(S["xT_even"], 4)
            for i in range(2):
                for b in range(4):
                    last = nc.tensor.transpose(ps[5 + i][:, 128 * b:128 * b + 128], Craw[i][:, b, :], ident[:, :])
                last.then_inc(S["par_t_done"], 1)
            pe.wait_ge(S["wu_in"], 16)
            for a in range(2):
                for k in range(KT):
                    last = mm(ps[a][:, :], hnC[:, k, 128 * a:128 * a + 128], w_in[:, 0, k, :], k == 0, k == KT - 1)
                last.then_inc(S["u_done"], 1)
            pe.wait_ge(S["par_evac"], 1)
            pe.wait_ge(S["ct_evac"], 4)
            for n in (1, 2):
                pe.wait_ge(S[("", "wq_in", "wk_in")[n]], 16)
                for a in range(2):
                    for k in range(KT):
                        last = mm(ps[1 + n + 2 * a][:, :], hnT[:, k, 128 * a:128 * a + 128], w_in[:, n, k, :], k == 0, k == KT - 1)
                    last.then_inc(S["qk_done"], 1)
            pe.wait_ge(S["Et_ready"], 1)
            pe.wait_ge(S["u_evac"], 2)
            for n in range(8):
                if n >= 2:
                    pe.wait_ge(S["E_act" if n % 2 == 0 else "E_dve"], n // 2)
                for m in range(4):
                    r, i = (4 * n + m) // 2, m % 2
                    last = nc.tensor.transpose(ps[n % 2][:, 128 * m:128 * m + 128],
                                               Et[i][:, 128 * r:128 * r + 128], ident[:, :])
                last.then_inc(S["E_done"], 1)
            pe.wait_ge(S["Bbar_ready"], 1)
            pe.wait_ge(S["G_ready"], 1)
            for n in range(8):
                if n < 2:
                    pe.wait_ge(S["E_act" if n % 2 == 0 else "E_dve"], 4)
                else:
                    pe.wait_ge(S["K_evac"], n - 1)
                for m in range(4):
                    r, rows = 4 * (n // 2) + m, slice(64 * (n % 2), 64 * (n % 2) + 64)
                    for i in range(2):
                        last = mm(ps[n % 2][0:16, 128 * m:128 * m + 128], Bbar[i][rows, r, :],
                                  GmV[i][rows, r, 0:8, :], i == 0, i == 1)
                last.then_inc(S["K_done"], 1)
            pe.wait_ge(S["K_evac"], 8)
            pe.wait_ge(S["U_ready"], 1)
            for i in range(2):
                for g in range(G):
                    r, s0 = g // 2, 64 * (g % 2)
                    last = mm(ps[i][s0:s0 + 64, C * r:C * r + C], EmV[:, r, i, s0:s0 + 64], UV[:, g, :])
                last.then_inc(S["V_done"], 1)
            pe.wait_ge(S["wv_in"], 16)
            for a in range(2):
                for k in range(KT):
                    last = mm(ps[6 + a][:, :], hnT[:, k, 128 * a:128 * a + 128], w_in[:, 3, k, :], k == 0, k == KT - 1)
                last.then_inc(S["v_done"], 1)
            pe.wait_ge(S["qk_normed"], 2)
            for n in range(4):
                for m in range(2):
                    for a in range(2):
                        c0 = 512 * (n // 2) + 128 * (2 * (n % 2) + m)
                        last = nc.tensor.transpose(ps[2 + n][:, 256 * m + 128 * a:256 * m + 128 * a + 128],
                                                   qk[:, a, c0:c0 + 128], ident[:, :])
                last.then_inc(S["qkT_done"], 1)

            def scores_of(h):
                m, rows = h // 2, slice(64 * (h % 2), 64 * (h % 2) + 64)
                z = ps[2 + h % 4]
                if h >= 4:
                    pe.wait_ge(S["w_ready"], h - 3)
                mm(z[:, 0:256], kT[rows, m, 0:128], qT[rows, m, :], True, False, skip_group_check=True)
                mm(z[:, 256:384], kT[rows, m, 128:256], qT[rows, m, 128:256], False, False,
                   skip_group_check=True).then_inc(S["z_done"], 1)

            def add_logs(h):
                z, Lm = ps[2 + h % 4], attL[h % 2]
                pe.wait_ge(S["L_ready"], h + 1)
                mm(z[:, 0:256], negtri[:, :], Lm[:, 0:256], False, False, skip_group_check=True)
                mm(z[:, 128:256], negones[:, :], Lm[:, 256:384], False, False, skip_group_check=True)
                mm(z[:, 256:384], negtri[:, :], Lm[:, 256:384], False, True, skip_group_check=True).then_inc(S["zi_done"], 1)

            def values_of(h):
                m, rows = h // 2, slice(64 * (h % 2), 64 * (h % 2) + 64)
                o = ps[6 + m % 2]
                if h % 2 == 0 and h >= 4:
                    pe.wait_ge(S["pv_act"], m - 1)
                pe.wait_ge(S["wm_ready"], h + 1)
                mm(o[rows, 0:256], v[:, 0, DH * h:DH * h + DH], attW[h % 2][:, 0:256], True, False, skip_group_check=True)
                last = mm(o[rows, 128:256], v[:, 1, DH * h:DH * h + DH], attW[h % 2][:, 256:384], False, True, skip_group_check=True)
                last.then_inc(S["pv_done"], 1)

            pe.wait_ge(S["qkT_act"], 2)
            pe.wait_ge(S["qkT_dve"], 2)
            pe.wait_ge(S["v_evac"], 2)
            pe.wait_ge(S["ones_ready"], 1)
            pe.wait_ge(S["negtri_ready"], 1)
            scores_of(0)
            scores_of(1)
            for h in range(NH + 1):
                if h < NH:
                    add_logs(h)
                    if h + 2 < NH:
                        scores_of(h + 2)
                if h >= 1:
                    values_of(h - 1)
            pe.wait_ge(S["S_ready"], 1)
            pe.wait_ge(S["T_dma"], L * 16)
            Sr, Si = (scan_t[n].rearrange("p (r c) -> p r c", r=PR) for n in (4, 5))
            for g in range(G):
                r, rows = g // 2, slice(64 * (g % 2), 64 * (g % 2) + 64)
                o = ps[g % 2][:, C * r:C * r + C]
                mm(o, GmV[0][rows, r, 1:9, :], Sr[rows, r, :], True, False)
                mm(o, GmV[1][rows, r, 1:9, :], Si[rows, r, :], False, False)
                last = mm(o, TmV[:, g, :], UV[:, g, :], False, True)
                if g >= G - 2:
                    last.then_inc(S["y5_done"], 1)
            pe.wait_ge(S["pv_act"], 4)
            for a in range(2):
                for m in range(4):
                    last = mm(ps[7][:, 2 + a:3 + a], sqa[:, m, 128 * a:128 * a + 128], ones_col, m == 0, m == 3)
            last.then_inc(S["sso_done"], 1)
            pe.wait_ge(S["wo_in"], 16)
            for a in range(2):
                for hf in range(2):
                    for k in range(4):
                        last = mm(ps[2 + 2 * a + hf][:, :], mixT[:, 4 + k, 128 * a:128 * a + 128],
                                  w_out[:, 4 + k, 512 * hf:512 * hf + 512], k == 0, k == 3)
                    last.then_inc(S["opa_done"], 1)
            pe.wait_ge(S["ytok_ready"], 1)
            yv = ytok.rearrange("p (a n) -> p a n", a=2)
            for n in range(2):
                for m in range(2):
                    for a in range(2):
                        k = 2 * n + m
                        last = nc.tensor.transpose(ps[n][:, 256 * m + 128 * a:256 * m + 128 * a + 128],
                                                   yv[:, a, 128 * k:128 * k + 128], ident[:, :])
                last.then_inc(S["yT_done"], 1)
            pe.wait_ge(S["glu_in"], 16)
            pe.wait_ge(S["yT_act"], 1)
            pe.wait_ge(S["yT_dve"], 1)
            for m in range(4):
                for k in range(4):
                    last = mm(ps[m // 2][:, 256 * (m % 2):256 * (m % 2) + 256], w_glu[:, k, 128 * m:128 * m + 128],
                              mixT[:, k, :], k == 0, k == 3)
                last.then_inc(S["zg_done"], 1)
            pe.wait_ge(S["sqs_ready"], 4)
            for a in range(2):
                for m in range(4):
                    last = mm(ps[7][:, a:a + 1], sqs[:, m, 128 * a:128 * a + 128], ones_col, m == 0, m == 3)
            last.then_inc(S["sso_done"], 1)
            pe.wait_ge(S["ys_ready"], 4)
            for a in range(2):
                for hf in range(2):
                    n = (0, 1, 6, 7)[2 * a + hf]
                    if n == 7:
                        pe.wait_ge(S["sso_evac"], 1)
                    for k in range(4):
                        last = mm(ps[n][:, :], mixT[:, k, 128 * a:128 * a + 128],
                                  w_out[:, k, 512 * hf:512 * hf + 512], k == 0, k == 3)
                    last.then_inc(S["ops_done"], 1)
            pe.wait_ge(S["hs_ready"], 2)
            for k in range(KT):
                for a in range(2):
                    last = nc.tensor.transpose(ps[k][:, 128 * a:128 * a + 128], hs[:, a, k, :], ident[:, :])
                last.then_inc(S["hT_done"], 1)
            pe.wait_ge(S["hT_act"], 4)
            pe.wait_ge(S["hT_dve"], 4)
            pe.wait_ge(S["wr_in"], 16)
            for a in range(2):
                for k in range(KT):
                    last = mm(ps[7][:, E * a:E * a + E], hn2T[:, k, 128 * a:128 * a + 128], w_rt[:, k, :], k == 0, k == KT - 1)
            last.then_inc(S["lg_done"], 1)
            pe.wait_ge(S["sh_in"], 48)
            for a in range(2):
                for k in range(KT):
                    last = mm(ps[a][:, :], hn2T[:, k, 128 * a:128 * a + 128], sh13[:, :, k, :], k == 0, k == KT - 1)
                last.then_inc(S["sh_up"], 1)
            pe.wait_ge(S["mask_ready"], 1)
            pe.wait_ge(S["trib_ready"], 1)
            pe.wait_ge(S["onesb_ready"], 1)
            mm(ps[6][:, 0:E], tri_b, mask_b[:, 0, :])
            mm(ps[6][:, E:2 * E], tri_b, mask_b[:, 1, :], True, False)
            mm(ps[6][:, E:2 * E], ones_b, mask_b[:, 0, :], False, True)
            mm(ps[6][:, 2 * E:3 * E], ones_b, mask_b[:, 0, :], True, False)
            mm(ps[6][:, 2 * E:3 * E], ones_b, mask_b[:, 1, :], False, True).then_inc(S["pos_done"], 1)
            for a in range(2):
                pe.wait_ge(S["sh_act"], a + 1)
                av = act_o[a].rearrange("p (m j) -> p j m", j=2)
                for j in range(2):
                    last = nc.tensor.transpose(ps[4 + a][:, 128 * j:128 * j + 128], av[:, j, :], ident[:, :])
                last.then_inc(S["sh_T"], 1)
            for a in range(2):
                pe.wait_ge(S["sh_actT"], a + 1)
                if a:
                    pe.wait_ge(S["shared_added"], 2)
                for hf in range(2):
                    for j in range(2):
                        last = mm(ps[2 + hf][:, :], actT[a][:, j, :], sh2[:, j, 512 * hf:512 * hf + 512], j == 0, j == 1)
                    last.then_inc(S["shd_done"], 1)
            pe.wait_ge(S["shared_added"], 4)
            pe.wait_ge(S["route_ready"], 1)

            def up(it, p):
                for i in range(2):
                    pe.wait_ge(w13_in[2 * (p % 2) + i], (it * 2 + (p // 2 + 1)) * 32)
                for k in range(KT):
                    for i in range(2):
                        e = 2 * p + i
                        last = mm(ps[p % 2][64 * i:64 * i + 64, :], xTg[:, k, SLOTS * e:SLOTS * e + SLOTS],
                                  slot13[2 * (p % 2) + i][:, :, k, :], k == 0, k == KT - 1)
                last.then_inc(S["up_done"], 1)

            def turn(it, p):
                n = it * NPAIR + p
                pe.wait_ge(S["act_ready"], n + 1)
                av = act_o[p % 2].rearrange("p (m j) -> p j m", j=2)
                for j in range(2):
                    last = nc.tensor.transpose(ps[4 + p % 2][:, 128 * j:128 * j + 128], av[:, j, :], ident[:, :])
                last.then_inc(S["t_done"], 1)

            def down(it, p):
                n = it * NPAIR + p
                pe.wait_ge(S["actT_ready"], n + 1)
                for i in range(2):
                    pe.wait_ge(w2_in[2 * (p % 2) + i], (it * 2 + (p // 2 + 1)) * 16)
                pe.wait_ge(S["ya"], n)
                pe.wait_ge(S["yd"], n)
                for hf in range(2):
                    for j in range(2):
                        for i in range(2):
                            last = mm(ps[2 + hf][64 * i:64 * i + 64, :], actT[p % 2][:, j, 64 * i:64 * i + 64],
                                      slot2[2 * (p % 2) + i][:, j, 512 * hf:512 * hf + 512], j == 0, j == 1)
                last.then_inc(S["down_done"], 1)

            def batch(r, b):
                it = r * NB + b
                pe.wait_ge(S["pbuilt"], r * (NB + 1) + b + 1)
                pe.wait_ge(S["comb_done"], it * 4)
                for k in range(KT):
                    if k >= 2:
                        pe.wait_ge(S["xa" if k % 2 == 0 else "xd"], it * 4 + k // 2)
                    for a in range(2):
                        for n in range(3):
                            last = mm(ps[6 + k % 2][:, :], parts[n][:, a, k, :], Pm[:, a], a + n == 0, a + n == 3)
                    last.then_inc(S["gath_done"], 1)
                for a in range(2):
                    pe.wait_ge(S["xa" if a == 0 else "xd"], it * 4 + 4)
                    for n in range(NPAIR):
                        last = nc.tensor.transpose(ps[6 + a][:, 128 * n:128 * n + 128],
                                                   PG[:, a, 2 * n:2 * n + 2, :], ident[:, :])
                    last.then_inc(S["gt_done"], 1)
                up(it, 0)
                up(it, 1)
                turn(it, 0)
                up(it, 2)
                down(it, 0)
                turn(it, 1)
                up(it, 3)
                down(it, 1)
                turn(it, 2)
                turn(it, 3)
                down(it, 2)
                down(it, 3)
                pe.wait_ge(S["gm_act"], it + 1)
                pe.wait_ge(S["gm_dve"], it + 1)
                pe.wait_ge(S["ya"], it * NPAIR + NPAIR)
                pe.wait_ge(S["yd"], it * NPAIR + NPAIR)
                for c in range(4):
                    a, hf = c // 2, c % 2
                    if c >= 2:
                        pe.wait_ge(S["comb_done"], it * 4 + (c - 1))
                    for n in range(NPAIR):
                        last = mm(ps[6 + c % 2][:, :], GmT[:, n, a, :], ysb[:, n, 512 * hf:512 * hf + 512], n == 0, n == NPAIR - 1)
                    last.then_inc(S["comb_mm"], 1)

            with pe.Fori(0, NB) as b:
                batch(0, b)
            n_pass = pe.value_load(passes[0:1, :], min_val=1, max_val=4)
            with pe.If(n_pass > 1):
                with pe.Fori(1, n_pass) as r:
                    with pe.Fori(0, NB) as b:
                        batch(r, b)

        @block.scalar
        def _(act):
            def copy(out_, in_, scale=1.0):
                return nc.scalar.activation(out_, in_, ACT.Copy, scale=scale)

            act.wait_ge(S["x_in"], 64)
            for a in range(2):
                nc.scalar.activation(xs[:, a, :], acc[:, D * a:D * a + D], ACT.Square, accum_out=ssx[:, a:a + 1]).then_inc(S["ssx_ready"], 1)
            act.wait_ge(S["gm_in"], 16)
            for k in range(1, KT, 2):
                act.wait_ge(S["xt_done"], k + 1)
                copy(hnC[:, k, :], ps[k][:, 0:256], scale=g_mix[:, k:k + 1])
                copy(chunked(hnT[:, k, :]), ps[k][:, 0:256].rearrange("p (a q c) -> p a q c", a=2, q=4),
                     scale=g_mix[:, k:k + 1]).then_inc(S["xT_odd"], 1)
            for i in range(2):
                act.wait_ge(S["par_t_done"], 2 + i)
                for half in range(2):
                    src = ps[5 + i][64 * half:64 * half + 64, :].rearrange("p (r i h) -> p r i h", r=PR, i=2)[:, :, half, :]
                    copy(Ct[i][64 * half:64 * half + 64, :, :], src).then_inc(S["ct_evac"], 1)
            uvv = uev.rearrange("p (g a h) -> p a g h", g=G, a=2)
            for a in range(2):
                act.wait_ge(S["u_done"], a + 1)
                copy(uvv[:, a], ps[a][:, :].rearrange("p (g h) -> p g h", g=G)).then_inc(S["u_evac"], 1)
            act.wait_ge(S["par_evac"], 1)
            nc.scalar.activation(ls, ls, ACT.Exp).then_inc(S["step_ready"], 1)
            act.wait_ge(S["a_ready"], 1)
            nc.scalar.activation(mag, mag, ACT.Exp)
            nc.scalar.activation(rho, rho, ACT.Exp)
            act.wait_ge(S["th_ready"], 1)
            nc.scalar.activation(sinv, th, ACT.Sin)
            nc.scalar.activation(cosv, th, ACT.Sin, scale=0.5).then_inc(S["exps_ready"], 1)
            for n in (0, 1):
                for a in range(2):
                    bank = ps[2 + n + 2 * a]
                    act.wait_ge(S["qk_done"], 2 * n + a + 1)
                    nc.scalar.activation(sqtmp[:, 1024 * a + 512 * n:1024 * a + 512 * n + 512], bank[:, :], ACT.Square)
                    copy(qk[:, a, 512 * n:512 * n + 512], bank[:, :]).then_inc(S["qk_evac"], 1)
            for n in range(0, 8, 2):
                act.wait_ge(S["E_done"], n + 1)
                copy(Em[:, 512 * n:512 * n + 512], ps[0][:, :]).then_inc(S["E_act"], 1)
            act.wait_ge(S["E_done"], 8)
            for n in range(8):
                act.wait_ge(S["K_done"], n + 1)
                copy(Kv[:, 8 * (n // 2) + n % 2:8 * (n // 2) + 8:2, :],
                     ps[n % 2][0:H, :].rearrange("p (m x) -> p m x", m=4)).then_inc(S["K_evac"], 1)
            for a in range(2):
                act.wait_ge(S["v_done"], a + 1)
                copy(v[:, a, :], ps[6 + a][:, :]).then_inc(S["v_evac"], 1)
            act.wait_ge(S["gq_ready"], 1)
            for n in (0, 1):
                act.wait_ge(S["qkT_done"], n + 1)
                copy(qT[:, 2 * n:2 * n + 2, :], ps[2 + n][:, :].rearrange("p (m t) -> p m t", m=2), scale=gq).then_inc(S["qkT_act"], 1)

            def exp_log(h):
                act.wait_ge(S["zc_ready"], h + 1)
                nc.scalar.activation(attE[h % 2], attE[h % 2], ACT.Exp).then_inc(S["e_ready"], 1)
                act.wait_ge(S["e_ready"], h + 1)
                nc.scalar.activation(attE[h % 2], attE[h % 2], ACT.Ln, bias=ones_col).then_inc(S["ln_ready"], 1)

            def weights(h):
                act.wait_ge(S["zi_done"], h + 1)
                if h >= 2:
                    act.wait_ge(S["pv_done"], h - 1)
                nc.scalar.activation(attW[h % 2], ps[2 + h % 4][:, 0:384], ACT.Exp).then_inc(S["w_ready"], 1)

            def evac_pv(m):
                act.wait_ge(S["pv_done"], 2 * m + 2)
                src = ps[6 + m % 2][:, 0:256].rearrange("p (c q a) -> p a q c", q=4, a=2)
                nc.scalar.activation(sqa[:, m, :].rearrange("p (a q c) -> p a q c", a=2, q=4), src, ACT.Square)
                copy(mixT[:, 4 + m, :].rearrange("p (a q c) -> p a q c", a=2, q=4), src, scale=g_oa[:, m:m + 1]).then_inc(S["pv_act"], 1)

            exp_log(0)
            for h in range(NH):
                if h + 1 < NH:
                    exp_log(h + 1)
                weights(h)
                if h >= 3 and h % 2 == 1:
                    evac_pv((h - 3) // 2)
            evac_pv(3)
            for i in range(2):
                act.wait_ge(S["y5_done"], i + 1)
                nc.scalar.activation(ygel.rearrange("p (r i c) -> p i r c", r=PR, i=2)[:, i], ps[i][:, :].rearrange("p (r c) -> p r c", r=PR), ACT.Gelu_apprx_tanh).then_inc(S["y5_gelu"], 1)
            act.wait_ge(S["yT_done"], 1)
            copy(mixT[:, 0:2, :], ps[0][:, :].rearrange("p (m t) -> p m t", m=2)).then_inc(S["yT_act"], 1)
            for m in range(4):
                act.wait_ge(S["zg_done"], 2 * (m // 2) + 2)
                nc.scalar.activation(sigt[:, m, :], ps[m // 2][:, 256 * (m % 2):256 * (m % 2) + 256], ACT.Sigmoid,
                                     bias=b_glu[:, m:m + 1]).then_inc(S["sig_ready"], 1)
            for a in range(2):
                act.wait_ge(S["h_ready"], 1 + a)
                nc.scalar.activation(sqtmp[:, 1024 * a:1024 * a + 1024], acc[:, D * a:D * a + D], ACT.Square,
                                     accum_out=ssx[:, a:a + 1]).then_inc(S["ssh_ready"], 1)
            for k in range(1, KT, 2):
                act.wait_ge(S["hT_done"], k + 1)
                copy(hn2T[:, k, :], ps[k][:, 0:256], scale=g_ffn[:, k:k + 1]).then_inc(S["hT_act"], 1)
            act.wait_ge(S["lg_done"], 1)
            nc.scalar.activation(scores, ps[7][:, 0:2 * E].rearrange("p (a e) -> p a e", a=2), ACT.Sigmoid).then_inc(S["scores_ready"], 1)
            copy(parts[0], hs).then_inc(S["p1_ready"], 1)
            act.wait_ge(S["rest_ready"], 1)
            copy(parts[1], rest).then_inc(S["p2_ready"], 1)
            for a in range(2):
                act.wait_ge(S["sh_up"], a + 1)
                nc.scalar.activation(silu_o[a], ps[a][:, 0:256], ACT.Silu).then_inc(S["sh_silu"], 1)
            for a in range(2):
                act.wait_ge(S["sh_T"], a + 1)
                copy(actT[a], ps[4 + a][:, 0:256].rearrange("p (j s) -> p j s", j=2)).then_inc(S["sh_actT"], 1)

            def silu(it, p):
                act.wait_ge(S["up_done"], it * NPAIR + (p + 1))
                nc.scalar.activation(silu_o[p % 2], ps[p % 2][:, 0:256], ACT.Silu).then_inc(S["silu_done"], 1)

            def turned(it, p):
                act.wait_ge(S["t_done"], it * NPAIR + (p + 1))
                copy(actT[p % 2], ps[4 + p % 2][:, 0:256].rearrange("p (j s) -> p j s", j=2)).then_inc(S["actT_ready"], 1)

            def y_out(it, p):
                act.wait_ge(S["down_done"], it * NPAIR + (p + 1))
                copy(ysb[:, p, 0:512], ps[2][:, :]).then_inc(S["ya"], 1)

            def batch(r, b):
                it = r * NB + b
                for k in range(0, KT, 2):
                    act.wait_ge(S["gath_done"], it * KT + (k + 1))
                    copy(xTg[:, k, :], ps[6][:, :], scale=g_ffn[:, k:k + 1]).then_inc(S["xa"], 1)
                act.wait_ge(S["gt_done"], it * 2 + 1)
                copy(GmT[:, :, 0, :], ps[6][:, :].rearrange("p (n t) -> p n t", n=NPAIR)).then_inc(S["gm_act"], 1)
                silu(it, 0)
                silu(it, 1)
                turned(it, 0)
                silu(it, 2)
                y_out(it, 0)
                turned(it, 1)
                silu(it, 3)
                y_out(it, 1)
                turned(it, 2)
                turned(it, 3)
                y_out(it, 2)
                y_out(it, 3)

            with act.Fori(0, NB) as b:
                batch(0, b)
            n_pass = act.value_load(passes[0:1, :], min_val=1, max_val=4)
            with act.If(n_pass > 1):
                with act.Fori(1, n_pass) as r:
                    with act.Fori(0, NB) as b:
                        batch(r, b)

        @block.vector
        def _(dve):
            n = [0]

            def step(ins):
                n[0] += 1
                ins.then_inc(S["dve_chain"], 1)
                dve.wait_ge(S["dve_chain"], n[0])

            def tt(out_, a, b, op):
                return nc.vector.tensor_tensor(out_, a, b, op)

            def ts(out_, a, s1, op0, s2=None, op1=ALU.bypass):
                return nc.vector.tensor_scalar(out_, a, s1, s2, op0, op1)

            def stt(out_, a, s1, b, op0, op1):
                return nc.vector.scalar_tensor_tensor(out=out_, in0=a, scalar=s1, in1=b, op0=op0, op1=op1)

            def rsqrt_of_mean(ss, w, count):
                m, y, t = nm[:, 0:w], ny[:, 0:w], nt[:, 0:w]
                step(ts(m, ss, 1.0 / count, ALU.mult, EPS, ALU.add))
                ts(nh[:, 0:w], m, -0.5, ALU.mult)
                step(ts(y.bitcast(I32), m.bitcast(I32), -0.5, ALU.mult, RSQRT_MAGIC, ALU.add))
                for _ in range(3):
                    step(tt(t, y, y, ALU.mult))
                    step(tt(t, t, nh[:, 0:w], ALU.mult))
                    step(stt(y, t, 1.5, y, ALU.add, ALU.mult))
                return y

            def cmul(outs, x, y, tmps, done=step):
                ta, tb, tc, td = tmps
                tt(ta, x[0], y[0], ALU.mult)
                tt(tb, x[1], y[1], ALU.mult)
                tt(tc, x[0], y[1], ALU.mult)
                step(tt(td, x[1], y[0], ALU.mult))
                tt(outs[0], ta, tb, ALU.subtract)
                done(tt(outs[1], tc, td, ALU.add))

            nc.vector.memset(negones[:, :], -1.0)
            nc.vector.memset(pos[:, :, E:PADE], -1.0)
            nc.vector.memset(gate[:, :, E:PADE], 0.0)
            nc.vector.memset(ones_col, 1.0).then_inc(S["ones_ready"], 1)
            dve.wait_ge(S["ssx_ready"], 2)
            y = rsqrt_of_mean(ssx, 2, D)
            for a in range(2):
                ts(xs[:, a, :], acc[:, D * a:D * a + D], y[:, a:a + 1], ALU.mult).then_inc(S["xs_ready"], 1)
            dve.wait_ge(S["params_in"], 16 * 4)
            nc.vector.tensor_copy(prm3[0:PR, :].rearrange("p (i s) -> p i s", i=2),
                                  ls2[0:PR, :].unsqueeze(2).to_broadcast([PR, 2, P])).then_inc(S["spread_ready"], 1)
            dve.wait_ge(S["gm_in"], 16)
            for k in range(0, KT, 2):
                dve.wait_ge(S["xt_done"], k + 1)
                ts(hnC[:, k, :], ps[k][:, 0:256], g_mix[:, k:k + 1], ALU.mult)
                ts(chunked(hnT[:, k, :]), ps[k][:, 0:256].rearrange("p (a q c) -> p a q c", a=2, q=4),
                   g_mix[:, k:k + 1], ALU.mult).then_inc(S["xT_even"], 1)
            dve.wait_ge(S["par_t_done"], 1)
            ts(lr, ps[7][:, 0:16], -1e-4, ALU.min)
            nc.vector.tensor_copy(li, ps[7][:, 16:32])
            nc.vector.tensor_copy(ls, ps[7][:, 32:48])
            nc.vector.tensor_copy(dT[0:H, :], ps[7][0:H, 64:96]).then_inc(S["par_evac"], 1)
            dve.wait_ge(S["par_evac"], 1)
            dve.wait_ge(S["step_ready"], 1)
            step(tt(mag, lr, ls, ALU.mult))
            ts(rho, mag, float(L), ALU.mult).then_inc(S["a_ready"], 1)
            step(tt(th, li, ls, ALU.mult))
            step(ts(t1, th, 1.0 / TWO_PI, ALU.mult, ROUND_MAGIC, ALU.add))
            step(ts(t1, t1, ROUND_MAGIC, ALU.subtract))
            for part in two_pi_parts():
                step(stt(th, t1, -part, th, ALU.mult, ALU.add))
            ts(th, th, PI_DOWN, ALU.min, -PI_DOWN, ALU.max).then_inc(S["th_ready"], 1)
            dve.wait_ge(S["u_evac"], 2)
            nc.vector.transpose(U, uev).then_inc(S["U_ready"], 1)
            dve.wait_ge(S["exps_ready"], 1)
            step(tt(cosv, cosv, cosv, ALU.mult))
            step(ts(cosv, cosv, -2.0, ALU.mult, 1.0, ALU.add))
            tt(lbr, mag, cosv, ALU.mult)
            step(tt(lbi, mag, sinv, ALU.mult))
            ts(t1, lbr, -1.0, ALU.add)
            tt(t2, lr, lr, ALU.mult)
            step(tt(t3, li, li, ALU.mult))
            step(tt(t2, t2, t3, ALU.add))
            step(nc.vector.reciprocal(den, t2))
            tt(t2, t1, lr, ALU.mult)
            step(tt(t3, lbi, li, ALU.mult))
            step(tt(t2, t2, t3, ALU.add))
            tt(cor, t2, den, ALU.mult)
            tt(t3, lbi, lr, ALU.mult)
            step(tt(t4, t1, li, ALU.mult))
            step(tt(t3, t3, t4, ALU.subtract))
            step(tt(coi, t3, den, ALU.mult))

            def over_h(w):
                return w.unsqueeze(2).to_broadcast([128, PR, H])

            big = [scan_t[i] for i in range(8)]
            dve.wait_ge(S["b_in"], 32)
            dve.wait_ge(S["par_t_done"], 3)
            tv = [big[i][:, 0:PR * H].rearrange("p (r h) -> p r h", r=PR) for i in range(4)]
            cmul(Bbar, Braw, [over_h(cor), over_h(coi)], tv, lambda ins: ins.then_inc(S["Bbar_ready"], 1))
            dve.wait_ge(S["Bbar_ready"], 1)
            nc.vector.memset(PW[0][:, 0, :], 1.0)
            nc.vector.memset(PW[1][:, 0, :], 0.0)
            nc.vector.tensor_copy(PW[0][:, 1, :], lbr)
            step(nc.vector.tensor_copy(PW[1][:, 1, :], lbi))
            for have in (1, 2, 4):
                by = [PW[i][:, have:have + 1, :].to_broadcast([128, have, PR]) for i in range(2)]
                tw = [big[i][:, 0:have * PR].rearrange("p (k r) -> p k r", k=have) for i in range(4)]
                cmul([PW[i][:, have + 1:2 * have + 1, :] for i in range(2)],
                     [PW[i][:, 1:have + 1, :] for i in range(2)], by, tw)

            def products(outs, mats, ks, sign, turn):
                for j, k in enumerate(ks):
                    w = [over_h(PW[i][:, k, :]) for i in range(2)]
                    tmps = [big[4 * ((j + turn) % 2) + i][:, 0:256].rearrange("p (r h) -> p r h", r=PR) for i in range(4)]
                    ta, tb, tc, td = tmps
                    tt(ta, mats[0], w[0], ALU.mult)
                    tt(tb, mats[1], w[1], ALU.mult)
                    tt(tc, mats[0], w[1], ALU.mult)
                    step(tt(td, mats[1], w[0], ALU.mult))
                    last = tt(outs[0][:, :, j, :], ta, tb, ALU.subtract)
                    if sign > 0:
                        last = tt(outs[1][:, :, j, :], tc, td, ALU.add)
                    else:
                        last = stt(outs[1][:, :, j, :], tc, -1.0, td, ALU.mult, ALU.subtract)
                return last

            dve.wait_ge(S["ct_evac"], 4)
            products(GmV, Ct, list(range(L + 1)), -1, 0).then_inc(S["G_ready"], 1)
            products(EtV, Bbar, [L - 1 - j for j in range(L)], 1, 1).then_inc(S["Et_ready"], 1)
            dve.wait_ge(S["qk_evac"], 4)
            for a in range(2):
                last = nc.vector.tensor_reduce(ssqk[:, 16 * a:16 * a + 16], sqtmp[:, 1024 * a:1024 * a + 1024].rearrange("p (h d) -> p h d", d=DH),
                                        AX.X, ALU.add)
            step(last)
            y = rsqrt_of_mean(ssqk, 32, DH)
            for a in range(2):
                q3 = qk[:, a, :].rearrange("p (h d) -> p h d", d=DH)
                tt(q3, q3, y[:, 16 * a:16 * a + 16].unsqueeze(2).to_broadcast([128, 16, DH]), ALU.mult).then_inc(S["qk_normed"], 1)
            dve.wait_ge(S["gains_in"], 16 * 8)
            ts(gq, gq, float(DH) ** -0.5, ALU.mult).then_inc(S["gq_ready"], 1)
            for n_ in range(1, 8, 2):
                dve.wait_ge(S["E_done"], n_ + 1)
                nc.vector.tensor_copy(Em[:, 512 * n_:512 * n_ + 512], ps[1][:, :]).then_inc(S["E_dve"], 1)
            cur, nxt = [cosv, sinv], [t1, t2]
            tq = [t3, t4, e8r, e8i]
            for _ in range(3):
                cmul(nxt, cur, cur, tq)
                cur, nxt = nxt, cur
            nc.vector.memset(rot[0][:, 0, :], 1.0)
            nc.vector.memset(rot[1][:, 0, :], 0.0)
            nc.vector.tensor_copy(rot[0][:, 1, :], cur[0])
            step(nc.vector.tensor_copy(rot[1][:, 1, :], cur[1]))
            for have in (1, 2, 4, 8, 16):
                by = [rot[i][:, have:have + 1, :].to_broadcast([128, have, PR]) for i in range(2)]
                tw = [rtmp[i][:, 0:have * PR].rearrange("p (k r) -> p k r", k=have) for i in range(4)]
                cmul([rot[i][:, have + 1:2 * have + 1, :] for i in range(2)],
                     [rot[i][:, 1:have + 1, :] for i in range(2)], by, tw)
            dve.wait_ge(S["ident_ready"], 1)
            step(tt(Kdiag, ident[0:H, 0:H].unsqueeze(1).to_broadcast([H, G, H]),
                    dT[0:H, :].unsqueeze(2).to_broadcast([H, G, H]), ALU.mult))
            dve.wait_ge(S["K_evac"], 8)
            tt(Kv[:, :, 0:H], Kv[:, :, 0:H], Kdiag, ALU.add).then_inc(S["diag_ready"], 1)
            dve.wait_ge(S["V_done"], 2)
            s3 = [w.rearrange("p (r c) -> p r c", r=PR) for w in scan_t]
            V3 = [ps[i][:, :].rearrange("p (r c) -> p r c", r=PR) for i in range(2)]
            R1 = [w[:, 1:33, :].rearrange("p c r -> p r c") for w in rot]
            tt(s3[0], V3[0], R1[0], ALU.mult)
            tt(s3[1], V3[1], R1[1], ALU.mult)
            tt(s3[2], V3[1], R1[0], ALU.mult)
            tt(s3[3], V3[0], R1[1], ALU.mult)
            step(nc.vector.tensor_copy(s3[6], rho.unsqueeze(2).to_broadcast([128, PR, C])))
            nc.vector.memset(s3[6][:, :, 0:1], 0.0)
            tt(s3[0], s3[0], s3[1], ALU.add)
            step(tt(s3[2], s3[2], s3[3], ALU.subtract))
            nc.vector.tensor_tensor_scan(scan_t[1], scan_t[6], scan_t[0], 0.0, ALU.mult, ALU.add)
            step(nc.vector.tensor_tensor_scan(scan_t[3], scan_t[6], scan_t[2], 0.0, ALU.mult, ALU.add))
            w = C - 1
            Rw = [x[:, :, 0:w] for x in R1]
            g_r, g_i = s3[1][:, :, 0:w], s3[3][:, :, 0:w]
            tt(s3[0][:, :, 0:w], g_r, Rw[0], ALU.mult)
            tt(s3[2][:, :, 0:w], g_i, Rw[1], ALU.mult)
            tt(s3[6][:, :, 0:w], g_r, Rw[1], ALU.mult)
            step(tt(s3[7][:, :, 0:w], g_i, Rw[0], ALU.mult))
            nc.vector.memset(s3[4][:, :, 0:1], 0.0)
            nc.vector.memset(s3[5][:, :, 0:1], 0.0)
            tt(s3[4][:, :, 1:C], s3[0][:, :, 0:w], s3[2][:, :, 0:w], ALU.subtract)
            tt(s3[5][:, :, 1:C], s3[6][:, :, 0:w], s3[7][:, :, 0:w], ALU.add).then_inc(S["S_ready"], 1)
            for n_ in (2, 3):
                dve.wait_ge(S["qkT_done"], n_ + 1)
                ts(kT[:, 2 * n_ - 4:2 * n_ - 2, :], ps[2 + n_][:, :].rearrange("p (m t) -> p m t", m=2), gk, ALU.mult).then_inc(S["qkT_dve"], 1)

            def clamp(h):
                dve.wait_ge(S["z_done"], h + 1)
                if h >= 2:
                    dve.wait_ge(S["sp_ready"], h - 1)
                ts(attE[h % 2], ps[2 + h % 4][:, 0:384], 80.0, ALU.min).then_inc(S["zc_ready"], 1)

            def softplus(h):
                dve.wait_ge(S["ln_ready"], h + 1)
                if h >= 2:
                    dve.wait_ge(S["zi_done"], h - 1)
                tt(attL[h % 2], attE[h % 2], ps[2 + h % 4][:, 0:384], ALU.max).then_inc(S["sp_ready"], 1)

            clamp(0)
            for h in range(NH):
                if h + 1 < NH:
                    clamp(h + 1)
                softplus(h)
            dve.wait_ge(S["sso_done"], 1)
            step(nc.vector.tensor_copy(sso[:, 2:4], ps[7][:, 2:4]))
            y = rsqrt_of_mean(sso[:, 2:4], 2, DS)
            step(nc.vector.tensor_copy(rso[:, 2:4], y))
            dve.wait_ge(S["y5_gelu"], 2)
            nc.vector.transpose(ytok.rearrange("p (a g h) -> p g a h", a=2, g=G), ygel.rearrange("p (g a h) -> p g a h", g=G, a=2)).then_inc(S["ytok_ready"], 1)

            def add_projection(a, hf, bank, col):
                part = acc[:, D * a + 512 * hf:D * a + 512 * hf + 512]
                return stt(part, bank[:, :], rso[:, col + a:col + a + 1], part, ALU.mult, ALU.add)

            for a in range(2):
                for hf in range(2):
                    dve.wait_ge(S["opa_done"], 2 * a + hf + 1)
                    last = add_projection(a, hf, ps[2 + 2 * a + hf], 2)
            step(last)
            dve.wait_ge(S["yT_done"], 2)
            nc.vector.tensor_copy(mixT[:, 2:4, :], ps[1][:, :].rearrange("p (m t) -> p m t", m=2)).then_inc(S["yT_dve"], 1)
            dve.wait_ge(S["zg_done"], 4)
            for m in range(4):
                dve.wait_ge(S["sig_ready"], m + 1)
                last = tt(mixT[:, m, :], mixT[:, m, :], sigt[:, m, :], ALU.mult)
            step(last)
            for m in range(4):
                tt(sqs[:, m, :], mixT[:, m, :], mixT[:, m, :], ALU.mult).then_inc(S["sqs_ready"], 1)
            for m in range(4):
                ts(mixT[:, m, :], mixT[:, m, :], g_os[:, m:m + 1], ALU.mult).then_inc(S["ys_ready"], 1)
            dve.wait_ge(S["sso_done"], 2)
            nc.vector.tensor_copy(sso[:, 0:2], ps[7][:, 0:2]).then_inc(S["sso_evac"], 1)
            dve.wait_ge(S["sso_evac"], 1)
            y = rsqrt_of_mean(sso[:, 0:2], 2, DS)
            step(nc.vector.tensor_copy(rso[:, 0:2], y))
            for a in range(2):
                for hf in range(2):
                    dve.wait_ge(S["ops_done"], 2 * a + hf + 1)
                    last = add_projection(a, hf, ps[(0, 1, 6, 7)[2 * a + hf]], 0)
                last.then_inc(S["h_ready"], 1)
            dve.wait_ge(S["ssh_ready"], 2)
            dve.wait_ge(S["h_ready"], 2)
            y = rsqrt_of_mean(ssx, 2, D)
            for a in range(2):
                ts(hs[:, a], acc[:, D * a:D * a + D].rearrange("p (m k) -> p k m", k=KT), y[:, a:a + 1], ALU.mult).then_inc(S["hs_ready"], 1)
            for k in range(0, KT, 2):
                dve.wait_ge(S["hT_done"], k + 1)
                ts(hn2T[:, k, :], ps[k][:, 0:256], g_ffn[:, k:k + 1], ALU.mult).then_inc(S["hT_dve"], 1)

            dve.wait_ge(S["scores_ready"], 1)
            dve.wait_ge(S["bias_in"], 16)
            step(tt(biased, scores, bias_bc.unsqueeze(1).to_broadcast([128, 2, E]), ALU.add))
            for a in range(2):
                for g in range(NG):
                    last = nc.vector.max(m8[:, a, g, :], biased[:, a, GE * g:GE * g + GE])
            step(last)
            step(tt(gs, m8[:, :, :, 0], m8[:, :, :, 1], ALU.add))
            gi = gs.unsqueeze(3).to_broadcast([128, 2, NG, NG])
            gj = gs.unsqueeze(2).to_broadcast([128, 2, NG, NG])
            tt(gt_c, gj, gi, ALU.is_gt)
            step(tt(eq_c, gj, gi, ALU.is_equal))
            dve.wait_ge(S["lower_ready"], 1)
            step(tt(eq_c, eq_c, lower.unsqueeze(1).to_broadcast([128, 2, NG, NG]), ALU.mult))
            step(tt(gt_c, gt_c, eq_c, ALU.add))
            step(nc.vector.tensor_reduce(rk1, gt_c, AX.X, ALU.add))
            step(ts(gmask, rk1, float(TOPG), ALU.is_lt))
            step(ts(rk1, gmask, -1.0, ALU.add, BIG, ALU.mult))
            b4 = biased.rearrange("p a (g x) -> p a g x", g=NG)
            s4 = sel.rearrange("p a (g x) -> p a g x", g=NG)
            step(tt(s4, b4, gmask.unsqueeze(3).to_broadcast([128, 2, NG, GE]), ALU.mult))
            step(tt(s4, s4, rk1.unsqueeze(3).to_broadcast([128, 2, NG, GE]), ALU.add))
            for a in range(2):
                step(nc.vector.max(top8[:, a, :], sel[:, a, :]))
                step(nc.vector.match_replace(out=repl[:, a, :], in_to_replace=top8[:, a, :], in_values=sel[:, a, :], imm_value=BIG))
            step(tt(mask, repl, sel, ALU.not_equal))
            nc.vector.tensor_copy(mask_b, mask).then_inc(S["mask_ready"], 1)
            step(tt(gate_r, scores, mask, ALU.mult))
            step(nc.vector.tensor_reduce(gsum, gate_r, AX.X, ALU.add))
            step(nc.vector.reciprocal(gsum, gsum))
            for a in range(2):
                ts(gate[:, a, 0:E], gate_r[:, a, :], gsum[:, a:a + 1], ALU.mult, ROUTED_SCALE, ALU.mult)
            dve.wait_ge(S["pos_done"], 1)
            step(nc.vector.reduce_max(mx[:, 0:1], ps[6][:, 2 * E:3 * E], AX.X))
            step(stt(pos[:, :, 0:E], ps[6][:, 0:2 * E].rearrange("p (a e) -> p a e", a=2), 1.0, mask, ALU.add, ALU.mult))
            step(ts(pos[:, :, 0:E], pos[:, :, 0:E], -1.0, ALU.add))
            step(ts(mx[:, 1:2], mx[:, 0:1], float(SLOTS), ALU.is_gt, 1.0, ALU.add))
            for most in (2 * SLOTS, 3 * SLOTS):
                step(stt(mx[:, 1:2], mx[:, 0:1], float(most), mx[:, 1:2], ALU.is_gt, ALU.add))
            nc.vector.tensor_copy(passes, mx[:, 1:2]).then_inc(S["route_ready"], 1)
            dve.wait_ge(S["p1_ready"], 1)
            tt(rest, hs, parts[0], ALU.subtract).then_inc(S["rest_ready"], 1)
            for a in range(2):
                dve.wait_ge(S["sh_silu"], a + 1)
                tt(act_o[a], silu_o[a], ps[a][:, 256:512], ALU.mult).then_inc(S["sh_act"], 1)

            def build_slots(n_built, b):
                nc.vector.tensor_copy(pos_b, pos[:, :, bass.ds(b * EB, EB)])
                nc.vector.tensor_copy(gate_b, gate[:, :, bass.ds(b * EB, EB)]).then_inc(S["slots_chain"], 1)
                dve.wait_ge(S["slots_chain"], n_built * 2 + 1)
                for a in range(2):
                    last = tt(Pm[:, a], iota.unsqueeze(1).to_broadcast([128, EB, SLOTS]),
                              pos_b[:, a].unsqueeze(2).to_broadcast([128, EB, SLOTS]), ALU.is_equal)
                last.then_inc(S["slots_chain"], 1)
                dve.wait_ge(S["slots_chain"], n_built * 2 + 2)
                for a in range(2):
                    last = tt(PG[:, a], Pm[:, a], gate_b[:, a].unsqueeze(2).to_broadcast([128, EB, SLOTS]), ALU.mult)
                last.then_inc(S["pbuilt"], 1)

            dve.wait_ge(S["parts_ready"], 1)
            dve.wait_ge(S["iota_ready"], 1)
            build_slots(0, 0)
            for a in range(2):
                for hf in range(2):
                    dve.wait_ge(S["shd_done"], 2 * a + hf + 1)
                    part = acc[:, D * a + 512 * hf:D * a + 512 * hf + 512]
                    tt(part, part, ps[2 + hf][:, :], ALU.add).then_inc(S["shared_added"], 1)
            dve.wait_ge(S["shared_added"], 4)

            def activate(it, p):
                dve.wait_ge(S["silu_done"], it * NPAIR + (p + 1))
                tt(act_o[p % 2], silu_o[p % 2], ps[p % 2][:, 256:512], ALU.mult).then_inc(S["act_ready"], 1)

            def y_out(it, p):
                dve.wait_ge(S["down_done"], it * NPAIR + (p + 1))
                nc.vector.tensor_copy(ysb[:, p, 512:1024], ps[3][:, :]).then_inc(S["yd"], 1)

            def batch(r, b):
                it = r * NB + b
                for k in range(1, KT, 2):
                    dve.wait_ge(S["gath_done"], it * KT + (k + 1))
                    ts(xTg[:, k, :], ps[7][:, :], g_ffn[:, k:k + 1], ALU.mult).then_inc(S["xd"], 1)
                dve.wait_ge(S["gt_done"], it * 2 + 2)
                nc.vector.tensor_copy(GmT[:, :, 1, :], ps[7][:, :].rearrange("p (n t) -> p n t", n=NPAIR)).then_inc(S["gm_dve"], 1)
                activate(it, 0)
                activate(it, 1)
                build_slots(r * (NB + 1) + (b + 1), b + 1)
                activate(it, 2)
                y_out(it, 0)
                activate(it, 3)
                y_out(it, 1)
                y_out(it, 2)
                y_out(it, 3)
                dve.wait_ge(S["comb_done"], it * 4)
                for c in range(4):
                    dve.wait_ge(S["comb_mm"], it * 4 + (c + 1))
                    part = acc[:, 512 * c:512 * c + 512]
                    tt(part, part, ps[6 + c % 2][:, :], ALU.add).then_inc(S["comb_done"], 1)

            with dve.Fori(0, NB) as b:
                batch(0, b)
            n_pass = dve.value_load(passes[0:1, :], min_val=1, max_val=4)
            with dve.If(n_pass > 1):
                with dve.Fori(1, n_pass) as r:
                    dve.wait_ge(S["gt_done"], r * (NB * 2))
                    ts(pos[:, :, 0:E], pos[:, :, 0:E], -float(SLOTS), ALU.add).then_inc(S["pos_moved"], 1)
                    dve.wait_ge(S["pos_moved"], r)
                    build_slots(r * (NB + 1), 0)
                    with dve.Fori(0, NB) as b:
                        batch(r, b)


_INS = ["x", "g_mix", "w_in", "lam_re", "lam_im", "b_re", "b_im", "c_re", "c_im", "d_skip", "log_step", "w_glu",
        "b_glu", "g_q", "g_k", "g_out_ssm", "g_out_att", "w_out", "g_ffn", "w_router", "router_bias", "e_w1", "e_w3",
        "e_w2", "s_w1", "s_w3", "s_w2"]


def kernel(**inputs):
    import numpy as _np
    import concourse.bacc as _bacc
    from concourse import mybir as _mybir
    from concourse.bass_utils import run_bass_kernel_spmd as _run

    nc = _bacc.Bacc("TRN2", target_bir_lowering=False, num_devices=1)
    arrays, args = {}, {}
    for name in _INS:
        a = _np.ascontiguousarray(inputs[name])
        arrays[f"in_{name}"] = a
        args[name] = nc.dram_tensor(f"in_{name}", a.shape, _mybir.dt.from_np(a.dtype), kind="ExternalInput").ap()
    out = nc.dram_tensor("out_h", (1, T, D), FP32, kind="ExternalOutput").ap()
    build(nc, args, out)
    r = _run(nc, [arrays], core_ids=[0])
    return r.results[0]["out_h"]
```

```python
from contextlib import ExitStack

import numpy as np

import concourse.bass as bass
from concourse import mybir

FP32 = mybir.dt.float32
BF16 = mybir.dt.bfloat16
I32 = mybir.dt.int32
ALU = mybir.AluOpType
ACT = mybir.ActivationFunctionType
AX = mybir.AxisListType

D = 1024
T = 256
DS = 512
KT = D // 128
G, P, H = 32, 64, 16
PR = G // 2
L = 8
C = T // L
NH, DH = 8, 64
E, TOPK, NG, GE, TOPG = 64, 8, 8, 8, 4
F = 256
SLOTS = 64
EB = 4
NB = E // EB
NPAIR = EB // 2
MAX_EXTRA = 32
assert MAX_EXTRA % EB == 0 and MAX_EXTRA >= T * TOPK // (SLOTS + 1)
COLS = E + MAX_EXTRA + EB
MAX_ITER = NB + MAX_EXTRA // EB
EPS = 1e-6
ROUTED_SCALE = 2.5
BIG = 3.0e38
TWO_PI = 2 * np.pi
PI_DOWN = 3.1415925
ROUND_MAGIC = 12582912.0
RSQRT_MAGIC = 1597463007.0


def two_pi_parts():
    parts, rest = [], TWO_PI
    for bits in (10, 10, 24):
        scale = 2.0 ** (bits - 1 - np.floor(np.log2(abs(rest))))
        part = float(np.round(rest * scale) / scale)
        parts.append(float(np.float32(part)))
        rest -= parts[-1]
    return parts


def build(nc, I, out):
    ctx = ExitStack()
    with ctx:
        def sb(name, words, dt=FP32, parts=128):
            return ctx.enter_context(nc.sbuf_tensor(name, [parts, words], dt))

        def sem(name):
            return ctx.enter_context(nc.semaphore(name))

        SLOT_W = 3 * 2048
        ring = sb("ring", 4 * SLOT_W)
        wreg = sb("wreg", 16384)
        acc = sb("acc", 2048)
        reg_a = sb("reg_a", 2048)
        reg_b = sb("reg_b", 2048)
        reg_c = sb("reg_c", 3072)
        reg_d = sb("reg_d", 2304)
        ident = sb("ident", 128)
        small = sb("small", 600)
        ps = [ctx.enter_context(nc.psum_tensor(f"bank{i}", [128, 512], FP32)) for i in range(8)]

        taken = {}

        def piece(region, words, size):
            at = taken.get(words, 0)
            taken[words] = at + size
            assert at + size <= region.shape[1], (words, at + size)
            return region[:, at:at + size]

        Et = [piece(ring, "s5", 2048) for _ in range(2)]
        EtV = [e.rearrange("p (r j h) -> p r j h", r=PR, j=L) for e in Et]
        Gm = [piece(ring, "s5", PR * 9 * H) for _ in range(2)]
        GmV = [g.rearrange("p (r j h) -> p r j h", r=PR, j=9) for g in Gm]
        Tm = piece(ring, "s5", G * 128)
        TmV = Tm.rearrange("p (g n) -> p g n", g=G)
        Em = piece(ring, "s5", PR * 2 * 128)
        EmV = Em.rearrange("p (r i s) -> p r i s", r=PR, i=2)
        U = piece(ring, "s5", G * C)
        UV = U.rearrange("p (g c) -> p g c", g=G)
        uev = piece(ring, "s5", 1024)
        par = lambda n: piece(ring, "s5", n)
        lr, li, ls, mag, th, cosv, sinv, lbr, lbi, t1, t2, t3, t4, cor, coi, den, e8r, e8i, rho = (
            par(PR) for _ in range(19))
        PW = [par(9 * PR).rearrange("p (k r) -> p k r", k=9) for _ in range(2)]
        Braw = [par(PR * H).rearrange("p (r h) -> p r h", r=PR) for _ in range(2)]
        Bbar = [par(PR * H).rearrange("p (r h) -> p r h", r=PR) for _ in range(2)]
        Ct = [par(PR * H).rearrange("p (r h) -> p r h", r=PR) for _ in range(2)]
        rot = [par(33 * PR).rearrange("p (c r) -> p c r", c=33) for _ in range(2)]
        dT = par(G)
        negtri = par(128)
        negones = par(128)
        prm = par(128)
        prm2 = par(128)
        prm3 = par(128)
        ls2 = par(2)
        dS = par(H)
        Craw = [Em[:, 512 * i:512 * i + 512].rearrange("p (b n) -> p b n", b=4) for i in range(2)]
        Kv = ring[0:H, 0:4096].rearrange("p (g n) -> p g n", g=G)
        Kdiag = par(G * H)[0:H, :].rearrange("p (g h) -> p g h", g=G)
        scan_t = [Em[:, 512 * i:512 * i + 512] for i in range(8)]
        rtmp = [uev[:, 256 * i:256 * i + 256] for i in range(4)]
        Vs = reg_d[:, 0:1024]
        ygel = reg_d[:, 0:1024]

        hnT = reg_a[:, :].rearrange("p (k t) -> p k t", k=KT)
        hnC = reg_d[:, 0:2048].rearrange("p (k t) -> p k t", k=KT)
        mixT = hnT
        mixV = reg_a[:, 0:1024].rearrange("p (m a q c) -> p a q m c", m=4, a=2, q=4)
        hT = hnT
        xs = reg_b[:, :].rearrange("p (a d) -> p a d", a=2)
        qk = reg_b[:, :].rearrange("p (a n) -> p a n", a=2)
        hs = reg_b[:, :].rearrange("p (a k m) -> p a k m", a=2, k=KT)
        v = reg_c[:, 0:1024].rearrange("p (a n) -> p a n", a=2)
        qT = reg_c[:, 1024:2048].rearrange("p (m t) -> p m t", m=4)
        kT = reg_c[:, 2048:3072].rearrange("p (m t) -> p m t", m=4)
        parts = [reg_c[:, 1024 * i:1024 * i + 1024].bitcast(BF16).rearrange("p (a k m) -> p a k m", a=2, k=KT)
                 for i in range(3)]
        sqa = reg_b[:, 0:1024].rearrange("p (m t) -> p m t", m=4)
        sqs = reg_b[:, 1024:2048].rearrange("p (m t) -> p m t", m=4)
        sigt = reg_c[:, 0:1024].rearrange("p (m t) -> p m t", m=4)
        attE = [reg_d[:, 1152 * i:1152 * i + 384] for i in range(2)]
        attL = [reg_d[:, 1152 * i + 384:1152 * i + 768] for i in range(2)]
        attW = [reg_d[:, 1152 * i + 768:1152 * i + 1152] for i in range(2)]
        sqtmp = reg_d[:, 0:2048]
        rest = reg_d[:, 0:2048].rearrange("p (a k m) -> p a k m", a=2, k=KT)
        rx_region = wreg[:, 4096:8192]
        rx = lambda n: piece(rx_region, "rx", n)
        Pm = rx(EB * SLOTS).bitcast(BF16).rearrange("p (a e s) -> p a e s", a=2, e=EB)
        PG = rx(2 * EB * SLOTS).rearrange("p (a e s) -> p a e s", a=2, e=EB)
        GmT = reg_a[:, 0:512].rearrange("p (n a t) -> p n a t", n=NPAIR, a=2)
        silu_o = [rx(F) for _ in range(2)]
        act_o = [rx(F) for _ in range(2)]
        actT = [rx(F).rearrange("p (j s) -> p j s", j=2) for _ in range(2)]

        w_in = wreg[:, :].rearrange("p (n k c) -> p n k c", n=4, k=KT)
        w_out = wreg[:, 0:8192].rearrange("p (k n) -> p k n", k=KT)
        w_glu = wreg[:, 8192:10240].rearrange("p (k n) -> p k n", k=4)
        sh13 = wreg[:, 10240:14336].rearrange("p (w k f) -> p w k f", w=2, k=KT)
        sh2 = wreg[:, 14336:16384].rearrange("p (j n) -> p j n", j=2)
        xTg = wreg[:, 0:2048].rearrange("p (k s) -> p k s", k=KT)
        ysb = wreg[:, 2048:4096].rearrange("p (n d) -> p n d", n=NPAIR)
        ringV = ring[:, :].rearrange("p (s w) -> p s w", s=4)
        slot13 = [ringV[:, s, 0:4096].rearrange("p (w k f) -> p w k f", w=2, k=KT) for s in range(4)]
        slot2 = [ringV[:, s, 4096:6144].rearrange("p (j n) -> p j n", j=2) for s in range(4)]

        rt = lambda n: piece(rt_region, "rt", n)
        rt_region = wreg[:, 8192:10240]
        w_rt = rt(KT * E).rearrange("p (k e) -> p k e", k=KT)
        two = lambda w: w.rearrange("p (a e) -> p a e", a=2)
        scores, biased, sel, repl, mask, gate_r = (two(rt(2 * E)) for _ in range(6))
        m8 = rt(2 * NG * 8).rearrange("p (a g x) -> p a g x", a=2, g=NG)
        gs = two(rt(2 * NG))
        gt_c = rt(2 * NG * NG).rearrange("p (a i j) -> p a i j", a=2, i=NG)
        eq_c = rt(2 * NG * NG).rearrange("p (a i j) -> p a i j", a=2, i=NG)
        rk1, gmask = two(rt(2 * NG)), two(rt(2 * NG))
        top8 = two(rt(16))
        mask_b = rt(E).bitcast(BF16).rearrange("p (a e) -> p a e", a=2)
        tri_b = rt(64).bitcast(BF16)
        ones_b = rt(64).bitcast(BF16)
        bias_bc = rt(E)
        lower = rt(64).rearrange("p (i j) -> p i j", i=NG)

        sm = lambda n: piece(small, "small", n)
        g_mix, g_ffn = sm(KT), sm(KT)
        gq, gk = sm(1), sm(1)
        g_os, g_oa, b_glu = sm(4), sm(4), sm(4)
        ones_col = sm(1)
        ssx, nm, ny, nt, nh = sm(2), sm(32), sm(32), sm(32), sm(32)
        ssqk = sm(32)
        sso = sm(4)
        rso = sm(4)
        rsh = sm(2)
        iota = sm(SLOTS)
        gate = sm(2 * COLS).rearrange("p (a e) -> p a e", a=2)
        pos = reg_d[:, 2048:2048 + 2 * COLS].rearrange("p (a e) -> p a e", a=2)
        n_iter = sm(1).bitcast(I32)
        gsum = sm(2)
        pgT = rx(4 * 128)[0:E].rearrange("p (w a t) -> p w a t", w=2, a=2)
        cnt, more, first, extra_its = rx(1), rx(1), rx(1), rx(1)
        more_b = rx(1).bitcast(BF16)[:, 0:1]
        depth, selx, offs = rx(MAX_EXTRA), rx(MAX_EXTRA), rx(MAX_EXTRA)
        iota_x, e_col, ones_f = rx(MAX_EXTRA), rx(1), rx(128)
        experts = rx(MAX_EXTRA).bitcast(I32)
        pos_b, gate_b = sm(2 * EB), sm(2 * EB)
        pos_b, gate_b = (w.rearrange("p (a e) -> p a e", a=2) for w in (pos_b, gate_b))

        names = """x_in gm_in params_in gains_in b_in c_in wu_in wq_in wk_in wv_in wo_in glu_in sh_in wr_in bias_in
        ident_ready negtri_ready iota_ready trib_ready onesb_ready lower_ready
        ones_ready ssx_ready xs_ready xT_even xT_odd xt_done spread_ready par_t_done par_evac ct_evac
        step_ready a_ready th_ready exps_ready u_done u_evac U_ready qk_done qk_evac qk_normed
        v_done v_evac gq_ready qkT_done qkT_act qkT_dve
        Et_ready Bbar_ready G_ready E_done E_act E_dve K_done K_evac diag_ready T_zero T_dma V_done V_act V_dve VT_done S_ready
        z_done zc_ready e_ready ln_ready sp_ready L_ready zi_done w_ready wm_ready pv_done pv_act
        y5_done y5_gelu  yT_done yT_act yT_dve zg_done sig_ready sqs_ready ys_ready sso_done sso_evac
        opa_done oa_added ops_done h_ready ssh_ready rsh_ready hs_ready hT_done hT_act hT_dve p1_ready rest_ready p2_ready
        parts_ready lg_done scores_ready mask_ready pos_done slots_ready pgT_done pgT_evac selx_ready
        extra_done route_ready P_ready PG_ready slots_copied rx_ready cnt_done first_done dve_chain pool_chain sh_up sh_silu sh_act sh_T sh_actT shd_done acc_added
        gath_done xa xd gt_done gm_act gm_dve up_done silu_done act_ready t_done actT_ready down_done ya yd
        comb_mm out_done""".split()
        S = {n: sem(n) for n in names}
        w13_in = [sem(f"w13_in{s}") for s in range(4)]
        w2_in = [sem(f"w2_in{s}") for s in range(4)]

        def chunked(ap):
            return ap.rearrange("p (c q a) -> p a q c", q=4, a=2)

        block = ctx.enter_context(nc.Block())

        @block.sync
        def _(sp):
            xv = I["x"].rearrange("o (c q a) d -> q c (o a d)", q=4, a=2)
            for q in range(4):
                sp.dma_start(acc[32 * q:32 * q + 32, :], xv[q]).then_inc(S["x_in"], 16)
            sp.dma_start(g_mix, I["g_mix"].rearrange("o (p k) -> (o p) k", k=KT)).then_inc(S["gm_in"], 16)
            wi = I["w_in"].rearrange("o (p k) (n c) -> n (o p) k c", k=KT, n=4)
            sp.dma_start(w_in[:, 0], wi[0]).then_inc(S["wu_in"], 16)
            lam = "o (r i) p -> (o r) (i p)"
            sp.dma_start(prm[0:PR, :], I["lam_re"].rearrange(lam, i=2)).then_inc(S["params_in"], 16)
            sp.dma_start(prm2[0:PR, :], I["lam_im"].rearrange(lam, i=2)).then_inc(S["params_in"], 16)
            sp.dma_start(ls2[0:PR, :], I["log_step"].rearrange("o (r i) -> (o r) i", i=2)).then_inc(S["params_in"], 16)
            sp.dma_start(dS[0:G, :], I["d_skip"].rearrange("o (g h) -> (o g) h", h=H)).then_inc(S["params_in"], 16)
            for i, n in enumerate(("c_re", "c_im")):
                cv = I[n].rearrange("o (b g) h p -> (o g h) b p", b=4)
                for half in range(2):
                    sp.dma_start(Craw[i][:, :, 64 * half:64 * half + 64], cv).then_inc(S["c_in"], 16)
            for i, n in enumerate(("b_re", "b_im")):
                bv = I[n].rearrange("o (r i) p h -> (o i p) r h", i=2)
                sp.dma_start(Braw[i], bv).then_inc(S["b_in"], 16)
            for n in (1, 2, 3):
                sp.dma_start(w_in[:, n], wi[n]).then_inc(S[("", "wq_in", "wk_in", "wv_in")[n]], 16)
            for t, n in ((gq, "g_q"), (gk, "g_k")):
                for i in range(2):
                    sp.dma_start(t[64 * i:64 * i + 64, :], I[n].rearrange("o (d i) -> (o d) i", i=1)).then_inc(S["gains_in"], 16)
            with nc.allow_non_contiguous_dma(reason="three vectors of 512 values"):
                for t, n in ((g_os, "g_out_ssm"), (g_oa, "g_out_att"), (b_glu, "b_glu")):
                    sp.dma_start(t, I[n].rearrange("o (k p) -> p (o k)", p=128)).then_inc(S["gains_in"], 16)
            sp.dma_start(g_ffn, I["g_ffn"].rearrange("o (p k) -> (o p) k", k=KT)).then_inc(S["gains_in"], 16)
            sp.wait_ge(S["qk_done"], 2)
            sp.dma_start(w_out, I["w_out"].rearrange("o (k p) n -> p (o k) n", k=KT)).then_inc(S["wo_in"], 16)
            sp.wait_ge(S["qk_done"], 4)
            sp.dma_start(w_glu, I["w_glu"].rearrange("o (k p) n -> p (o k) n", k=4)).then_inc(S["glu_in"], 16)
            sp.wait_ge(S["T_zero"], 1)
            sp.wait_ge(S["diag_ready"], 1)
            for j in range(L):
                sp.dma_start(TmV[16 * j:16 * j + 16, :, 16 * j:128], Kv[:, :, 0:128 - 16 * j]).then_inc(S["T_dma"], 16)
            sp.wait_ge(S["v_done"], 2)
            for w, n in enumerate(("s_w1", "s_w3")):
                sp.dma_start(sh13[:, w], I[n].rearrange("o (p k) f -> (o p) k f", k=KT)).then_inc(S["sh_in"], 16)
            sp.dma_start(sh2, I["s_w2"].rearrange("o (p j) n -> (o p) j n", j=2)).then_inc(S["sh_in"], 16)

            w1v = I["e_w1"].rearrange("o e (p k) f -> (o e) p (k f)", k=KT)
            w3v = I["e_w3"].rearrange("o e (p k) f -> (o e) p (k f)", k=KT)
            w2v = I["e_w2"].rearrange("o e (p j) n -> (o e) p (j n)", j=2)

            def load_batch(experts_of, b=None):
                for p in range(NPAIR):
                    if b is not None:
                        sp.wait_ge(S["up_done"], (b - 1) * NPAIR + (p + 1))
                    for s in (2 * p, 2 * p + 1):
                        e = experts_of[s]
                        sp.dma_start(ringV[:, s, 0:2048], w1v[bass.ds(e, 1)].rearrange("o p w -> (o p) w")).then_inc(w13_in[s], 16)
                        sp.dma_start(ringV[:, s, 2048:4096], w3v[bass.ds(e, 1)].rearrange("o p w -> (o p) w")).then_inc(w13_in[s], 16)
                for p in range(NPAIR):
                    if b is not None:
                        sp.wait_ge(S["down_done"], (b - 1) * NPAIR + (p + 1))
                    for s in (2 * p, 2 * p + 1):
                        e = experts_of[s]
                        sp.dma_start(ringV[:, s, 4096:6144], w2v[bass.ds(e, 1)].rearrange("o p w -> (o p) w")).then_inc(w2_in[s], 16)

            sp.wait_ge(S["y5_done"], 2)
            sp.wait_ge(S["zi_done"], NH)
            load_batch(list(range(EB)))
            sp.wait_ge(S["zg_done"], 4)
            sp.dma_start(w_rt, I["w_router"].rearrange("o (p k) e -> (o p) k e", k=KT)).then_inc(S["wr_in"], 16)
            sp.dma_start(bias_bc, I["router_bias"].to_broadcast([128, E])).then_inc(S["bias_in"], 16)
            with sp.Fori(1, NB) as b:
                load_batch([b * EB + s for s in range(EB)], b)
            sp.wait_ge(S["route_ready"], 1)
            n_it = sp.value_load(n_iter[0:1, :], min_val=NB, max_val=MAX_ITER)
            with sp.If(n_it > NB):
                with sp.Fori(NB, n_it) as b:
                    load_batch([sp.value_load(experts[0:1, bass.ds(b * EB - (E - s), 1)], min_val=0, max_val=E - 1)
                                for s in range(EB)], b)
            sp.wait_ge(S["acc_added"], n_it * 4 + 4)
            ov = out.rearrange("o (c q a) d -> q c (o a d)", q=4, a=2)
            for q in range(4):
                sp.dma_start(ov[q], acc[32 * q:32 * q + 32, :]).then_inc(S["out_done"], 16)
            sp.wait_ge(S["out_done"], 64)

        @block.gpsimd
        def _(pool):
            n = [0]

            def step(ins):
                n[0] += 1
                ins.then_inc(S["pool_chain"], 1)
                pool.wait_ge(S["pool_chain"], n[0])

            step(nc.gpsimd.memset(ident[:, :], 0.0))
            nc.gpsimd.affine_select(out=ident[:, :], in_=ident[:, :], compare_op=ALU.not_equal, fill=1.0,
                                    base=0, pattern=[[-1, 128]], channel_multiplier=1).then_inc(S["ident_ready"], 1)
            nc.gpsimd.memset(Tm, 0.0).then_inc(S["T_zero"], 1)
            step(nc.gpsimd.memset(negtri[:, :], -1.0))
            nc.gpsimd.affine_select(out=negtri[:, :], in_=negtri[:, :], compare_op=ALU.is_ge, fill=0.0,
                                    base=0, pattern=[[-1, 128]], channel_multiplier=1).then_inc(S["negtri_ready"], 1)
            nc.gpsimd.iota(iota, pattern=[[1, SLOTS]], base=1, channel_multiplier=0,
                           allow_small_or_imprecise_dtypes=True).then_inc(S["iota_ready"], 1)

            def causal(buf, done):
                d = buf.rearrange("p (b t) -> p b t", b=3)[:, 0::2, :]
                nc.gpsimd.affine_select(out=d, in_=d, compare_op=ALU.is_gt, fill=0.0, base=0,
                                        pattern=[[0, 2], [1, 128]], channel_multiplier=-1).then_inc(S[done], 1)

            for i in range(NH + 1):
                if i < NH:
                    pool.wait_ge(S["sp_ready"], i + 1)
                    causal(attL[i % 2], "L_ready")
                if i >= 1:
                    pool.wait_ge(S["w_ready"], i)
                    causal(attW[(i - 1) % 2], "wm_ready")
            pool.wait_ge(S["zg_done"], 4)
            step(nc.gpsimd.memset(tri_b, 1.0))
            nc.gpsimd.affine_select(out=tri_b, in_=tri_b, compare_op=ALU.is_gt, fill=0.0, base=0,
                                    pattern=[[1, 128]], channel_multiplier=-1).then_inc(S["trib_ready"], 1)
            nc.gpsimd.memset(ones_b, 1.0).then_inc(S["onesb_ready"], 1)
            step(nc.gpsimd.memset(lower, 1.0))
            nc.gpsimd.affine_select(out=lower, in_=lower, compare_op=ALU.is_gt, fill=0.0, base=0,
                                    pattern=[[1, NG], [-1, NG]], channel_multiplier=0).then_inc(S["lower_ready"], 1)
            pool.wait_ge(S["ops_done"], 4)
            nc.gpsimd.iota(iota_x, pattern=[[1, MAX_EXTRA]], base=0, channel_multiplier=0,
                           allow_small_or_imprecise_dtypes=True)
            nc.gpsimd.iota(e_col, pattern=[[0, 1]], base=0, channel_multiplier=1,
                           allow_small_or_imprecise_dtypes=True)
            nc.gpsimd.memset(ones_f, 1.0).then_inc(S["rx_ready"], 1)
            pool.wait_ge(S["p2_ready"], 1)
            pool.wait_ge(S["rest_ready"], 1)
            nc.gpsimd.tensor_tensor(parts[2], rest, parts[1], ALU.subtract).then_inc(S["parts_ready"], 1)

        @block.tensor
        def _(pe):
            def mm(out_, lhsT, rhs, start=True, stop=True, **kw):
                return nc.tensor.matmul(out_, lhsT, rhs, start=start, stop=stop, **kw)

            pe.wait_ge(S["ident_ready"], 1)
            pe.wait_ge(S["xs_ready"], 2)
            xsv = xs.rearrange("p a (m k) -> p a k m", k=KT)
            for k in range(KT):
                for a in range(2):
                    last = nc.tensor.transpose(ps[k][:, 128 * a:128 * a + 128], xsv[:, a, k, :], ident[:, :])
                last.then_inc(S["xt_done"], 1)
            pe.wait_ge(S["params_in"], 16 * 4)
            pe.wait_ge(S["spread_ready"], 1)
            pe.wait_ge(S["xT_odd"], 4)
            for n, t in enumerate((prm, prm2, prm3)):
                nc.tensor.transpose(ps[7][:, 16 * n:16 * n + 16], t[0:PR, :], ident[0:PR, 0:PR])
            nc.tensor.transpose(ps[7][0:16, 64:96], dS[0:G, :], ident[0:G, 0:G]).then_inc(S["par_t_done"], 1)
            pe.wait_ge(S["c_in"], 16 * 4)
            pe.wait_ge(S["xT_even"], 4)
            for i in range(2):
                for b in range(4):
                    last = nc.tensor.transpose(ps[5 + i][:, 128 * b:128 * b + 128], Craw[i][:, b, :], ident[:, :])
                last.then_inc(S["par_t_done"], 1)
            pe.wait_ge(S["wu_in"], 16)
            for a in range(2):
                for k in range(KT):
                    last = mm(ps[a][:, :], hnC[:, k, 128 * a:128 * a + 128], w_in[:, 0, k, :], k == 0, k == KT - 1)
                last.then_inc(S["u_done"], 1)
            pe.wait_ge(S["par_evac"], 1)
            pe.wait_ge(S["ct_evac"], 4)
            for n in (1, 2):
                pe.wait_ge(S[("", "wq_in", "wk_in")[n]], 16)
                for a in range(2):
                    for k in range(KT):
                        last = mm(ps[1 + n + 2 * a][:, :], hnT[:, k, 128 * a:128 * a + 128], w_in[:, n, k, :], k == 0, k == KT - 1)
                    last.then_inc(S["qk_done"], 1)
            pe.wait_ge(S["wv_in"], 16)
            for a in range(2):
                for k in range(KT):
                    last = mm(ps[6 + a][:, :], hnT[:, k, 128 * a:128 * a + 128], w_in[:, 3, k, :], k == 0, k == KT - 1)
                last.then_inc(S["v_done"], 1)
            pe.wait_ge(S["Et_ready"], 1)
            pe.wait_ge(S["u_evac"], 2)
            for n in range(8):
                if n >= 2:
                    pe.wait_ge(S["E_act" if n % 2 == 0 else "E_dve"], n // 2)
                for m in range(4):
                    r, i = (4 * n + m) // 2, m % 2
                    last = nc.tensor.transpose(ps[n % 2][:, 128 * m:128 * m + 128],
                                               Et[i][:, 128 * r:128 * r + 128], ident[:, :])
                last.then_inc(S["E_done"], 1)
            pe.wait_ge(S["Bbar_ready"], 1)
            pe.wait_ge(S["G_ready"], 1)
            pe.wait_ge(S["E_act"], 4)
            pe.wait_ge(S["E_dve"], 4)
            for half in range(2):
                rows = slice(64 * half, 64 * half + 64)
                for n in range(4):
                    for i in range(2):
                        for m in range(4):
                            last = mm(ps[half][32 * m:32 * m + H, 128 * n:128 * n + 128], Bbar[i][rows, 4 * n + m, :],
                                      GmV[i][rows, 4 * n + m, 0:8, :], i == 0, i == 1)
                last.then_inc(S["K_done"], 1)
            pe.wait_ge(S["K_evac"], 8)
            pe.wait_ge(S["U_ready"], 1)
            for b in range(2):
                for i in range(4 * b, 4 * b + 4):
                    o = ps[b].rearrange("p (r i s) -> p r i s", r=2, i=2)[:, (i // 2) % 2, :, 64 * (i % 2):64 * (i % 2) + 64]
                    for q in range(4):
                        last = mm(o[32 * q:32 * q + 32], UV[:, 8 * q + i, :],
                                  EmV[:, 4 * q + i // 2, :, 64 * (i % 2):64 * (i % 2) + 64])
                last.then_inc(S["V_done"], 1)
            pe.wait_ge(S["qk_normed"], 2)
            for n in range(4):
                for m in range(2):
                    for a in range(2):
                        c0 = 512 * (n // 2) + 128 * (2 * (n % 2) + m)
                        last = nc.tensor.transpose(ps[2 + n][:, 256 * m + 128 * a:256 * m + 128 * a + 128],
                                                   qk[:, a, c0:c0 + 128], ident[:, :])
                last.then_inc(S["qkT_done"], 1)

            pe.wait_ge(S["V_act"], 1)
            pe.wait_ge(S["V_dve"], 1)
            for i in range(2):
                for r in range(4):
                    last = nc.tensor.transpose(ps[i][:, 128 * r:128 * r + 128], Vs[:, 256 * r + 128 * i:256 * r + 128 * i + 128], ident[:, :])
                last.then_inc(S["VT_done"], 1)

            def scores_of(h):
                m, rows = h // 2, slice(64 * (h % 2), 64 * (h % 2) + 64)
                z = ps[2 + h % 4]
                if h >= 4:
                    pe.wait_ge(S["w_ready"], h - 3)
                mm(z[:, 0:256], kT[rows, m, 0:128], qT[rows, m, :], True, False, skip_group_check=True)
                mm(z[:, 256:384], kT[rows, m, 128:256], qT[rows, m, 128:256], False, False,
                   skip_group_check=True).then_inc(S["z_done"], 1)

            def add_logs(h):
                z, Lm = ps[2 + h % 4], attL[h % 2]
                pe.wait_ge(S["L_ready"], h + 1)
                mm(z[:, 0:256], negtri[:, :], Lm[:, 0:256], False, False, skip_group_check=True)
                mm(z[:, 128:256], negones[:, :], Lm[:, 256:384], False, False, skip_group_check=True)
                mm(z[:, 256:384], negtri[:, :], Lm[:, 256:384], False, True, skip_group_check=True).then_inc(S["zi_done"], 1)

            def values_of(h):
                m, rows = h // 2, slice(64 * (h % 2), 64 * (h % 2) + 64)
                o = ps[6 + m % 2]
                if h % 2 == 0 and h >= 4:
                    pe.wait_ge(S["pv_act"], m - 1)
                pe.wait_ge(S["wm_ready"], h + 1)
                mm(o[rows, 0:256], v[:, 0, DH * h:DH * h + DH], attW[h % 2][:, 0:256], True, False, skip_group_check=True)
                last = mm(o[rows, 128:256], v[:, 1, DH * h:DH * h + DH], attW[h % 2][:, 256:384], False, True, skip_group_check=True)
                last.then_inc(S["pv_done"], 1)

            Sr, Si = (scan_t[n].rearrange("p (r c) -> p r c", r=PR) for n in (4, 5))
            def s5_output(i):
                if i == 0:
                    pe.wait_ge(S["S_ready"], 1)
                    pe.wait_ge(S["T_dma"], L * 16)
                rows = slice(64 * (i % 2), 64 * (i % 2) + 64)
                tile = lambda q: ps[i % 2][32 * q:32 * q + 32, 128 * (i // 2):128 * (i // 2) + 128]
                for w, st in enumerate((Sr, Si)):
                    for q in range(4):
                        r = 4 * q + i // 2
                        mm(tile(q), st[rows, r, :], GmV[w][rows, r, 1:9, :], w == 0, False)
                for q in range(4):
                    last = mm(tile(q), UV[:, 8 * q + i, :], TmV[:, 8 * q + i, :], False, True)
                if i >= 6:
                    last.then_inc(S["y5_done"], 1)

            pe.wait_ge(S["qkT_act"], 2)
            pe.wait_ge(S["qkT_dve"], 2)
            pe.wait_ge(S["v_evac"], 2)
            pe.wait_ge(S["ones_ready"], 1)
            pe.wait_ge(S["negtri_ready"], 1)
            scores_of(0)
            scores_of(1)
            for h in range(NH + 1):
                if h < NH:
                    add_logs(h)
                    if h + 2 < NH:
                        scores_of(h + 2)
                if h >= 1:
                    values_of(h - 1)
                if 4 <= h < NH:
                    s5_output(2 * h - 8)
                    s5_output(2 * h - 7)
            pe.wait_ge(S["pv_act"], 4)
            for a in range(2):
                for m in range(4):
                    last = mm(ps[7][:, 2 + a:3 + a], sqa[:, m, 128 * a:128 * a + 128], ones_col, m == 0, m == 3)
            last.then_inc(S["sso_done"], 1)
            pe.wait_ge(S["wo_in"], 16)

            def project_attention(a):
                for hf in range(2):
                    for k in range(4):
                        last = mm(ps[2 + 2 * a + hf][:, :], mixT[:, 4 + k, 128 * a:128 * a + 128],
                                  w_out[:, 4 + k, 512 * hf:512 * hf + 512], k == 0, k == 3)
                    last.then_inc(S["opa_done"], 1)

            project_attention(0)
            pe.wait_ge(S["y5_gelu"], 2)
            for a in range(2):
                for q in range(4):
                    j = 2 * q + a
                    last = nc.tensor.transpose(ps[a][:, 128 * q:128 * q + 128], ygel[:, 128 * j:128 * j + 128], ident[:, :])
                last.then_inc(S["yT_done"], 1)
            pe.wait_ge(S["glu_in"], 16)
            pe.wait_ge(S["yT_act"], 1)
            pe.wait_ge(S["yT_dve"], 1)
            for m in range(4):
                for k in range(4):
                    last = mm(ps[m // 2][:, 256 * (m % 2):256 * (m % 2) + 256], w_glu[:, k, 128 * m:128 * m + 128],
                              mixT[:, k, :], k == 0, k == 3)
                last.then_inc(S["zg_done"], 1)
            project_attention(1)
            pe.wait_ge(S["sqs_ready"], 4)
            for a in range(2):
                for m in range(4):
                    last = mm(ps[7][:, a:a + 1], sqs[:, m, 128 * a:128 * a + 128], ones_col, m == 0, m == 3)
            last.then_inc(S["sso_done"], 1)
            pe.wait_ge(S["ys_ready"], 4)
            for a in range(2):
                for hf in range(2):
                    n = (0, 1, 6, 7)[2 * a + hf]
                    if n == 7:
                        pe.wait_ge(S["sso_evac"], 1)
                    for k in range(4):
                        last = mm(ps[n][:, :], mixT[:, k, 128 * a:128 * a + 128],
                                  w_out[:, k, 512 * hf:512 * hf + 512], k == 0, k == 3)
                    last.then_inc(S["ops_done"], 1)
            for a in range(2):
                pe.wait_ge(S["h_ready"], a + 1)
                av = acc[:, D * a:D * a + D].rearrange("p (m k) -> p k m", k=KT)
                for k in range(KT):
                    c0 = 256 * (k % 2) + 128 * a
                    last = nc.tensor.transpose(ps[2 + k // 2][:, c0:c0 + 128], av[:, k, :], ident[:, :])
                    if a == 1 and k % 2 == 1:
                        last.then_inc(S["hT_done"], 1)
            pe.wait_ge(S["hT_act"], 2)
            pe.wait_ge(S["hT_dve"], 2)
            pe.wait_ge(S["wr_in"], 16)
            for a in range(2):
                for k in range(KT):
                    last = mm(ps[7][:, E * a:E * a + E], hT[:, k, 128 * a:128 * a + 128], w_rt[:, k, :], k == 0, k == KT - 1)
            last.then_inc(S["lg_done"], 1)
            pe.wait_ge(S["sh_in"], 48)

            def shared_up(a, ks):
                for k in ks:
                    last = mm(ps[a][:, :], hT[:, k, 128 * a:128 * a + 128], sh13[:, :, k, :], k == 0, k == KT - 1)
                if k == KT - 1:
                    last.then_inc(S["sh_up"], 1)

            shared_up(0, range(KT))
            shared_up(1, range(0, 4))
            pe.wait_ge(S["mask_ready"], 1)
            pe.wait_ge(S["trib_ready"], 1)
            pe.wait_ge(S["onesb_ready"], 1)
            mm(ps[6][:, 0:E], tri_b, mask_b[:, 0, :])
            mm(ps[6][:, E:2 * E], tri_b, mask_b[:, 1, :], True, False)
            mm(ps[6][:, E:2 * E], ones_b, mask_b[:, 0, :], False, True)
            mm(ps[6][0:E, 2 * E:2 * E + 1], mask_b[:, 0, :], ones_b[:, 0:1], True, False)
            mm(ps[6][0:E, 2 * E:2 * E + 1], mask_b[:, 1, :], ones_b[:, 0:1], False, True).then_inc(S["pos_done"], 1)
            shared_up(1, range(4, 6))
            pe.wait_ge(S["cnt_done"], 1)
            mm(ps[6][0:E, 2 * E + 1:2 * E + 2], tri_b[0:E, 0:E], more_b[0:E, :])
            mm(ps[6][:, 2 * E + 2:2 * E + 3], ones_b[0:E, :], more_b[0:E, :]).then_inc(S["first_done"], 1)
            pe.wait_ge(S["slots_ready"], 1)
            for w, t in enumerate((pos, gate)):
                for a in range(2):
                    last = nc.tensor.transpose(ps[7][0:E, 256 * w + 128 * a:256 * w + 128 * a + 128], t[:, a, 0:E], ident[:, :])
            last.then_inc(S["pgT_done"], 1)
            shared_up(1, range(6, KT))
            pe.wait_ge(S["selx_ready"], 1)
            pe.wait_ge(S["pgT_evac"], 1)
            pe.wait_ge(S["rx_ready"], 1)
            X = MAX_EXTRA
            for a in range(2):
                mm(ps[6][:, X * a:X * a + X], pgT[:, 0, a, :], selx[0:E, :], True, False)
                mm(ps[6][:, X * a:X * a + X], ones_f[0:E, :], offs[0:E, :], False, True)
                mm(ps[6][:, X * (2 + a):X * (3 + a)], pgT[:, 1, a, :], selx[0:E, :])
            mm(ps[6][0:1, 4 * X:5 * X], e_col[0:E, :], selx[0:E, :]).then_inc(S["extra_done"], 1)

            def gather_slices(n):
                for k in (2 * n, 2 * n + 1):
                    o = ps[6 + n % 2][:, 256 * (k % 2):256 * (k % 2) + 256]
                    for a in range(2):
                        for w in range(3):
                            last = mm(o, parts[w][:, a, k, :], Pm[:, a], a + w == 0, a + w == 3)
                last.then_inc(S["gath_done"], 1)

            pe.wait_ge(S["P_ready"], 1)
            pe.wait_ge(S["parts_ready"], 1)
            pe.wait_ge(S["route_ready"], 1)
            gather_slices(0)
            gather_slices(1)
            pe.wait_ge(S["xa"], 1)
            gather_slices(2)
            pe.wait_ge(S["xd"], 1)
            gather_slices(3)
            for a in range(2):
                pe.wait_ge(S["sh_act"], a + 1)
                av = act_o[a].rearrange("p (m j) -> p j m", j=2)
                for j in range(2):
                    last = nc.tensor.transpose(ps[4 + a][:, 128 * j:128 * j + 128], av[:, j, :], ident[:, :])
                last.then_inc(S["sh_T"], 1)
            for a in range(2):
                pe.wait_ge(S["sh_actT"], a + 1)
                for hf in range(2):
                    for j in range(2):
                        last = mm(ps[2 + 2 * a + hf][:, :], actT[a][:, j, :], sh2[:, j, 512 * hf:512 * hf + 512], j == 0, j == 1)
                    last.then_inc(S["shd_done"], 1)
            def up(it, p):
                for i in range(2):
                    pe.wait_ge(w13_in[2 * p + i], it * 32 + 32)
                for k in range(KT):
                    for i in range(2):
                        e = 2 * p + i
                        last = mm(ps[p][64 * i:64 * i + 64, :], xTg[:, k, SLOTS * e:SLOTS * e + SLOTS],
                                  slot13[e][:, :, k, :], k == 0, k == KT - 1)
                last.then_inc(S["up_done"], 1)

            def turn(it, p):
                pe.wait_ge(S["act_ready"], it * NPAIR + (p + 1))
                av = act_o[p].rearrange("p (m j) -> p j m", j=2)
                for j in range(2):
                    last = nc.tensor.transpose(ps[4 + p][:, 128 * j:128 * j + 128], av[:, j, :], ident[:, :])
                last.then_inc(S["t_done"], 1)

            def down(it, p):
                pe.wait_ge(S["actT_ready"], it * NPAIR + (p + 1))
                for i in range(2):
                    pe.wait_ge(w2_in[2 * p + i], it * 16 + 16)
                if p:
                    pe.wait_ge(S["ya"], it * NPAIR + p)
                    pe.wait_ge(S["yd"], it * NPAIR + p)
                for hf in range(2):
                    for j in range(2):
                        for i in range(2):
                            last = mm(ps[2 + hf][64 * i:64 * i + 64, :], actT[p][:, j, 64 * i:64 * i + 64],
                                      slot2[2 * p + i][:, j, 512 * hf:512 * hf + 512], j == 0, j == 1)
                last.then_inc(S["down_done"], 1)

            n_it = pe.value_load(n_iter[0:1, :], min_val=NB, max_val=MAX_ITER)
            with pe.Fori(0, n_it) as it:
                pe.wait_ge(S["xa"], it * 2 + 2)
                pe.wait_ge(S["xd"], it * 2 + 2)
                up(it, 0)
                pe.wait_ge(S["PG_ready"], it + 1)
                pe.wait_ge(S["acc_added"], it * 4 + 4)
                for a in range(2):
                    for n in range(NPAIR):
                        last = nc.tensor.transpose(ps[4 + a][:, 256 + 128 * n:384 + 128 * n],
                                                   PG[:, a, 2 * n:2 * n + 2, :], ident[:, :])
                    last.then_inc(S["gt_done"], 1)
                up(it, 1)
                pe.wait_ge(S["gm_act"], it + 1)
                turn(it, 0)
                pe.wait_ge(S["P_ready"], it + 2)
                gather_slices(0)
                gather_slices(1)
                down(it, 0)
                pe.wait_ge(S["gm_dve"], it + 1)
                turn(it, 1)
                pe.wait_ge(S["xa"], it * 2 + 3)
                gather_slices(2)
                pe.wait_ge(S["xd"], it * 2 + 3)
                gather_slices(3)
                down(it, 1)
                pe.wait_ge(S["xa"], it * 2 + 4)
                pe.wait_ge(S["xd"], it * 2 + 4)
                for a in range(2):
                    for n in range(NPAIR):
                        if a == 0:
                            pe.wait_ge(S["ya"], it * NPAIR + (n + 1))
                            pe.wait_ge(S["yd"], it * NPAIR + (n + 1))
                        for hf in range(2):
                            if a == 1 and n == 0:
                                pe.wait_ge(S["acc_added"], it * 4 + (5 + hf))
                            last = mm(ps[6 + hf][:, :], GmT[:, n, a, :], ysb[:, n, 512 * hf:512 * hf + 512],
                                      n == 0, n == NPAIR - 1)
                            if n == NPAIR - 1:
                                last.then_inc(S["comb_mm"], 1)

        @block.scalar
        def _(act):
            def copy(out_, in_, scale=1.0):
                return nc.scalar.activation(out_, in_, ACT.Copy, scale=scale)

            act.wait_ge(S["x_in"], 64)
            for a in range(2):
                nc.scalar.activation(xs[:, a, :], acc[:, D * a:D * a + D], ACT.Square, accum_out=ssx[:, a:a + 1]).then_inc(S["ssx_ready"], 1)
            act.wait_ge(S["gm_in"], 16)
            for k in range(1, KT, 2):
                act.wait_ge(S["xt_done"], k + 1)
                copy(hnC[:, k, :], ps[k][:, 0:256], scale=g_mix[:, k:k + 1])
                copy(chunked(hnT[:, k, :]), ps[k][:, 0:256].rearrange("p (a q c) -> p a q c", a=2, q=4),
                     scale=g_mix[:, k:k + 1]).then_inc(S["xT_odd"], 1)
            for i in range(2):
                act.wait_ge(S["par_t_done"], 2 + i)
                for half in range(2):
                    src = ps[5 + i][64 * half:64 * half + 64, :].rearrange("p (r i h) -> p r i h", r=PR, i=2)[:, :, half, :]
                    copy(Ct[i][64 * half:64 * half + 64, :, :], src).then_inc(S["ct_evac"], 1)
            act.wait_ge(S["par_evac"], 1)
            nc.scalar.activation(ls, ls, ACT.Exp).then_inc(S["step_ready"], 1)
            act.wait_ge(S["a_ready"], 1)
            nc.scalar.activation(mag, mag, ACT.Exp)
            nc.scalar.activation(rho, rho, ACT.Exp)
            act.wait_ge(S["th_ready"], 1)
            nc.scalar.activation(sinv, th, ACT.Sin)
            nc.scalar.activation(cosv, th, ACT.Sin, scale=0.5).then_inc(S["exps_ready"], 1)
            uvv = uev.rearrange("p (g a h) -> p a g h", g=G, a=2)
            for a in range(2):
                act.wait_ge(S["u_done"], a + 1)
                copy(uvv[:, a], ps[a][:, :].rearrange("p (g h) -> p g h", g=G)).then_inc(S["u_evac"], 1)
            for n in (0, 1):
                for a in range(2):
                    bank = ps[2 + n + 2 * a]
                    act.wait_ge(S["qk_done"], 2 * n + a + 1)
                    nc.scalar.activation(sqtmp[:, 1024 * a + 512 * n:1024 * a + 512 * n + 512], bank[:, :], ACT.Square)
                    copy(qk[:, a, 512 * n:512 * n + 512], bank[:, :]).then_inc(S["qk_evac"], 1)
            for a in range(2):
                act.wait_ge(S["v_done"], a + 1)
                copy(v[:, a, :], ps[6 + a][:, :]).then_inc(S["v_evac"], 1)
            for n in range(0, 8, 2):
                act.wait_ge(S["E_done"], n + 1)
                copy(Em[:, 512 * n:512 * n + 512], ps[0][:, :]).then_inc(S["E_act"], 1)
            act.wait_ge(S["E_done"], 8)
            for half in range(2):
                act.wait_ge(S["K_done"], half + 1)
                for m in range(4):
                    copy(Kv[:, 2 * m + half:G:8, :],
                         ps[half][32 * m:32 * m + H, :].rearrange("p (n x) -> p n x", n=4)).then_inc(S["K_evac"], 1)
            act.wait_ge(S["V_done"], 1)
            act.wait_ge(S["qk_normed"], 2)
            copy(Vs[:, 0:512], ps[0][:, :]).then_inc(S["V_act"], 1)
            act.wait_ge(S["gq_ready"], 1)
            for n in (0, 1):
                act.wait_ge(S["qkT_done"], n + 1)
                copy(qT[:, 2 * n:2 * n + 2, :], ps[2 + n][:, :].rearrange("p (m t) -> p m t", m=2), scale=gq).then_inc(S["qkT_act"], 1)

            def exp_log(h):
                act.wait_ge(S["zc_ready"], h + 1)
                nc.scalar.activation(attE[h % 2], attE[h % 2], ACT.Exp).then_inc(S["e_ready"], 1)
                act.wait_ge(S["e_ready"], h + 1)
                nc.scalar.activation(attE[h % 2], attE[h % 2], ACT.Ln, bias=ones_col).then_inc(S["ln_ready"], 1)

            def weights(h):
                act.wait_ge(S["zi_done"], h + 1)
                if h >= 2:
                    act.wait_ge(S["pv_done"], h - 1)
                nc.scalar.activation(attW[h % 2], ps[2 + h % 4][:, 0:384], ACT.Exp).then_inc(S["w_ready"], 1)

            def evac_pv(m):
                act.wait_ge(S["pv_done"], 2 * m + 2)
                src = ps[6 + m % 2][:, 0:256].rearrange("p (c q a) -> p a q c", q=4, a=2)
                nc.scalar.activation(sqa[:, m, :].rearrange("p (a q c) -> p a q c", a=2, q=4), src, ACT.Square)
                copy(mixT[:, 4 + m, :].rearrange("p (a q c) -> p a q c", a=2, q=4), src, scale=g_oa[:, m:m + 1]).then_inc(S["pv_act"], 1)

            nc.scalar.preload_act_table_set("natural_log_exp_and_others")
            exp_log(0)
            for h in range(NH):
                if h + 1 < NH:
                    exp_log(h + 1)
                weights(h)
                if h >= 3 and h % 2 == 1:
                    evac_pv((h - 3) // 2)
            evac_pv(3)
            for i in range(2):
                act.wait_ge(S["y5_done"], i + 1)
                nc.scalar.activation(ygel.rearrange("p (j i b h) -> p b i j h", j=L, i=4, b=2)[:, i],
                                     ps[i][:, :].rearrange("p (i j h) -> p i j h", i=4, j=L), ACT.Gelu_apprx_tanh).then_inc(S["y5_gelu"], 1)
            act.wait_ge(S["yT_done"], 1)
            copy(mixV[:, 0], ps[0][:, :].rearrange("p (q m c) -> p q m c", q=4, m=4)).then_inc(S["yT_act"], 1)
            for m in range(4):
                act.wait_ge(S["zg_done"], 2 * (m // 2) + 2)
                nc.scalar.activation(sigt[:, m, :], ps[m // 2][:, 256 * (m % 2):256 * (m % 2) + 256], ACT.Sigmoid,
                                     bias=b_glu[:, m:m + 1]).then_inc(S["sig_ready"], 1)
            for a in range(2):
                act.wait_ge(S["h_ready"], 1 + a)
                nc.scalar.activation(sqtmp[:, 1024 * a:1024 * a + 1024], acc[:, D * a:D * a + D], ACT.Square,
                                     accum_out=ssx[:, a:a + 1]).then_inc(S["ssh_ready"], 1)
            for k in (2, 3, 6, 7):
                act.wait_ge(S["hT_done"], k // 2 + 1)
                last = copy(hT[:, k, :], ps[2 + k // 2][:, 256 * (k % 2):256 * (k % 2) + 256], scale=g_ffn[:, k:k + 1])
                if k % 2 == 1:
                    last.then_inc(S["hT_act"], 1)
            act.wait_ge(S["rsh_ready"], 1)
            act.wait_ge(S["lg_done"], 1)
            for a in range(2):
                last = nc.scalar.activation(scores[:, a], ps[7][:, E * a:E * a + E], ACT.Sigmoid, scale=rsh[:, a:a + 1])
            last.then_inc(S["scores_ready"], 1)
            act.wait_ge(S["hs_ready"], 2)
            copy(parts[0], hs).then_inc(S["p1_ready"], 1)
            act.wait_ge(S["rest_ready"], 1)
            copy(parts[1], rest).then_inc(S["p2_ready"], 1)
            def shared_silu(a):
                act.wait_ge(S["sh_up"], a + 1)
                nc.scalar.activation(silu_o[a], ps[a][:, 0:256], ACT.Silu, scale=rsh[:, a:a + 1]).then_inc(S["sh_silu"], 1)

            shared_silu(0)
            act.wait_ge(S["pgT_done"], 1)
            copy(pgT, ps[7][0:E, :].rearrange("p (w a t) -> p w a t", w=2, a=2)).then_inc(S["pgT_evac"], 1)
            shared_silu(1)

            def gathered(g, n):
                act.wait_ge(S["gath_done"], g * 4 + (2 * n + 1))
                for k in (4 * n, 4 * n + 1):
                    last = copy(xTg[:, k, :], ps[6][:, 256 * (k % 2):256 * (k % 2) + 256], scale=g_ffn[:, k:k + 1])
                last.then_inc(S["xa"], 1)

            def silu(it, p):
                act.wait_ge(S["up_done"], it * NPAIR + (p + 1))
                nc.scalar.activation(silu_o[p], ps[p][:, 0:256], ACT.Silu).then_inc(S["silu_done"], 1)

            def turned(it, p):
                act.wait_ge(S["t_done"], it * NPAIR + (p + 1))
                copy(actT[p], ps[4 + p][:, 0:256].rearrange("p (j s) -> p j s", j=2)).then_inc(S["actT_ready"], 1)

            def y_out(it, p):
                act.wait_ge(S["down_done"], it * NPAIR + (p + 1))
                copy(ysb[:, p, 0:512], ps[2][:, :]).then_inc(S["ya"], 1)

            gathered(0, 0)
            gathered(0, 1)
            for a in range(2):
                act.wait_ge(S["sh_T"], a + 1)
                copy(actT[a], ps[4 + a][:, 0:256].rearrange("p (j s) -> p j s", j=2)).then_inc(S["sh_actT"], 1)
            act.wait_ge(S["route_ready"], 1)
            n_it = act.value_load(n_iter[0:1, :], min_val=NB, max_val=MAX_ITER)
            with act.Fori(0, n_it) as it:
                silu(it, 0)
                act.wait_ge(S["gt_done"], it * 2 + 1)
                copy(GmT[:, :, 0, :], ps[4][:, 256:512].rearrange("p (n t) -> p n t", n=NPAIR)).then_inc(S["gm_act"], 1)
                silu(it, 1)
                turned(it, 0)
                gathered(it + 1, 0)
                y_out(it, 0)
                turned(it, 1)
                gathered(it + 1, 1)
                y_out(it, 1)

        @block.vector
        def _(dve):
            n = [0]

            def step(ins):
                n[0] += 1
                ins.then_inc(S["dve_chain"], 1)
                dve.wait_ge(S["dve_chain"], n[0])

            def tt(out_, a, b, op):
                return nc.vector.tensor_tensor(out_, a, b, op)

            def ts(out_, a, s1, op0, s2=None, op1=ALU.bypass):
                return nc.vector.tensor_scalar(out_, a, s1, s2, op0, op1)

            def stt(out_, a, s1, b, op0, op1):
                return nc.vector.scalar_tensor_tensor(out=out_, in0=a, scalar=s1, in1=b, op0=op0, op1=op1)

            def rsqrt_of_mean(ss, w, count):
                m, y, t = nm[:, 0:w], ny[:, 0:w], nt[:, 0:w]
                step(ts(m, ss, 1.0 / count, ALU.mult, EPS, ALU.add))
                ts(nh[:, 0:w], m, -0.5, ALU.mult)
                step(ts(y.bitcast(I32), m.bitcast(I32), -0.5, ALU.mult, RSQRT_MAGIC, ALU.add))
                for _ in range(3):
                    step(tt(t, y, y, ALU.mult))
                    step(tt(t, t, nh[:, 0:w], ALU.mult))
                    step(stt(y, t, 1.5, y, ALU.add, ALU.mult))
                return y

            def cmul(outs, x, y, tmps, done=step):
                ta, tb, tc, td = tmps
                tt(ta, x[0], y[0], ALU.mult)
                tt(tb, x[1], y[1], ALU.mult)
                tt(tc, x[0], y[1], ALU.mult)
                step(tt(td, x[1], y[0], ALU.mult))
                tt(outs[0], ta, tb, ALU.subtract)
                done(tt(outs[1], tc, td, ALU.add))

            nc.vector.memset(negones[:, :], -1.0)
            nc.vector.memset(ones_col, 1.0).then_inc(S["ones_ready"], 1)
            dve.wait_ge(S["ssx_ready"], 2)
            y = rsqrt_of_mean(ssx, 2, D)
            for a in range(2):
                ts(xs[:, a, :], acc[:, D * a:D * a + D], y[:, a:a + 1], ALU.mult).then_inc(S["xs_ready"], 1)
            dve.wait_ge(S["params_in"], 16 * 4)
            nc.vector.tensor_copy(prm3[0:PR, :].rearrange("p (i s) -> p i s", i=2),
                                  ls2[0:PR, :].unsqueeze(2).to_broadcast([PR, 2, P])).then_inc(S["spread_ready"], 1)
            dve.wait_ge(S["gm_in"], 16)
            for k in range(0, KT, 2):
                dve.wait_ge(S["xt_done"], k + 1)
                ts(hnC[:, k, :], ps[k][:, 0:256], g_mix[:, k:k + 1], ALU.mult)
                ts(chunked(hnT[:, k, :]), ps[k][:, 0:256].rearrange("p (a q c) -> p a q c", a=2, q=4),
                   g_mix[:, k:k + 1], ALU.mult).then_inc(S["xT_even"], 1)
            dve.wait_ge(S["par_t_done"], 1)
            ts(lr, ps[7][:, 0:16], -1e-4, ALU.min)
            nc.vector.tensor_copy(li, ps[7][:, 16:32])
            nc.vector.tensor_copy(ls, ps[7][:, 32:48])
            nc.vector.tensor_copy(dT[0:H, :], ps[7][0:H, 64:96]).then_inc(S["par_evac"], 1)
            dve.wait_ge(S["par_evac"], 1)
            dve.wait_ge(S["step_ready"], 1)
            step(tt(mag, lr, ls, ALU.mult))
            ts(rho, mag, float(L), ALU.mult).then_inc(S["a_ready"], 1)
            step(tt(th, li, ls, ALU.mult))
            step(ts(t1, th, 1.0 / TWO_PI, ALU.mult, ROUND_MAGIC, ALU.add))
            step(ts(t1, t1, ROUND_MAGIC, ALU.subtract))
            for part in two_pi_parts():
                step(stt(th, t1, -part, th, ALU.mult, ALU.add))
            ts(th, th, PI_DOWN, ALU.min, -PI_DOWN, ALU.max).then_inc(S["th_ready"], 1)
            dve.wait_ge(S["exps_ready"], 1)
            step(tt(cosv, cosv, cosv, ALU.mult))
            step(ts(cosv, cosv, -2.0, ALU.mult, 1.0, ALU.add))
            tt(lbr, mag, cosv, ALU.mult)
            step(tt(lbi, mag, sinv, ALU.mult))
            ts(t1, lbr, -1.0, ALU.add)
            tt(t2, lr, lr, ALU.mult)
            step(tt(t3, li, li, ALU.mult))
            step(tt(t2, t2, t3, ALU.add))
            step(nc.vector.reciprocal(den, t2))
            tt(t2, t1, lr, ALU.mult)
            step(tt(t3, lbi, li, ALU.mult))
            step(tt(t2, t2, t3, ALU.add))
            tt(cor, t2, den, ALU.mult)
            tt(t3, lbi, lr, ALU.mult)
            step(tt(t4, t1, li, ALU.mult))
            step(tt(t3, t3, t4, ALU.subtract))
            step(tt(coi, t3, den, ALU.mult))

            def over_h(w):
                return w.unsqueeze(2).to_broadcast([128, PR, H])

            big = [scan_t[i] for i in range(8)]
            dve.wait_ge(S["b_in"], 32)
            dve.wait_ge(S["par_t_done"], 3)
            tv = [big[i][:, 0:PR * H].rearrange("p (r h) -> p r h", r=PR) for i in range(4)]
            cmul(Bbar, Braw, [over_h(cor), over_h(coi)], tv, lambda ins: ins.then_inc(S["Bbar_ready"], 1))
            dve.wait_ge(S["Bbar_ready"], 1)
            nc.vector.memset(PW[0][:, 0, :], 1.0)
            nc.vector.memset(PW[1][:, 0, :], 0.0)
            nc.vector.tensor_copy(PW[0][:, 1, :], lbr)
            step(nc.vector.tensor_copy(PW[1][:, 1, :], lbi))
            for have in (1, 2, 4):
                by = [PW[i][:, have:have + 1, :].to_broadcast([128, have, PR]) for i in range(2)]
                tw = [big[i][:, 0:have * PR].rearrange("p (k r) -> p k r", k=have) for i in range(4)]
                cmul([PW[i][:, have + 1:2 * have + 1, :] for i in range(2)],
                     [PW[i][:, 1:have + 1, :] for i in range(2)], by, tw)

            def products(outs, mats, ks, sign, turn):
                for j, k in enumerate(ks):
                    w = [over_h(PW[i][:, k, :]) for i in range(2)]
                    tmps = [big[4 * ((j + turn) % 2) + i][:, 0:256].rearrange("p (r h) -> p r h", r=PR) for i in range(4)]
                    ta, tb, tc, td = tmps
                    tt(ta, mats[0], w[0], ALU.mult)
                    tt(tb, mats[1], w[1], ALU.mult)
                    tt(tc, mats[0], w[1], ALU.mult)
                    step(tt(td, mats[1], w[0], ALU.mult))
                    last = tt(outs[0][:, :, j, :], ta, tb, ALU.subtract)
                    if sign > 0:
                        last = tt(outs[1][:, :, j, :], tc, td, ALU.add)
                    else:
                        last = stt(outs[1][:, :, j, :], tc, -1.0, td, ALU.mult, ALU.subtract)
                return last

            dve.wait_ge(S["ct_evac"], 4)
            products(GmV, Ct, list(range(L + 1)), -1, 0).then_inc(S["G_ready"], 1)
            products(EtV, Bbar, [L - 1 - j for j in range(L)], 1, 1).then_inc(S["Et_ready"], 1)
            dve.wait_ge(S["u_evac"], 2)
            nc.vector.transpose(U, uev).then_inc(S["U_ready"], 1)
            dve.wait_ge(S["qk_evac"], 4)
            for a in range(2):
                last = nc.vector.tensor_reduce(ssqk[:, 16 * a:16 * a + 16], sqtmp[:, 1024 * a:1024 * a + 1024].rearrange("p (h d) -> p h d", d=DH),
                                        AX.X, ALU.add)
            step(last)
            y = rsqrt_of_mean(ssqk, 32, DH)
            for a in range(2):
                q3 = qk[:, a, :].rearrange("p (h d) -> p h d", d=DH)
                tt(q3, q3, y[:, 16 * a:16 * a + 16].unsqueeze(2).to_broadcast([128, 16, DH]), ALU.mult).then_inc(S["qk_normed"], 1)
            dve.wait_ge(S["gains_in"], 16 * 8)
            ts(gq, gq, float(DH) ** -0.5, ALU.mult).then_inc(S["gq_ready"], 1)
            for n_ in range(1, 8, 2):
                dve.wait_ge(S["E_done"], n_ + 1)
                nc.vector.tensor_copy(Em[:, 512 * n_:512 * n_ + 512], ps[1][:, :]).then_inc(S["E_dve"], 1)
            dve.wait_ge(S["U_ready"], 1)
            cur, nxt = [cosv, sinv], [t1, t2]
            tq = [t3, t4, e8r, e8i]
            for _ in range(3):
                cmul(nxt, cur, cur, tq)
                cur, nxt = nxt, cur
            nc.vector.memset(rot[0][:, 0, :], 1.0)
            nc.vector.memset(rot[1][:, 0, :], 0.0)
            nc.vector.tensor_copy(rot[0][:, 1, :], cur[0])
            step(nc.vector.tensor_copy(rot[1][:, 1, :], cur[1]))
            for have in (1, 2, 4, 8, 16):
                by = [rot[i][:, have:have + 1, :].to_broadcast([128, have, PR]) for i in range(2)]
                tw = [rtmp[i][:, 0:have * PR].rearrange("p (k r) -> p k r", k=have) for i in range(4)]
                cmul([rot[i][:, have + 1:2 * have + 1, :] for i in range(2)],
                     [rot[i][:, 1:have + 1, :] for i in range(2)], by, tw)
            dve.wait_ge(S["ident_ready"], 1)
            step(tt(Kdiag, ident[0:H, 0:H].unsqueeze(1).to_broadcast([H, G, H]),
                    dT[0:H, :].unsqueeze(2).to_broadcast([H, G, H]), ALU.mult))
            dve.wait_ge(S["K_evac"], 8)
            tt(Kv[:, :, 0:H], Kv[:, :, 0:H], Kdiag, ALU.add).then_inc(S["diag_ready"], 1)
            dve.wait_ge(S["V_done"], 2)
            nc.vector.tensor_copy(Vs[:, 512:1024], ps[1][:, :]).then_inc(S["V_dve"], 1)
            s3 = [w.rearrange("p (r c) -> p r c", r=PR) for w in scan_t]
            s4 = [w.rearrange("p (q r c) -> p q r c", q=4, r=4) for w in scan_t]
            V4 = [ps[i][:, :].rearrange("p (r q c) -> p q r c", r=4, q=4) for i in range(2)]
            R1 = [w[:, 1:33, :].rearrange("p c r -> p r c") for w in rot]
            R4 = [w[:, 1:33, :].rearrange("p c (q r) -> p q r c", q=4) for w in rot]
            def scan_turn():
                dve.wait_ge(S["VT_done"], 2)
                tt(s4[0], V4[0], R4[0], ALU.mult)
                tt(s4[1], V4[1], R4[1], ALU.mult)
                tt(s4[2], V4[1], R4[0], ALU.mult)
                tt(s4[3], V4[0], R4[1], ALU.mult)
                step(nc.vector.tensor_copy(s3[6], rho.unsqueeze(2).to_broadcast([128, PR, C])))
                nc.vector.memset(s3[6][:, :, 0:1], 0.0)
                tt(s3[0], s3[0], s3[1], ALU.add)
                step(tt(s3[2], s3[2], s3[3], ALU.subtract))

            def scan_run():
                nc.vector.tensor_tensor_scan(scan_t[1], scan_t[6], scan_t[0], 0.0, ALU.mult, ALU.add)
                step(nc.vector.tensor_tensor_scan(scan_t[3], scan_t[6], scan_t[2], 0.0, ALU.mult, ALU.add))

            def scan_back():
                w = C - 1
                Rw = [x[:, :, 0:w] for x in R1]
                g_r, g_i = s3[1][:, :, 0:w], s3[3][:, :, 0:w]
                tt(s3[0][:, :, 0:w], g_r, Rw[0], ALU.mult)
                tt(s3[2][:, :, 0:w], g_i, Rw[1], ALU.mult)
                tt(s3[6][:, :, 0:w], g_r, Rw[1], ALU.mult)
                step(tt(s3[7][:, :, 0:w], g_i, Rw[0], ALU.mult))
                nc.vector.memset(s3[4][:, :, 0:1], 0.0)
                nc.vector.memset(s3[5][:, :, 0:1], 0.0)
                tt(s3[4][:, :, 1:C], s3[0][:, :, 0:w], s3[2][:, :, 0:w], ALU.subtract)
                tt(s3[5][:, :, 1:C], s3[6][:, :, 0:w], s3[7][:, :, 0:w], ALU.add).then_inc(S["S_ready"], 1)

            for n_ in (2, 3):
                dve.wait_ge(S["qkT_done"], n_ + 1)
                ts(kT[:, 2 * n_ - 4:2 * n_ - 2, :], ps[2 + n_][:, :].rearrange("p (m t) -> p m t", m=2), gk, ALU.mult).then_inc(S["qkT_dve"], 1)

            def clamp(h):
                dve.wait_ge(S["z_done"], h + 1)
                if h >= 2:
                    dve.wait_ge(S["sp_ready"], h - 1)
                ts(attE[h % 2], ps[2 + h % 4][:, 0:384], 80.0, ALU.min).then_inc(S["zc_ready"], 1)

            def softplus(h):
                dve.wait_ge(S["ln_ready"], h + 1)
                if h >= 2:
                    dve.wait_ge(S["zi_done"], h - 1)
                tt(attL[h % 2], attE[h % 2], ps[2 + h % 4][:, 0:384], ALU.max).then_inc(S["sp_ready"], 1)

            clamp(0)
            for h in range(NH):
                if h + 1 < NH:
                    clamp(h + 1)
                softplus(h)
                if h < 3:
                    (scan_turn, scan_run, scan_back)[h]()
            dve.wait_ge(S["sso_done"], 1)
            step(nc.vector.tensor_copy(sso[:, 2:4], ps[7][:, 2:4]))
            y = rsqrt_of_mean(sso[:, 2:4], 2, DS)
            step(nc.vector.tensor_copy(rso[:, 2:4], y))
            def add_projection(a, hf, bank, col):
                part = acc[:, D * a + 512 * hf:D * a + 512 * hf + 512]
                return stt(part, bank[:, :], rso[:, col + a:col + a + 1], part, ALU.mult, ALU.add)

            def add_attention(a):
                for hf in range(2):
                    dve.wait_ge(S["opa_done"], 2 * a + hf + 1)
                    last = add_projection(a, hf, ps[2 + 2 * a + hf], 2)
                last.then_inc(S["oa_added"], 1)

            add_attention(0)
            dve.wait_ge(S["yT_done"], 2)
            nc.vector.tensor_copy(mixV[:, 1], ps[1][:, :].rearrange("p (q m c) -> p q m c", q=4, m=4)).then_inc(S["yT_dve"], 1)
            dve.wait_ge(S["zg_done"], 4)
            for m in range(4):
                dve.wait_ge(S["sig_ready"], m + 1)
                last = tt(mixT[:, m, :], mixT[:, m, :], sigt[:, m, :], ALU.mult)
            step(last)
            for m in range(4):
                tt(sqs[:, m, :], mixT[:, m, :], mixT[:, m, :], ALU.mult).then_inc(S["sqs_ready"], 1)
            for m in range(4):
                ts(mixT[:, m, :], mixT[:, m, :], g_os[:, m:m + 1], ALU.mult).then_inc(S["ys_ready"], 1)
            add_attention(1)
            dve.wait_ge(S["sso_done"], 2)
            nc.vector.tensor_copy(sso[:, 0:2], ps[7][:, 0:2]).then_inc(S["sso_evac"], 1)
            dve.wait_ge(S["sso_evac"], 1)
            y = rsqrt_of_mean(sso[:, 0:2], 2, DS)
            step(nc.vector.tensor_copy(rso[:, 0:2], y))
            for a in range(2):
                dve.wait_ge(S["oa_added"], a + 1)
                for hf in range(2):
                    dve.wait_ge(S["ops_done"], 2 * a + hf + 1)
                    last = add_projection(a, hf, ps[(0, 1, 6, 7)[2 * a + hf]], 0)
                last.then_inc(S["h_ready"], 1)
            for k in (0, 1, 4, 5):
                dve.wait_ge(S["hT_done"], k // 2 + 1)
                last = ts(hT[:, k, :], ps[2 + k // 2][:, 256 * (k % 2):256 * (k % 2) + 256], g_ffn[:, k:k + 1], ALU.mult)
                if k % 2 == 1:
                    last.then_inc(S["hT_dve"], 1)
            dve.wait_ge(S["ssh_ready"], 2)
            y = rsqrt_of_mean(ssx, 2, D)
            nc.vector.tensor_copy(rsh, y).then_inc(S["rsh_ready"], 1)
            for a in range(2):
                ts(hs[:, a], acc[:, D * a:D * a + D].rearrange("p (m k) -> p k m", k=KT), y[:, a:a + 1], ALU.mult).then_inc(S["hs_ready"], 1)

            dve.wait_ge(S["scores_ready"], 1)
            dve.wait_ge(S["bias_in"], 16)
            step(tt(biased, scores, bias_bc.unsqueeze(1).to_broadcast([128, 2, E]), ALU.add))
            for a in range(2):
                for g in range(NG):
                    last = nc.vector.max(m8[:, a, g, :], biased[:, a, GE * g:GE * g + GE])
            step(last)
            step(tt(gs, m8[:, :, :, 0], m8[:, :, :, 1], ALU.add))
            gi = gs.unsqueeze(3).to_broadcast([128, 2, NG, NG])
            gj = gs.unsqueeze(2).to_broadcast([128, 2, NG, NG])
            tt(gt_c, gj, gi, ALU.is_gt)
            step(tt(eq_c, gj, gi, ALU.is_equal))
            dve.wait_ge(S["lower_ready"], 1)
            step(tt(eq_c, eq_c, lower.unsqueeze(1).to_broadcast([128, 2, NG, NG]), ALU.mult))
            step(tt(gt_c, gt_c, eq_c, ALU.add))
            step(nc.vector.tensor_reduce(rk1, gt_c, AX.X, ALU.add))
            step(ts(gmask, rk1, float(TOPG), ALU.is_lt))
            dve.wait_ge(S["p1_ready"], 1)
            tt(rest, hs, parts[0], ALU.subtract).then_inc(S["rest_ready"], 1)
            step(ts(rk1, gmask, -1.0, ALU.add, BIG, ALU.mult))
            b4 = biased.rearrange("p a (g x) -> p a g x", g=NG)
            s4 = sel.rearrange("p a (g x) -> p a g x", g=NG)
            step(tt(s4, b4, gmask.unsqueeze(3).to_broadcast([128, 2, NG, GE]), ALU.mult))
            step(tt(s4, s4, rk1.unsqueeze(3).to_broadcast([128, 2, NG, GE]), ALU.add))
            for a in range(2):
                step(nc.vector.max(top8[:, a, :], sel[:, a, :]))
                step(nc.vector.match_replace(out=repl[:, a, :], in_to_replace=top8[:, a, :], in_values=sel[:, a, :], imm_value=BIG))
            step(tt(mask, repl, sel, ALU.not_equal))
            nc.vector.tensor_copy(mask_b, mask).then_inc(S["mask_ready"], 1)
            step(tt(gate_r, scores, mask, ALU.mult))
            step(nc.vector.tensor_reduce(gsum, gate_r, AX.X, ALU.add))
            step(nc.vector.reciprocal(gsum, gsum))
            for a in range(2):
                ts(gate[:, a, 0:E], gate_r[:, a, :], gsum[:, a:a + 1], ALU.mult, ROUTED_SCALE, ALU.mult)
            for t in (pos, gate):
                nc.vector.memset(t[:, :, E + MAX_EXTRA:COLS], 0.0)
            dve.wait_ge(S["pos_done"], 1)
            tt_pos = stt(pos[:, :, 0:E], ps[6][:, 0:2 * E].rearrange("p (a e) -> p a e", a=2), 1.0, mask, ALU.add, ALU.mult)
            tt_pos.then_inc(S["slots_ready"], 1)
            dve.wait_ge(S["rx_ready"], 1)
            step(nc.vector.tensor_copy(cnt[0:E, :], ps[6][0:E, 2 * E:2 * E + 1]))
            step(ts(more[0:E, :], cnt[0:E, :], float(SLOTS), ALU.is_gt))
            for most in range(2 * SLOTS, T, SLOTS):
                step(stt(more[0:E, :], cnt[0:E, :], float(most), more[0:E, :], ALU.is_gt, ALU.add))
            nc.vector.tensor_copy(more_b[0:E, :], more[0:E, :]).then_inc(S["cnt_done"], 1)
            def place(g):
                nc.vector.tensor_copy(gate_b, gate[:, :, bass.ds(g * EB, EB)])
                nc.vector.tensor_copy(pos_b, pos[:, :, bass.ds(g * EB, EB)]).then_inc(S["slots_copied"], 1)
                dve.wait_ge(S["slots_copied"], g + 1)
                for a in range(2):
                    last = tt(Pm[:, a], iota.unsqueeze(1).to_broadcast([128, EB, SLOTS]),
                              pos_b[:, a].unsqueeze(2).to_broadcast([128, EB, SLOTS]), ALU.is_equal)
                last.then_inc(S["P_ready"], 1)

            def place_gates(g):
                dve.wait_ge(S["P_ready"], g + 1)
                for a in range(2):
                    last = tt(PG[:, a], Pm[:, a], gate_b[:, a].unsqueeze(2).to_broadcast([128, EB, SLOTS]), ALU.mult)
                last.then_inc(S["PG_ready"], 1)

            dve.wait_ge(S["iota_ready"], 1)
            place(0)
            dve.wait_ge(S["first_done"], 1)
            nc.vector.tensor_copy(first[0:E, :], ps[6][0:E, 2 * E + 1:2 * E + 2])
            step(ts(extra_its, ps[6][:, 2 * E + 2:2 * E + 3], 1.0 / EB, ALU.mult, NB + 0.5 - 0.5 / EB, ALU.add))
            ts(depth[0:E, :], iota_x[0:E, :], first[0:E, :], ALU.subtract)
            step(ts(extra_its, extra_its, ROUND_MAGIC, ALU.add))
            step(ts(extra_its, extra_its, ROUND_MAGIC, ALU.subtract))
            nc.vector.tensor_copy(n_iter, extra_its)
            step(ts(selx[0:E, :], depth[0:E, :], more[0:E, :], ALU.is_lt))
            step(stt(selx[0:E, :], depth[0:E, :], 0.0, selx[0:E, :], ALU.is_ge, ALU.mult))
            step(ts(depth[0:E, :], depth[0:E, :], -float(SLOTS), ALU.mult, -float(SLOTS), ALU.add))
            tt(offs[0:E, :], depth[0:E, :], selx[0:E, :], ALU.mult).then_inc(S["selx_ready"], 1)
            def gathered(g, n):
                dve.wait_ge(S["gath_done"], g * 4 + (2 * n + 2))
                for k in (4 * n + 2, 4 * n + 3):
                    last = ts(xTg[:, k, :], ps[7][:, 256 * (k % 2):256 * (k % 2) + 256], g_ffn[:, k:k + 1], ALU.mult)
                last.then_inc(S["xd"], 1)

            place_gates(0)
            dve.wait_ge(S["extra_done"], 1)
            X = MAX_EXTRA
            nc.vector.tensor_copy(pos[:, :, E:E + X], ps[6][:, 0:2 * X].rearrange("p (a k) -> p a k", a=2))
            nc.vector.tensor_copy(gate[:, :, E:E + X], ps[6][:, 2 * X:4 * X].rearrange("p (a k) -> p a k", a=2))
            nc.vector.tensor_copy(experts[0:1, :], ps[6][0:1, 4 * X:5 * X]).then_inc(S["route_ready"], 1)
            for a in range(2):
                dve.wait_ge(S["sh_silu"], a + 1)
                stt(act_o[a], ps[a][:, 256:512], rsh[:, a:a + 1], silu_o[a], ALU.mult, ALU.mult).then_inc(S["sh_act"], 1)
            gathered(0, 0)
            gathered(0, 1)
            for a in range(2):
                for hf in range(2):
                    dve.wait_ge(S["shd_done"], 2 * a + hf + 1)
                    part = acc[:, D * a + 512 * hf:D * a + 512 * hf + 512]
                    tt(part, part, ps[2 + 2 * a + hf][:, :], ALU.add).then_inc(S["acc_added"], 1)

            def activate(it, p):
                dve.wait_ge(S["silu_done"], it * NPAIR + (p + 1))
                tt(act_o[p], silu_o[p], ps[p][:, 256:512], ALU.mult).then_inc(S["act_ready"], 1)

            def y_out(it, p):
                dve.wait_ge(S["down_done"], it * NPAIR + (p + 1))
                nc.vector.tensor_copy(ysb[:, p, 512:1024], ps[3][:, :]).then_inc(S["yd"], 1)

            dve.wait_ge(S["route_ready"], 1)
            n_it = dve.value_load(n_iter[0:1, :], min_val=NB, max_val=MAX_ITER)
            with dve.Fori(0, n_it) as it:
                dve.wait_ge(S["PG_ready"], it + 1)
                place(it + 1)
                activate(it, 0)
                dve.wait_ge(S["gt_done"], it * 2 + 2)
                nc.vector.tensor_copy(GmT[:, :, 1, :], ps[5][:, 256:512].rearrange("p (n t) -> p n t", n=NPAIR)).then_inc(S["gm_dve"], 1)
                place_gates(it + 1)
                activate(it, 1)
                gathered(it + 1, 0)
                y_out(it, 0)
                gathered(it + 1, 1)
                y_out(it, 1)
                dve.wait_ge(S["acc_added"], it * 4 + 4)
                for c in range(4):
                    dve.wait_ge(S["comb_mm"], it * 4 + (c + 1))
                    part = acc[:, 512 * c:512 * c + 512]
                    tt(part, part, ps[6 + c % 2][:, :], ALU.add).then_inc(S["acc_added"], 1)


_INS = ["x", "g_mix", "w_in", "lam_re", "lam_im", "b_re", "b_im", "c_re", "c_im", "d_skip", "log_step", "w_glu",
        "b_glu", "g_q", "g_k", "g_out_ssm", "g_out_att", "w_out", "g_ffn", "w_router", "router_bias", "e_w1", "e_w3",
        "e_w2", "s_w1", "s_w3", "s_w2"]


def kernel(**inputs):
    import numpy as _np
    import concourse.bacc as _bacc
    from concourse import mybir as _mybir
    from concourse.bass_utils import run_bass_kernel_spmd as _run

    nc = _bacc.Bacc("TRN2", target_bir_lowering=False, num_devices=1)
    arrays, args = {}, {}
    for name in _INS:
        a = _np.ascontiguousarray(inputs[name])
        arrays[f"in_{name}"] = a
        args[name] = nc.dram_tensor(f"in_{name}", a.shape, _mybir.dt.from_np(a.dtype), kind="ExternalInput").ap()
    out = nc.dram_tensor("out_h", (1, T, D), FP32, kind="ExternalOutput").ap()
    build(nc, args, out)
    r = _run(nc, [arrays], core_ids=[0])
    return r.results[0]["out_h"]
```

```python
from contextlib import ExitStack

import numpy as np

import concourse.bass as bass
from concourse import mybir

FP32 = mybir.dt.float32
BF16 = mybir.dt.bfloat16
I32 = mybir.dt.int32
ALU = mybir.AluOpType
ACT = mybir.ActivationFunctionType
AX = mybir.AxisListType

D = 1024
T = 256
DS = 512
KT = D // 128
G, P, H = 32, 64, 16
PR = G // 2
L = 8
C = T // L
NH, DH = 8, 64
E, TOPK, NG, GE, TOPG = 64, 8, 8, 8, 4
F = 256
SLOTS = 64
EB = 4
NB = E // EB
NPAIR = EB // 2
MAX_EXTRA = 32
assert MAX_EXTRA % EB == 0 and MAX_EXTRA >= T * TOPK // (SLOTS + 1)
COLS = E + MAX_EXTRA + EB
MAX_FULL = NB + MAX_EXTRA // EB
EPS = 1e-6
ROUTED_SCALE = 2.5
BIG = 3.0e38
TWO_PI = 2 * np.pi
PI_DOWN = 3.1415925
ROUND_MAGIC = 12582912.0
RSQRT_MAGIC = 1597463007.0


def two_pi_parts():
    parts, rest = [], TWO_PI
    for bits in (10, 10, 24):
        scale = 2.0 ** (bits - 1 - np.floor(np.log2(abs(rest))))
        part = float(np.round(rest * scale) / scale)
        parts.append(float(np.float32(part)))
        rest -= parts[-1]
    return parts


def build(nc, I, out):
    ctx = ExitStack()
    with ctx:
        def sb(name, words, dt=FP32, parts=128):
            return ctx.enter_context(nc.sbuf_tensor(name, [parts, words], dt))

        def sem(name):
            return ctx.enter_context(nc.semaphore(name))

        SLOT_W = 3 * 2048
        ring = sb("ring", 4 * SLOT_W)
        wreg = sb("wreg", 16384)
        acc = sb("acc", 2048)
        reg_a = sb("reg_a", 2048)
        reg_b = sb("reg_b", 2048)
        reg_c = sb("reg_c", 3072)
        reg_d = sb("reg_d", 2304)
        ident = sb("ident", 128)
        small = sb("small", 600)
        ps = [ctx.enter_context(nc.psum_tensor(f"bank{i}", [128, 512], FP32)) for i in range(8)]

        taken = {}

        def piece(region, words, size):
            at = taken.get(words, 0)
            taken[words] = at + size
            assert at + size <= region.shape[1], (words, at + size)
            return region[:, at:at + size]

        Et = [piece(ring, "s5", 2048) for _ in range(2)]
        EtV = [e.rearrange("p (r j h) -> p r j h", r=PR, j=L) for e in Et]
        Gm = [piece(ring, "s5", PR * 9 * H) for _ in range(2)]
        GmV = [g.rearrange("p (r j h) -> p r j h", r=PR, j=9) for g in Gm]
        Tm = piece(ring, "s5", G * 128)
        TmV = Tm.rearrange("p (g n) -> p g n", g=G)
        Em = piece(ring, "s5", PR * 2 * 128)
        EmV = Em.rearrange("p (r i s) -> p r i s", r=PR, i=2)
        U = piece(ring, "s5", G * C)
        UV = U.rearrange("p (g c) -> p g c", g=G)
        uev = piece(ring, "s5", 1024)
        par = lambda n: piece(ring, "s5", n)
        lr, li, ls, mag, th, cosv, sinv, lbr, lbi, t1, t2, t3, t4, cor, coi, den, e8r, e8i, rho = (
            par(PR) for _ in range(19))
        PW = [par(9 * PR).rearrange("p (k r) -> p k r", k=9) for _ in range(2)]
        Braw = [par(PR * H).rearrange("p (r h) -> p r h", r=PR) for _ in range(2)]
        Bbar = [par(PR * H).rearrange("p (r h) -> p r h", r=PR) for _ in range(2)]
        Ct = [par(PR * H).rearrange("p (r h) -> p r h", r=PR) for _ in range(2)]
        rot = [par(33 * PR).rearrange("p (c r) -> p c r", c=33) for _ in range(2)]
        dT = par(G)
        negtri = par(128)
        negones = par(128)
        prm = par(128)
        prm2 = par(128)
        prm3 = par(128)
        ls2 = par(2)
        dS = par(H)
        Craw = [Em[:, 512 * i:512 * i + 512].rearrange("p (b n) -> p b n", b=4) for i in range(2)]
        Kv = ring[0:H, 0:4096].rearrange("p (g n) -> p g n", g=G)
        Kdiag = par(G * H)[0:H, :].rearrange("p (g h) -> p g h", g=G)
        scan_t = [Em[:, 512 * i:512 * i + 512] for i in range(8)]
        rtmp = [uev[:, 256 * i:256 * i + 256] for i in range(4)]
        Vs = reg_d[:, 0:1024]
        ygel = reg_d[:, 0:1024]

        hnT = reg_a[:, :].rearrange("p (k t) -> p k t", k=KT)
        hnC = reg_d[:, 0:2048].rearrange("p (k t) -> p k t", k=KT)
        mixT = hnT
        mixV = reg_a[:, 0:1024].rearrange("p (m a q c) -> p a q m c", m=4, a=2, q=4)
        hT = hnT
        xs = reg_b[:, :].rearrange("p (a d) -> p a d", a=2)
        qk = reg_b[:, :].rearrange("p (a n) -> p a n", a=2)
        hs = reg_b[:, :].rearrange("p (a k m) -> p a k m", a=2, k=KT)
        v = reg_c[:, 0:1024].rearrange("p (a n) -> p a n", a=2)
        qT = reg_c[:, 1024:2048].rearrange("p (m t) -> p m t", m=4)
        kT = reg_c[:, 2048:3072].rearrange("p (m t) -> p m t", m=4)
        parts = [reg_c[:, 1024 * i:1024 * i + 1024].bitcast(BF16).rearrange("p (a k m) -> p a k m", a=2, k=KT)
                 for i in range(3)]
        sqa = reg_b[:, 0:1024].rearrange("p (m t) -> p m t", m=4)
        sqs = reg_b[:, 1024:2048].rearrange("p (m t) -> p m t", m=4)
        sigt = reg_c[:, 0:1024].rearrange("p (m t) -> p m t", m=4)
        attE = [reg_d[:, 1152 * i:1152 * i + 384] for i in range(2)]
        attL = [reg_d[:, 1152 * i + 384:1152 * i + 768] for i in range(2)]
        attW = [reg_d[:, 1152 * i + 768:1152 * i + 1152] for i in range(2)]
        sqtmp = reg_d[:, 0:2048]
        rest = reg_d[:, 0:2048].rearrange("p (a k m) -> p a k m", a=2, k=KT)
        rx_region = wreg[:, 4096:8192]
        rx = lambda n: piece(rx_region, "rx", n)
        Pm = rx(EB * SLOTS).bitcast(BF16).rearrange("p (a e s) -> p a e s", a=2, e=EB)
        PG = rx(2 * EB * SLOTS).rearrange("p (a e s) -> p a e s", a=2, e=EB)
        PT = rx(256).bitcast(BF16).rearrange("p (n a t) -> p n a t", n=NPAIR, a=2)
        gate_s = rx(NPAIR)
        ident_b = rx(64).bitcast(BF16)
        silu_o = [rx(F) for _ in range(2)]
        act_o = [rx(F) for _ in range(2)]
        actT = [rx(F).rearrange("p (j s) -> p j s", j=2) for _ in range(2)]
        actT_s = [rx(F).rearrange("p (j s) -> p j s", j=2) for _ in range(2)]

        w_in = wreg[:, :].rearrange("p (n k c) -> p n k c", n=4, k=KT)
        w_out = wreg[:, 0:8192].rearrange("p (k n) -> p k n", k=KT)
        w_glu = wreg[:, 8192:10240].rearrange("p (k n) -> p k n", k=4)
        sh13 = wreg[:, 10240:14336].rearrange("p (w k f) -> p w k f", w=2, k=KT)
        sh2 = wreg[:, 14336:16384].rearrange("p (j n) -> p j n", j=2)
        xTg = wreg[:, 0:2048].rearrange("p (k s) -> p k s", k=KT)
        y_parts = [w.bitcast(BF16).rearrange("p (n d) -> p n d", n=NPAIR)
                   for w in (reg_b[:, 0:1024], reg_b[:, 1024:2048], reg_d[:, 0:1024])]
        y_rest = reg_d[:, 1024:2048]
        ringV = ring[:, :].rearrange("p (s w) -> p s w", s=4)
        slot13 = [ringV[:, s, 0:4096].rearrange("p (w k f) -> p w k f", w=2, k=KT) for s in range(4)]
        slot2 = [ringV[:, s, 4096:6144].rearrange("p (j n) -> p j n", j=2) for s in range(4)]
        early13 = {0: wreg[:, 10240:14336]}
        early2 = {0: wreg[:, 2048:4096], 1: reg_a[:, :]}

        def weights13(it, s):
            if s in early13:
                if isinstance(it, int) and it == 1:
                    return early13[s].rearrange("p (w k f) -> p w k f", w=2, k=KT), early13_in[s], 32
                if not isinstance(it, int):
                    return slot13[s], w13_in[s], it * 32
            return slot13[s], w13_in[s], it * 32 + 32

        def weights2(it, s):
            if s in early2:
                if isinstance(it, int) and it == 1:
                    return early2[s].rearrange("p (j n) -> p j n", j=2), early2_in[s], 16
                if not isinstance(it, int):
                    return slot2[s], w2_in[s], it * 16
            return slot2[s], w2_in[s], it * 16 + 16

        rt = lambda n: piece(rt_region, "rt", n)
        rt_region = wreg[:, 8192:10240]
        w_rt = rt(KT * E).rearrange("p (k e) -> p k e", k=KT)
        two = lambda w: w.rearrange("p (a e) -> p a e", a=2)
        scores, biased, sel, repl, mask, gate_r = (two(rt(2 * E)) for _ in range(6))
        m8 = rt(2 * NG * 8).rearrange("p (a g x) -> p a g x", a=2, g=NG)
        gs = two(rt(2 * NG))
        gt_c = rt(2 * NG * NG).rearrange("p (a i j) -> p a i j", a=2, i=NG)
        eq_c = rt(2 * NG * NG).rearrange("p (a i j) -> p a i j", a=2, i=NG)
        rk1, gmask = two(rt(2 * NG)), two(rt(2 * NG))
        top8 = two(rt(16))
        mask_b = rt(E).bitcast(BF16).rearrange("p (a e) -> p a e", a=2)
        tri_b = rt(64).bitcast(BF16)
        ones_b = rt(64).bitcast(BF16)
        bias_bc = rt(E)
        lower = rt(64).rearrange("p (i j) -> p i j", i=NG)

        sm = lambda n: piece(small, "small", n)
        g_mix, g_ffn = sm(KT), sm(KT)
        gq, gk = sm(1), sm(1)
        g_os, g_oa, b_glu = sm(4), sm(4), sm(4)
        ones_col = sm(1)
        ssx, nm, ny, nt, nh = sm(2), sm(32), sm(32), sm(32), sm(32)
        ssqk = sm(32)
        sso = sm(4)
        rso = sm(4)
        rsh = sm(2)
        iota = sm(SLOTS)
        gate = sm(2 * COLS).rearrange("p (a e) -> p a e", a=2)
        pos = reg_d[:, 2048:2048 + 2 * COLS].rearrange("p (a e) -> p a e", a=2)
        n_iter = sm(1).bitcast(I32)
        n_last = sm(1).bitcast(I32)
        n_tail = sm(1).bitcast(I32)
        gsum = sm(2)
        pgT = rx(4 * 128)[0:E].rearrange("p (w a t) -> p w a t", w=2, a=2)
        cnt, more, first, n_full, n_rest = rx(1), rx(1), rx(1), rx(1), rx(1)
        more_b = rx(1).bitcast(BF16)[:, 0:1]
        depth, selx, offs = rx(MAX_EXTRA), rx(MAX_EXTRA), rx(MAX_EXTRA)
        iota_x, e_col, ones_f = rx(MAX_EXTRA), rx(1), rx(128)
        experts = rx(MAX_EXTRA + EB).bitcast(I32)
        pos_b, gate_b = sm(2 * EB), sm(2 * EB)
        pos_b, gate_b = (w.rearrange("p (a e) -> p a e", a=2) for w in (pos_b, gate_b))

        names = """x_in gm_in params_in gains_in b_in c_in wu_in wq_in wk_in wv_in wo_in glu_in sh_in wr_in bias_in
        ident_ready negtri_ready iota_ready trib_ready onesb_ready lower_ready
        ones_ready ssx_ready xs_ready xT_even xT_odd xt_done spread_ready par_t_done par_evac ct_evac
        step_ready a_ready th_ready exps_ready u_done u_evac U_ready qk_done qk_evac qk_normed
        v_done v_evac gq_ready qkT_done qkT_act qkT_dve
        Et_ready Bbar_ready G_ready E_done E_act E_dve K_done K_evac diag_ready T_zero T_dma V_done V_act V_dve VT_done S_ready
        z_done zc_ready e_ready ln_ready sp_ready L_ready zi_done w_ready wm_ready pv_done pv_act
        y5_done y5_gelu  yT_done yT_act yT_dve zg_done sig_ready sqs_ready ys_ready sso_done sso_evac
        opa_done oa_added ops_done h_ready ssh_ready rsh_ready hs_ready hT_done hT_act hT_dve p1_ready rest_ready p2_ready
        parts_ready lg_done scores_ready mask_ready pos_done slots_ready pgT_done pgT_evac selx_ready
        extra_done route_ready P_ready PG_ready slots_copied rx_ready cnt_done first_done dve_chain pool_chain sh_up sh_silu sh_act sh_T sh_actT shd_done acc_added
        gath_done xa xd gt_done gm_act gm_dve identb_ready up_done silu_done act_ready t_done actT_ready down_done
        y1_ready y_rest_ready y2_ready y3_ready
        comb_mm out_done""".split()
        S = {n: sem(n) for n in names}
        w13_in = [sem(f"w13_in{s}") for s in range(4)]
        w2_in = [sem(f"w2_in{s}") for s in range(4)]
        early13_in = {s: sem(f"early13_in{s}") for s in early13}
        early2_in = {s: sem(f"early2_in{s}") for s in early2}

        def chunked(ap):
            return ap.rearrange("p (c q a) -> p a q c", q=4, a=2)

        def sum_bank(c):
            return (6, 7, 2, 3)[c]

        def y_bank(p):
            return 2 - 2 * p

        block = ctx.enter_context(nc.Block())

        @block.sync
        def _(sp):
            xv = I["x"].rearrange("o (c q a) d -> q c (o a d)", q=4, a=2)
            for q in range(4):
                sp.dma_start(acc[32 * q:32 * q + 32, :], xv[q]).then_inc(S["x_in"], 16)
            sp.dma_start(g_mix, I["g_mix"].rearrange("o (p k) -> (o p) k", k=KT)).then_inc(S["gm_in"], 16)
            wi = I["w_in"].rearrange("o (p k) (n c) -> n (o p) k c", k=KT, n=4)
            sp.dma_start(w_in[:, 0], wi[0]).then_inc(S["wu_in"], 16)
            lam = "o (r i) p -> (o r) (i p)"
            sp.dma_start(prm[0:PR, :], I["lam_re"].rearrange(lam, i=2)).then_inc(S["params_in"], 16)
            sp.dma_start(prm2[0:PR, :], I["lam_im"].rearrange(lam, i=2)).then_inc(S["params_in"], 16)
            sp.dma_start(ls2[0:PR, :], I["log_step"].rearrange("o (r i) -> (o r) i", i=2)).then_inc(S["params_in"], 16)
            sp.dma_start(dS[0:G, :], I["d_skip"].rearrange("o (g h) -> (o g) h", h=H)).then_inc(S["params_in"], 16)
            for i, n in enumerate(("c_re", "c_im")):
                cv = I[n].rearrange("o (b g) h p -> (o g h) b p", b=4)
                for half in range(2):
                    sp.dma_start(Craw[i][:, :, 64 * half:64 * half + 64], cv).then_inc(S["c_in"], 16)
            for i, n in enumerate(("b_re", "b_im")):
                bv = I[n].rearrange("o (r i) p h -> (o i p) r h", i=2)
                sp.dma_start(Braw[i], bv).then_inc(S["b_in"], 16)
            for n in (1, 2, 3):
                sp.dma_start(w_in[:, n], wi[n]).then_inc(S[("", "wq_in", "wk_in", "wv_in")[n]], 16)
            for t, n in ((gq, "g_q"), (gk, "g_k")):
                for i in range(2):
                    sp.dma_start(t[64 * i:64 * i + 64, :], I[n].rearrange("o (d i) -> (o d) i", i=1)).then_inc(S["gains_in"], 16)
            with nc.allow_non_contiguous_dma(reason="three vectors of 512 values"):
                for t, n in ((g_os, "g_out_ssm"), (g_oa, "g_out_att"), (b_glu, "b_glu")):
                    sp.dma_start(t, I[n].rearrange("o (k p) -> p (o k)", p=128)).then_inc(S["gains_in"], 16)
            sp.dma_start(g_ffn, I["g_ffn"].rearrange("o (p k) -> (o p) k", k=KT)).then_inc(S["gains_in"], 16)
            sp.wait_ge(S["qk_done"], 2)
            sp.dma_start(w_out, I["w_out"].rearrange("o (k p) n -> p (o k) n", k=KT)).then_inc(S["wo_in"], 16)
            sp.wait_ge(S["qk_done"], 4)
            sp.dma_start(w_glu, I["w_glu"].rearrange("o (k p) n -> p (o k) n", k=4)).then_inc(S["glu_in"], 16)
            sp.wait_ge(S["T_zero"], 1)
            sp.wait_ge(S["diag_ready"], 1)
            for j in range(L):
                sp.dma_start(TmV[16 * j:16 * j + 16, :, 16 * j:128], Kv[:, :, 0:128 - 16 * j]).then_inc(S["T_dma"], 16)
            sp.wait_ge(S["v_done"], 2)
            for w, n in enumerate(("s_w1", "s_w3")):
                sp.dma_start(sh13[:, w], I[n].rearrange("o (p k) f -> (o p) k f", k=KT)).then_inc(S["sh_in"], 16)
            sp.dma_start(sh2, I["s_w2"].rearrange("o (p j) n -> (o p) j n", j=2)).then_inc(S["sh_in"], 16)

            w1v = I["e_w1"].rearrange("o e (p k) f -> (o e) p (k f)", k=KT)
            w3v = I["e_w3"].rearrange("o e (p k) f -> (o e) p (k f)", k=KT)
            w2v = I["e_w2"].rearrange("o e (p j) n -> (o e) p (j n)", j=2)

            def load13(dst, e, done):
                sp.dma_start(dst[:, 0:2048], w1v[bass.ds(e, 1)].rearrange("o p w -> (o p) w")).then_inc(done, 16)
                sp.dma_start(dst[:, 2048:4096], w3v[bass.ds(e, 1)].rearrange("o p w -> (o p) w")).then_inc(done, 16)

            def load2(dst, e, done):
                sp.dma_start(dst, w2v[bass.ds(e, 1)].rearrange("o p w -> (o p) w")).then_inc(done, 16)

            def load_batch(experts_of, before=None, skip13=(), skip2=()):
                pairs = range(len(experts_of) // 2)
                for p in pairs:
                    if before is not None:
                        sp.wait_ge(S["up_done"], before * NPAIR + (p + 1))
                    for s in (2 * p, 2 * p + 1):
                        if s not in skip13:
                            load13(ringV[:, s, 0:4096], experts_of[s], w13_in[s])
                for p in pairs:
                    if before is not None:
                        sp.wait_ge(S["down_done"], before * NPAIR + (p + 1))
                    for s in (2 * p, 2 * p + 1):
                        if s not in skip2:
                            load2(ringV[:, s, 4096:6144], experts_of[s], w2_in[s])

            def further(b, count):
                return [sp.value_load(experts[0:1, bass.ds(b * EB - (E - s), 1)], min_val=0, max_val=E - 1)
                        for s in range(count)]

            sp.wait_ge(S["y5_done"], 2)
            sp.wait_ge(S["zi_done"], NH)
            load_batch(list(range(EB)))
            sp.wait_ge(S["zg_done"], 4)
            sp.dma_start(w_rt, I["w_router"].rearrange("o (p k) e -> (o p) k e", k=KT)).then_inc(S["wr_in"], 16)
            sp.dma_start(bias_bc, I["router_bias"].to_broadcast([128, E])).then_inc(S["bias_in"], 16)
            sp.wait_ge(S["ops_done"], 4)
            load2(early2[0], EB, early2_in[0])
            sp.wait_ge(S["sh_up"], 2)
            load13(early13[0], EB, early13_in[0])
            load2(early2[1], EB + 1, early2_in[1])
            load_batch(list(range(EB, 2 * EB)), 0, early13, early2)
            load13(ringV[:, 0, 0:4096], 2 * EB, w13_in[0])
            for s in early2:
                load2(ringV[:, s, 4096:6144], 2 * EB + s, w2_in[s])
            load_batch(list(range(2 * EB, 3 * EB)), 1, early13, early2)
            with sp.Fori(3, NB) as b:
                load_batch([b * EB + s for s in range(EB)], b - 1)
            sp.wait_ge(S["route_ready"], 1)
            n_it = sp.value_load(n_iter[0:1, :], min_val=NB, max_val=MAX_FULL)
            last_full = sp.value_load(n_last[0:1, :], min_val=NB - 1, max_val=MAX_FULL - 1)
            tail = sp.value_load(n_tail[0:1, :], min_val=0, max_val=1)
            with sp.If(n_it > NB):
                with sp.Fori(NB, n_it) as b:
                    load_batch(further(b, EB), b - 1)
            with sp.If(tail > 0):
                load_batch(further(n_it, 2), last_full)
            sp.wait_ge(S["acc_added"], (n_it + tail) * 4 + 4)
            ov = out.rearrange("o (c q a) d -> q c (o a d)", q=4, a=2)
            for q in range(4):
                sp.dma_start(ov[q], acc[32 * q:32 * q + 32, :]).then_inc(S["out_done"], 16)
            sp.wait_ge(S["out_done"], 64)

        @block.gpsimd
        def _(pool):
            n = [0]

            def step(ins):
                n[0] += 1
                ins.then_inc(S["pool_chain"], 1)
                pool.wait_ge(S["pool_chain"], n[0])

            step(nc.gpsimd.memset(ident[:, :], 0.0))
            nc.gpsimd.affine_select(out=ident[:, :], in_=ident[:, :], compare_op=ALU.not_equal, fill=1.0,
                                    base=0, pattern=[[-1, 128]], channel_multiplier=1).then_inc(S["ident_ready"], 1)
            nc.gpsimd.memset(Tm, 0.0).then_inc(S["T_zero"], 1)
            step(nc.gpsimd.memset(negtri[:, :], -1.0))
            nc.gpsimd.affine_select(out=negtri[:, :], in_=negtri[:, :], compare_op=ALU.is_ge, fill=0.0,
                                    base=0, pattern=[[-1, 128]], channel_multiplier=1).then_inc(S["negtri_ready"], 1)
            nc.gpsimd.iota(iota, pattern=[[1, SLOTS]], base=1, channel_multiplier=0,
                           allow_small_or_imprecise_dtypes=True).then_inc(S["iota_ready"], 1)

            def causal(buf, done):
                d = buf.rearrange("p (b t) -> p b t", b=3)[:, 0::2, :]
                nc.gpsimd.affine_select(out=d, in_=d, compare_op=ALU.is_gt, fill=0.0, base=0,
                                        pattern=[[0, 2], [1, 128]], channel_multiplier=-1).then_inc(S[done], 1)

            for i in range(NH + 1):
                if i < NH:
                    pool.wait_ge(S["sp_ready"], i + 1)
                    causal(attL[i % 2], "L_ready")
                if i >= 1:
                    pool.wait_ge(S["w_ready"], i)
                    causal(attW[(i - 1) % 2], "wm_ready")
            pool.wait_ge(S["zg_done"], 4)
            step(nc.gpsimd.memset(tri_b, 1.0))
            nc.gpsimd.affine_select(out=tri_b, in_=tri_b, compare_op=ALU.is_gt, fill=0.0, base=0,
                                    pattern=[[1, 128]], channel_multiplier=-1).then_inc(S["trib_ready"], 1)
            nc.gpsimd.memset(ones_b, 1.0).then_inc(S["onesb_ready"], 1)
            step(nc.gpsimd.memset(lower, 1.0))
            nc.gpsimd.affine_select(out=lower, in_=lower, compare_op=ALU.is_gt, fill=0.0, base=0,
                                    pattern=[[1, NG], [-1, NG]], channel_multiplier=0).then_inc(S["lower_ready"], 1)
            pool.wait_ge(S["ops_done"], 4)
            nc.gpsimd.iota(iota_x, pattern=[[1, MAX_EXTRA]], base=0, channel_multiplier=0,
                           allow_small_or_imprecise_dtypes=True)
            nc.gpsimd.iota(e_col, pattern=[[0, 1]], base=0, channel_multiplier=1,
                           allow_small_or_imprecise_dtypes=True)
            nc.gpsimd.memset(ones_f, 1.0).then_inc(S["rx_ready"], 1)
            pool.wait_ge(S["p2_ready"], 1)
            pool.wait_ge(S["rest_ready"], 1)
            nc.gpsimd.tensor_tensor(parts[2], rest, parts[1], ALU.subtract).then_inc(S["parts_ready"], 1)

        @block.tensor
        def _(pe):
            def mm(out_, lhsT, rhs, start=True, stop=True, **kw):
                return nc.tensor.matmul(out_, lhsT, rhs, start=start, stop=stop, **kw)

            pe.wait_ge(S["ident_ready"], 1)
            pe.wait_ge(S["xs_ready"], 2)
            xsv = xs.rearrange("p a (m k) -> p a k m", k=KT)
            for k in range(KT):
                for a in range(2):
                    last = nc.tensor.transpose(ps[k][:, 128 * a:128 * a + 128], xsv[:, a, k, :], ident[:, :])
                last.then_inc(S["xt_done"], 1)
            pe.wait_ge(S["params_in"], 16 * 4)
            pe.wait_ge(S["spread_ready"], 1)
            pe.wait_ge(S["xT_odd"], 4)
            for n, t in enumerate((prm, prm2, prm3)):
                nc.tensor.transpose(ps[7][:, 16 * n:16 * n + 16], t[0:PR, :], ident[0:PR, 0:PR])
            nc.tensor.transpose(ps[7][0:16, 64:96], dS[0:G, :], ident[0:G, 0:G]).then_inc(S["par_t_done"], 1)
            pe.wait_ge(S["c_in"], 16 * 4)
            pe.wait_ge(S["xT_even"], 4)
            for i in range(2):
                for b in range(4):
                    last = nc.tensor.transpose(ps[5 + i][:, 128 * b:128 * b + 128], Craw[i][:, b, :], ident[:, :])
                last.then_inc(S["par_t_done"], 1)
            pe.wait_ge(S["wu_in"], 16)
            for a in range(2):
                for k in range(KT):
                    last = mm(ps[a][:, :], hnC[:, k, 128 * a:128 * a + 128], w_in[:, 0, k, :], k == 0, k == KT - 1)
                last.then_inc(S["u_done"], 1)
            pe.wait_ge(S["par_evac"], 1)
            pe.wait_ge(S["ct_evac"], 4)
            for n in (1, 2):
                pe.wait_ge(S[("", "wq_in", "wk_in")[n]], 16)
                for a in range(2):
                    for k in range(KT):
                        last = mm(ps[1 + n + 2 * a][:, :], hnT[:, k, 128 * a:128 * a + 128], w_in[:, n, k, :], k == 0, k == KT - 1)
                    last.then_inc(S["qk_done"], 1)
            pe.wait_ge(S["wv_in"], 16)
            for a in range(2):
                for k in range(KT):
                    last = mm(ps[6 + a][:, :], hnT[:, k, 128 * a:128 * a + 128], w_in[:, 3, k, :], k == 0, k == KT - 1)
                last.then_inc(S["v_done"], 1)
            pe.wait_ge(S["Et_ready"], 1)
            pe.wait_ge(S["u_evac"], 2)
            for n in range(8):
                if n >= 2:
                    pe.wait_ge(S["E_act" if n % 2 == 0 else "E_dve"], n // 2)
                for m in range(4):
                    r, i = (4 * n + m) // 2, m % 2
                    last = nc.tensor.transpose(ps[n % 2][:, 128 * m:128 * m + 128],
                                               Et[i][:, 128 * r:128 * r + 128], ident[:, :])
                last.then_inc(S["E_done"], 1)
            pe.wait_ge(S["Bbar_ready"], 1)
            pe.wait_ge(S["G_ready"], 1)
            pe.wait_ge(S["E_act"], 4)
            pe.wait_ge(S["E_dve"], 4)
            for half in range(2):
                rows = slice(64 * half, 64 * half + 64)
                for n in range(4):
                    for i in range(2):
                        for m in range(4):
                            last = mm(ps[half][32 * m:32 * m + H, 128 * n:128 * n + 128], Bbar[i][rows, 4 * n + m, :],
                                      GmV[i][rows, 4 * n + m, 0:8, :], i == 0, i == 1)
                last.then_inc(S["K_done"], 1)
            pe.wait_ge(S["K_evac"], 8)
            pe.wait_ge(S["U_ready"], 1)
            for b in range(2):
                for i in range(4 * b, 4 * b + 4):
                    o = ps[b].rearrange("p (r i s) -> p r i s", r=2, i=2)[:, (i // 2) % 2, :, 64 * (i % 2):64 * (i % 2) + 64]
                    for q in range(4):
                        last = mm(o[32 * q:32 * q + 32], UV[:, 8 * q + i, :],
                                  EmV[:, 4 * q + i // 2, :, 64 * (i % 2):64 * (i % 2) + 64])
                last.then_inc(S["V_done"], 1)
            pe.wait_ge(S["qk_normed"], 2)
            for n in range(4):
                for m in range(2):
                    for a in range(2):
                        c0 = 512 * (n // 2) + 128 * (2 * (n % 2) + m)
                        last = nc.tensor.transpose(ps[2 + n][:, 256 * m + 128 * a:256 * m + 128 * a + 128],
                                                   qk[:, a, c0:c0 + 128], ident[:, :])
                last.then_inc(S["qkT_done"], 1)

            pe.wait_ge(S["V_act"], 1)
            pe.wait_ge(S["V_dve"], 1)
            for i in range(2):
                for r in range(4):
                    last = nc.tensor.transpose(ps[i][:, 128 * r:128 * r + 128], Vs[:, 256 * r + 128 * i:256 * r + 128 * i + 128], ident[:, :])
                last.then_inc(S["VT_done"], 1)

            def scores_of(h):
                m, rows = h // 2, slice(64 * (h % 2), 64 * (h % 2) + 64)
                z = ps[2 + h % 4]
                if h >= 4:
                    pe.wait_ge(S["w_ready"], h - 3)
                mm(z[:, 0:256], kT[rows, m, 0:128], qT[rows, m, :], True, False, skip_group_check=True)
                mm(z[:, 256:384], kT[rows, m, 128:256], qT[rows, m, 128:256], False, False,
                   skip_group_check=True).then_inc(S["z_done"], 1)

            def add_logs(h):
                z, Lm = ps[2 + h % 4], attL[h % 2]
                pe.wait_ge(S["L_ready"], h + 1)
                mm(z[:, 0:256], negtri[:, :], Lm[:, 0:256], False, False, skip_group_check=True)
                mm(z[:, 128:256], negones[:, :], Lm[:, 256:384], False, False, skip_group_check=True)
                mm(z[:, 256:384], negtri[:, :], Lm[:, 256:384], False, True, skip_group_check=True).then_inc(S["zi_done"], 1)

            def values_of(h):
                m, rows = h // 2, slice(64 * (h % 2), 64 * (h % 2) + 64)
                o = ps[6 + m % 2]
                if h % 2 == 0 and h >= 4:
                    pe.wait_ge(S["pv_act"], m - 1)
                pe.wait_ge(S["wm_ready"], h + 1)
                mm(o[rows, 0:256], v[:, 0, DH * h:DH * h + DH], attW[h % 2][:, 0:256], True, False, skip_group_check=True)
                last = mm(o[rows, 128:256], v[:, 1, DH * h:DH * h + DH], attW[h % 2][:, 256:384], False, True, skip_group_check=True)
                last.then_inc(S["pv_done"], 1)

            Sr, Si = (scan_t[n].rearrange("p (r c) -> p r c", r=PR) for n in (4, 5))
            def s5_output(i):
                if i == 0:
                    pe.wait_ge(S["S_ready"], 1)
                    pe.wait_ge(S["T_dma"], L * 16)
                rows = slice(64 * (i % 2), 64 * (i % 2) + 64)
                tile = lambda q: ps[i % 2][32 * q:32 * q + 32, 128 * (i // 2):128 * (i // 2) + 128]
                for w, st in enumerate((Sr, Si)):
                    for q in range(4):
                        r = 4 * q + i // 2
                        mm(tile(q), st[rows, r, :], GmV[w][rows, r, 1:9, :], w == 0, False)
                for q in range(4):
                    last = mm(tile(q), UV[:, 8 * q + i, :], TmV[:, 8 * q + i, :], False, True)
                if i >= 6:
                    last.then_inc(S["y5_done"], 1)

            pe.wait_ge(S["qkT_act"], 2)
            pe.wait_ge(S["qkT_dve"], 2)
            pe.wait_ge(S["v_evac"], 2)
            pe.wait_ge(S["ones_ready"], 1)
            pe.wait_ge(S["negtri_ready"], 1)
            scores_of(0)
            scores_of(1)
            for h in range(NH + 1):
                if h < NH:
                    add_logs(h)
                    if h + 2 < NH:
                        scores_of(h + 2)
                if h >= 1:
                    values_of(h - 1)
                if 4 <= h < NH:
                    s5_output(2 * h - 8)
                    s5_output(2 * h - 7)
            pe.wait_ge(S["pv_act"], 4)
            for a in range(2):
                for m in range(4):
                    last = mm(ps[7][:, 2 + a:3 + a], sqa[:, m, 128 * a:128 * a + 128], ones_col, m == 0, m == 3)
            last.then_inc(S["sso_done"], 1)
            pe.wait_ge(S["wo_in"], 16)

            def project_attention(a):
                for hf in range(2):
                    for k in range(4):
                        last = mm(ps[2 + 2 * a + hf][:, :], mixT[:, 4 + k, 128 * a:128 * a + 128],
                                  w_out[:, 4 + k, 512 * hf:512 * hf + 512], k == 0, k == 3)
                    last.then_inc(S["opa_done"], 1)

            project_attention(0)
            pe.wait_ge(S["y5_gelu"], 2)
            for a in range(2):
                for q in range(4):
                    j = 2 * q + a
                    last = nc.tensor.transpose(ps[a][:, 128 * q:128 * q + 128], ygel[:, 128 * j:128 * j + 128], ident[:, :])
                last.then_inc(S["yT_done"], 1)
            pe.wait_ge(S["glu_in"], 16)
            pe.wait_ge(S["yT_act"], 1)
            pe.wait_ge(S["yT_dve"], 1)
            for m in range(4):
                for k in range(4):
                    last = mm(ps[m // 2][:, 256 * (m % 2):256 * (m % 2) + 256], w_glu[:, k, 128 * m:128 * m + 128],
                              mixT[:, k, :], k == 0, k == 3)
                last.then_inc(S["zg_done"], 1)
            project_attention(1)
            pe.wait_ge(S["sqs_ready"], 4)
            for a in range(2):
                for m in range(4):
                    last = mm(ps[7][:, a:a + 1], sqs[:, m, 128 * a:128 * a + 128], ones_col, m == 0, m == 3)
            last.then_inc(S["sso_done"], 1)
            pe.wait_ge(S["ys_ready"], 4)
            for a in range(2):
                for hf in range(2):
                    n = (0, 1, 6, 7)[2 * a + hf]
                    if n == 7:
                        pe.wait_ge(S["sso_evac"], 1)
                    for k in range(4):
                        last = mm(ps[n][:, :], mixT[:, k, 128 * a:128 * a + 128],
                                  w_out[:, k, 512 * hf:512 * hf + 512], k == 0, k == 3)
                    last.then_inc(S["ops_done"], 1)
            for a in range(2):
                pe.wait_ge(S["h_ready"], a + 1)
                av = acc[:, D * a:D * a + D].rearrange("p (m k) -> p k m", k=KT)
                for k in range(KT):
                    c0 = 256 * (k % 2) + 128 * a
                    last = nc.tensor.transpose(ps[2 + k // 2][:, c0:c0 + 128], av[:, k, :], ident[:, :])
                    if a == 1 and k % 2 == 1:
                        last.then_inc(S["hT_done"], 1)
            pe.wait_ge(S["hT_act"], 2)
            pe.wait_ge(S["hT_dve"], 2)
            pe.wait_ge(S["wr_in"], 16)
            for a in range(2):
                for k in range(KT):
                    last = mm(ps[7][:, E * a:E * a + E], hT[:, k, 128 * a:128 * a + 128], w_rt[:, k, :], k == 0, k == KT - 1)
            last.then_inc(S["lg_done"], 1)
            pe.wait_ge(S["sh_in"], 48)

            def shared_up(a, ks):
                for k in ks:
                    last = mm(ps[a][:, :], hT[:, k, 128 * a:128 * a + 128], sh13[:, :, k, :], k == 0, k == KT - 1)
                if k == KT - 1:
                    last.then_inc(S["sh_up"], 1)

            shared_up(0, range(KT))
            shared_up(1, range(0, 4))
            pe.wait_ge(S["mask_ready"], 1)
            pe.wait_ge(S["trib_ready"], 1)
            pe.wait_ge(S["onesb_ready"], 1)
            mm(ps[6][:, 0:E], tri_b, mask_b[:, 0, :])
            mm(ps[6][:, E:2 * E], tri_b, mask_b[:, 1, :], True, False)
            mm(ps[6][:, E:2 * E], ones_b, mask_b[:, 0, :], False, True)
            mm(ps[6][0:E, 2 * E:2 * E + 1], mask_b[:, 0, :], ones_b[:, 0:1], True, False)
            mm(ps[6][0:E, 2 * E:2 * E + 1], mask_b[:, 1, :], ones_b[:, 0:1], False, True).then_inc(S["pos_done"], 1)
            shared_up(1, range(4, 6))
            pe.wait_ge(S["cnt_done"], 1)
            mm(ps[6][0:E, 2 * E + 1:2 * E + 2], tri_b[0:E, 0:E], more_b[0:E, :])
            mm(ps[6][:, 2 * E + 2:2 * E + 3], ones_b[0:E, :], more_b[0:E, :]).then_inc(S["first_done"], 1)
            pe.wait_ge(S["slots_ready"], 1)
            for w, t in enumerate((pos, gate)):
                for a in range(2):
                    last = nc.tensor.transpose(ps[7][0:E, 256 * w + 128 * a:256 * w + 128 * a + 128], t[:, a, 0:E], ident[:, :])
            last.then_inc(S["pgT_done"], 1)
            shared_up(1, range(6, KT))
            pe.wait_ge(S["selx_ready"], 1)
            pe.wait_ge(S["pgT_evac"], 1)
            pe.wait_ge(S["rx_ready"], 1)
            X = MAX_EXTRA
            for a in range(2):
                mm(ps[6][:, X * a:X * a + X], pgT[:, 0, a, :], selx[0:E, :], True, False)
                mm(ps[6][:, X * a:X * a + X], ones_f[0:E, :], offs[0:E, :], False, True)
                mm(ps[6][:, X * (2 + a):X * (3 + a)], pgT[:, 1, a, :], selx[0:E, :])
            mm(ps[6][0:1, 4 * X:5 * X], e_col[0:E, :], selx[0:E, :]).then_inc(S["extra_done"], 1)

            def gather_slices(n):
                for k in (2 * n, 2 * n + 1):
                    o = ps[6 + n % 2][:, 256 * (k % 2):256 * (k % 2) + 256]
                    for a in range(2):
                        for w in range(3):
                            last = mm(o, parts[w][:, a, k, :], Pm[:, a], a + w == 0, a + w == 3)
                last.then_inc(S["gath_done"], 1)

            pe.wait_ge(S["P_ready"], 1)
            pe.wait_ge(S["parts_ready"], 1)
            pe.wait_ge(S["route_ready"], 1)
            gather_slices(0)
            gather_slices(1)
            pe.wait_ge(S["xa"], 1)
            gather_slices(2)
            pe.wait_ge(S["xd"], 1)
            gather_slices(3)
            for a in range(2):
                pe.wait_ge(S["sh_act"], a + 1)
                av = act_o[a].rearrange("p (m j) -> p j m", j=2)
                for j in range(2):
                    last = nc.tensor.transpose(ps[2 + a][:, 128 * j:128 * j + 128], av[:, j, :], ident[:, :])
                last.then_inc(S["sh_T"], 1)

            def up(it, p):
                w13, arrived, count = zip(*(weights13(it, 2 * p + i) for i in range(2)))
                for i in range(2):
                    pe.wait_ge(arrived[i], count[i])
                for k in range(KT):
                    for i in range(2):
                        e = 2 * p + i
                        last = mm(ps[p][64 * i:64 * i + 64, :], xTg[:, k, SLOTS * e:SLOTS * e + SLOTS],
                                  w13[i][:, :, k, :], k == 0, k == KT - 1)
                last.then_inc(S["up_done"], 1)

            def turn(it, p):
                pe.wait_ge(S["act_ready"], it * NPAIR + (p + 1))
                av = act_o[p].rearrange("p (m j) -> p j m", j=2)
                for j in range(2):
                    last = nc.tensor.transpose(ps[4 + p][:, 128 * j:128 * j + 128], av[:, j, :], ident[:, :])
                last.then_inc(S["t_done"], 1)

            def down(it, p):
                pe.wait_ge(S["actT_ready"], it * NPAIR + (p + 1))
                w2, arrived, count = zip(*(weights2(it, 2 * p + i) for i in range(2)))
                for i in range(2):
                    pe.wait_ge(arrived[i], count[i])
                for hf in range(2):
                    for j in range(2):
                        for i in range(2):
                            last = mm(ps[y_bank(p) + hf][64 * i:64 * i + 64, :], actT[p][:, j, 64 * i:64 * i + 64],
                                      w2[i][:, j, 512 * hf:512 * hf + 512], j == 0, j == 1)
                last.then_inc(S["down_done"], 1)

            def turn_slots(it, pairs):
                pe.wait_ge(S["PG_ready"], it + 1)
                for n in range(pairs):
                    for a in range(2):
                        mm(ps[5][:, n:n + 1], PG[:, a, 2 * n:2 * n + 2, :], ones_col, a == 0, a == 1)
                for a in range(2):
                    for n in range(pairs):
                        last = mm(ps[4 + a][:, 256 + 128 * n:384 + 128 * n], Pm[:, a, 2 * n:2 * n + 2, :], ident_b)
                    last.then_inc(S["gt_done"], 1)

            def combine(it, pairs):
                for n in range(pairs):
                    pe.wait_ge(S["y2_ready"], it * NPAIR + (n + 1))
                    pe.wait_ge(S["y3_ready"], it * NPAIR + (n + 1))
                    for c in range(4):
                        a, hf = c // 2, c % 2
                        if n == 0 and c < 2:
                            pe.wait_ge(S["xa" if c == 0 else "xd"], it * 2 + (4 if pairs == NPAIR else 2))
                        for w in range(3):
                            last = mm(ps[sum_bank(c)][:, :], PT[:, n, a, :], y_parts[w][:, n, 512 * hf:512 * hf + 512],
                                      n + w == 0, n == pairs - 1 and w == 2)
                        if n == pairs - 1:
                            last.then_inc(S["comb_mm"], 1)

            def shared_down():
                pe.wait_ge(S["sh_actT"], 2)
                for a in range(2):
                    for hf in range(2):
                        for j in range(2):
                            last = mm(ps[4 * a + hf][:, :], actT_s[a][:, j, :], sh2[:, j, 512 * hf:512 * hf + 512], j == 0, j == 1)
                        last.then_inc(S["shd_done"], 1)

            def batch(it, first=False):
                turn_slots(it, NPAIR)
                pe.wait_ge(S["xa"], it * 2 + 2)
                pe.wait_ge(S["xd"], it * 2 + 2)
                up(it, 0)
                up(it, 1)
                pe.wait_ge(S["gm_act"], it + 1)
                if not first:
                    pe.wait_ge(S["acc_added"], it * 4)
                turn(it, 0)
                pe.wait_ge(S["P_ready"], it + 2)
                gather_slices(0)
                down(it, 0)
                pe.wait_ge(S["gm_dve"], it + 1)
                turn(it, 1)
                gather_slices(1)
                down(it, 1)
                pe.wait_ge(S["xa"], it * 2 + 3)
                gather_slices(2)
                pe.wait_ge(S["xd"], it * 2 + 3)
                gather_slices(3)
                combine(it, NPAIR)

            pe.wait_ge(S["identb_ready"], 1)
            batch(0, first=True)
            batch(1)
            n_it = pe.value_load(n_iter[0:1, :], min_val=NB, max_val=MAX_FULL)
            tail = pe.value_load(n_tail[0:1, :], min_val=0, max_val=1)
            with pe.Fori(2, n_it) as it:
                batch(it)
            with pe.If(tail > 0):
                turn_slots(n_it, 1)
                pe.wait_ge(S["xa"], n_it * 2 + 2)
                pe.wait_ge(S["xd"], n_it * 2 + 2)
                up(n_it, 0)
                pe.wait_ge(S["gm_act"], n_it + 1)
                turn(n_it, 0)
                down(n_it, 0)
                pe.wait_ge(S["gm_dve"], n_it + 1)
            shared_down()
            with pe.If(tail > 0):
                pe.wait_ge(S["acc_added"], n_it * 4)
                combine(n_it, 1)

        @block.scalar
        def _(act):
            def copy(out_, in_, scale=1.0):
                return nc.scalar.activation(out_, in_, ACT.Copy, scale=scale)

            act.wait_ge(S["x_in"], 64)
            for a in range(2):
                nc.scalar.activation(xs[:, a, :], acc[:, D * a:D * a + D], ACT.Square, accum_out=ssx[:, a:a + 1]).then_inc(S["ssx_ready"], 1)
            act.wait_ge(S["gm_in"], 16)
            for k in range(1, KT, 2):
                act.wait_ge(S["xt_done"], k + 1)
                copy(hnC[:, k, :], ps[k][:, 0:256], scale=g_mix[:, k:k + 1])
                copy(chunked(hnT[:, k, :]), ps[k][:, 0:256].rearrange("p (a q c) -> p a q c", a=2, q=4),
                     scale=g_mix[:, k:k + 1]).then_inc(S["xT_odd"], 1)
            for i in range(2):
                act.wait_ge(S["par_t_done"], 2 + i)
                for half in range(2):
                    src = ps[5 + i][64 * half:64 * half + 64, :].rearrange("p (r i h) -> p r i h", r=PR, i=2)[:, :, half, :]
                    copy(Ct[i][64 * half:64 * half + 64, :, :], src).then_inc(S["ct_evac"], 1)
            act.wait_ge(S["par_evac"], 1)
            nc.scalar.activation(ls, ls, ACT.Exp).then_inc(S["step_ready"], 1)
            act.wait_ge(S["a_ready"], 1)
            nc.scalar.activation(mag, mag, ACT.Exp)
            nc.scalar.activation(rho, rho, ACT.Exp)
            act.wait_ge(S["th_ready"], 1)
            nc.scalar.activation(sinv, th, ACT.Sin)
            nc.scalar.activation(cosv, th, ACT.Sin, scale=0.5).then_inc(S["exps_ready"], 1)
            uvv = uev.rearrange("p (g a h) -> p a g h", g=G, a=2)
            for a in range(2):
                act.wait_ge(S["u_done"], a + 1)
                copy(uvv[:, a], ps[a][:, :].rearrange("p (g h) -> p g h", g=G)).then_inc(S["u_evac"], 1)
            for n in (0, 1):
                for a in range(2):
                    bank = ps[2 + n + 2 * a]
                    act.wait_ge(S["qk_done"], 2 * n + a + 1)
                    nc.scalar.activation(sqtmp[:, 1024 * a + 512 * n:1024 * a + 512 * n + 512], bank[:, :], ACT.Square)
                    copy(qk[:, a, 512 * n:512 * n + 512], bank[:, :]).then_inc(S["qk_evac"], 1)
            for a in range(2):
                act.wait_ge(S["v_done"], a + 1)
                copy(v[:, a, :], ps[6 + a][:, :]).then_inc(S["v_evac"], 1)
            for n in range(0, 8, 2):
                act.wait_ge(S["E_done"], n + 1)
                copy(Em[:, 512 * n:512 * n + 512], ps[0][:, :]).then_inc(S["E_act"], 1)
            act.wait_ge(S["E_done"], 8)
            for half in range(2):
                act.wait_ge(S["K_done"], half + 1)
                for m in range(4):
                    copy(Kv[:, 2 * m + half:G:8, :],
                         ps[half][32 * m:32 * m + H, :].rearrange("p (n x) -> p n x", n=4)).then_inc(S["K_evac"], 1)
            act.wait_ge(S["V_done"], 1)
            act.wait_ge(S["qk_normed"], 2)
            copy(Vs[:, 0:512], ps[0][:, :]).then_inc(S["V_act"], 1)
            act.wait_ge(S["gq_ready"], 1)
            for n in (0, 1):
                act.wait_ge(S["qkT_done"], n + 1)
                copy(qT[:, 2 * n:2 * n + 2, :], ps[2 + n][:, :].rearrange("p (m t) -> p m t", m=2), scale=gq).then_inc(S["qkT_act"], 1)

            def exp_log(h):
                act.wait_ge(S["zc_ready"], h + 1)
                nc.scalar.activation(attE[h % 2], attE[h % 2], ACT.Exp).then_inc(S["e_ready"], 1)
                act.wait_ge(S["e_ready"], h + 1)
                nc.scalar.activation(attE[h % 2], attE[h % 2], ACT.Ln, bias=ones_col).then_inc(S["ln_ready"], 1)

            def weights(h):
                act.wait_ge(S["zi_done"], h + 1)
                if h >= 2:
                    act.wait_ge(S["pv_done"], h - 1)
                nc.scalar.activation(attW[h % 2], ps[2 + h % 4][:, 0:384], ACT.Exp).then_inc(S["w_ready"], 1)

            def evac_pv(m):
                act.wait_ge(S["pv_done"], 2 * m + 2)
                src = ps[6 + m % 2][:, 0:256].rearrange("p (c q a) -> p a q c", q=4, a=2)
                nc.scalar.activation(sqa[:, m, :].rearrange("p (a q c) -> p a q c", a=2, q=4), src, ACT.Square)
                copy(mixT[:, 4 + m, :].rearrange("p (a q c) -> p a q c", a=2, q=4), src, scale=g_oa[:, m:m + 1]).then_inc(S["pv_act"], 1)

            nc.scalar.preload_act_table_set("natural_log_exp_and_others")
            exp_log(0)
            for h in range(NH):
                if h + 1 < NH:
                    exp_log(h + 1)
                weights(h)
                if h >= 3 and h % 2 == 1:
                    evac_pv((h - 3) // 2)
            evac_pv(3)
            for i in range(2):
                act.wait_ge(S["y5_done"], i + 1)
                nc.scalar.activation(ygel.rearrange("p (j i b h) -> p b i j h", j=L, i=4, b=2)[:, i],
                                     ps[i][:, :].rearrange("p (i j h) -> p i j h", i=4, j=L), ACT.Gelu_apprx_tanh).then_inc(S["y5_gelu"], 1)
            act.wait_ge(S["yT_done"], 1)
            copy(mixV[:, 0], ps[0][:, :].rearrange("p (q m c) -> p q m c", q=4, m=4)).then_inc(S["yT_act"], 1)
            for m in range(4):
                act.wait_ge(S["zg_done"], 2 * (m // 2) + 2)
                nc.scalar.activation(sigt[:, m, :], ps[m // 2][:, 256 * (m % 2):256 * (m % 2) + 256], ACT.Sigmoid,
                                     bias=b_glu[:, m:m + 1]).then_inc(S["sig_ready"], 1)
            for a in range(2):
                act.wait_ge(S["h_ready"], 1 + a)
                nc.scalar.activation(sqtmp[:, 1024 * a:1024 * a + 1024], acc[:, D * a:D * a + D], ACT.Square,
                                     accum_out=ssx[:, a:a + 1]).then_inc(S["ssh_ready"], 1)
            for k in (2, 3, 6, 7):
                act.wait_ge(S["hT_done"], k // 2 + 1)
                last = copy(hT[:, k, :], ps[2 + k // 2][:, 256 * (k % 2):256 * (k % 2) + 256], scale=g_ffn[:, k:k + 1])
                if k % 2 == 1:
                    last.then_inc(S["hT_act"], 1)
            act.wait_ge(S["rsh_ready"], 1)
            act.wait_ge(S["lg_done"], 1)
            for a in range(2):
                last = nc.scalar.activation(scores[:, a], ps[7][:, E * a:E * a + E], ACT.Sigmoid, scale=rsh[:, a:a + 1])
            last.then_inc(S["scores_ready"], 1)
            act.wait_ge(S["hs_ready"], 2)
            copy(parts[0], hs).then_inc(S["p1_ready"], 1)
            act.wait_ge(S["rest_ready"], 1)
            copy(parts[1], rest).then_inc(S["p2_ready"], 1)
            def shared_silu(a):
                act.wait_ge(S["sh_up"], a + 1)
                nc.scalar.activation(silu_o[a], ps[a][:, 0:256], ACT.Silu, scale=rsh[:, a:a + 1]).then_inc(S["sh_silu"], 1)

            shared_silu(0)
            act.wait_ge(S["pgT_done"], 1)
            copy(pgT, ps[7][0:E, :].rearrange("p (w a t) -> p w a t", w=2, a=2)).then_inc(S["pgT_evac"], 1)
            shared_silu(1)

            def gathered(g, n):
                act.wait_ge(S["gath_done"], g * 4 + (2 * n + 1))
                for k in (4 * n, 4 * n + 1):
                    last = copy(xTg[:, k, :], ps[6][:, 256 * (k % 2):256 * (k % 2) + 256], scale=g_ffn[:, k:k + 1])
                last.then_inc(S["xa"], 1)

            def silu(it, p):
                act.wait_ge(S["up_done"], it * NPAIR + (p + 1))
                nc.scalar.activation(silu_o[p], ps[p][:, 0:256], ACT.Silu).then_inc(S["silu_done"], 1)

            def turned(it, p):
                act.wait_ge(S["t_done"], it * NPAIR + (p + 1))
                copy(actT[p], ps[4 + p][:, 0:256].rearrange("p (j s) -> p j s", j=2)).then_inc(S["actT_ready"], 1)

            def y_first(it, p):
                act.wait_ge(S["down_done"], it * NPAIR + (p + 1))
                for hf in range(2):
                    copy(y_parts[0][:, p, 512 * hf:512 * hf + 512], ps[y_bank(p) + hf][:, :]).then_inc(S["y1_ready"], 1)

            def y_second(it, p):
                act.wait_ge(S["y_rest_ready"], it * (2 * NPAIR) + (2 * p + 2))
                copy(y_parts[1][:, p, :], y_rest).then_inc(S["y2_ready"], 1)

            gathered(0, 0)
            gathered(0, 1)
            for a in range(2):
                act.wait_ge(S["sh_T"], a + 1)
                copy(actT_s[a], ps[2 + a][:, 0:256].rearrange("p (j s) -> p j s", j=2)).then_inc(S["sh_actT"], 1)
            act.wait_ge(S["route_ready"], 1)
            def slots_out(it, pairs):
                act.wait_ge(S["gt_done"], it * 2 + 1)
                copy(PT[:, 0:pairs, 0, :], ps[4][:, 256:256 + 128 * pairs].rearrange("p (n t) -> p n t", n=pairs)).then_inc(S["gm_act"], 1)

            def batch(it):
                slots_out(it, NPAIR)
                silu(it, 0)
                silu(it, 1)
                turned(it, 0)
                gathered(it + 1, 0)
                turned(it, 1)
                y_first(it, 0)
                y_second(it, 0)
                y_first(it, 1)
                gathered(it + 1, 1)
                y_second(it, 1)

            n_it = act.value_load(n_iter[0:1, :], min_val=NB, max_val=MAX_FULL)
            tail = act.value_load(n_tail[0:1, :], min_val=0, max_val=1)
            batch(0)
            batch(1)
            with act.Fori(2, n_it) as it:
                batch(it)
            with act.If(tail > 0):
                slots_out(n_it, 1)
                silu(n_it, 0)
                turned(n_it, 0)
                y_first(n_it, 0)
                y_second(n_it, 0)

        @block.vector
        def _(dve):
            n = [0]

            def step(ins):
                n[0] += 1
                ins.then_inc(S["dve_chain"], 1)
                dve.wait_ge(S["dve_chain"], n[0])

            def tt(out_, a, b, op):
                return nc.vector.tensor_tensor(out_, a, b, op)

            def ts(out_, a, s1, op0, s2=None, op1=ALU.bypass):
                return nc.vector.tensor_scalar(out_, a, s1, s2, op0, op1)

            def stt(out_, a, s1, b, op0, op1):
                return nc.vector.scalar_tensor_tensor(out=out_, in0=a, scalar=s1, in1=b, op0=op0, op1=op1)

            def rsqrt_of_mean(ss, w, count):
                m, y, t = nm[:, 0:w], ny[:, 0:w], nt[:, 0:w]
                step(ts(m, ss, 1.0 / count, ALU.mult, EPS, ALU.add))
                ts(nh[:, 0:w], m, -0.5, ALU.mult)
                step(ts(y.bitcast(I32), m.bitcast(I32), -0.5, ALU.mult, RSQRT_MAGIC, ALU.add))
                for _ in range(3):
                    step(tt(t, y, y, ALU.mult))
                    step(tt(t, t, nh[:, 0:w], ALU.mult))
                    step(stt(y, t, 1.5, y, ALU.add, ALU.mult))
                return y

            def cmul(outs, x, y, tmps, done=step):
                ta, tb, tc, td = tmps
                tt(ta, x[0], y[0], ALU.mult)
                tt(tb, x[1], y[1], ALU.mult)
                tt(tc, x[0], y[1], ALU.mult)
                step(tt(td, x[1], y[0], ALU.mult))
                tt(outs[0], ta, tb, ALU.subtract)
                done(tt(outs[1], tc, td, ALU.add))

            nc.vector.memset(negones[:, :], -1.0)
            nc.vector.memset(ones_col, 1.0).then_inc(S["ones_ready"], 1)
            dve.wait_ge(S["ssx_ready"], 2)
            y = rsqrt_of_mean(ssx, 2, D)
            for a in range(2):
                ts(xs[:, a, :], acc[:, D * a:D * a + D], y[:, a:a + 1], ALU.mult).then_inc(S["xs_ready"], 1)
            dve.wait_ge(S["params_in"], 16 * 4)
            nc.vector.tensor_copy(prm3[0:PR, :].rearrange("p (i s) -> p i s", i=2),
                                  ls2[0:PR, :].unsqueeze(2).to_broadcast([PR, 2, P])).then_inc(S["spread_ready"], 1)
            dve.wait_ge(S["gm_in"], 16)
            for k in range(0, KT, 2):
                dve.wait_ge(S["xt_done"], k + 1)
                ts(hnC[:, k, :], ps[k][:, 0:256], g_mix[:, k:k + 1], ALU.mult)
                ts(chunked(hnT[:, k, :]), ps[k][:, 0:256].rearrange("p (a q c) -> p a q c", a=2, q=4),
                   g_mix[:, k:k + 1], ALU.mult).then_inc(S["xT_even"], 1)
            dve.wait_ge(S["par_t_done"], 1)
            ts(lr, ps[7][:, 0:16], -1e-4, ALU.min)
            nc.vector.tensor_copy(li, ps[7][:, 16:32])
            nc.vector.tensor_copy(ls, ps[7][:, 32:48])
            nc.vector.tensor_copy(dT[0:H, :], ps[7][0:H, 64:96]).then_inc(S["par_evac"], 1)
            dve.wait_ge(S["par_evac"], 1)
            dve.wait_ge(S["step_ready"], 1)
            step(tt(mag, lr, ls, ALU.mult))
            ts(rho, mag, float(L), ALU.mult).then_inc(S["a_ready"], 1)
            step(tt(th, li, ls, ALU.mult))
            step(ts(t1, th, 1.0 / TWO_PI, ALU.mult, ROUND_MAGIC, ALU.add))
            step(ts(t1, t1, ROUND_MAGIC, ALU.subtract))
            for part in two_pi_parts():
                step(stt(th, t1, -part, th, ALU.mult, ALU.add))
            ts(th, th, PI_DOWN, ALU.min, -PI_DOWN, ALU.max).then_inc(S["th_ready"], 1)
            dve.wait_ge(S["exps_ready"], 1)
            step(tt(cosv, cosv, cosv, ALU.mult))
            step(ts(cosv, cosv, -2.0, ALU.mult, 1.0, ALU.add))
            tt(lbr, mag, cosv, ALU.mult)
            step(tt(lbi, mag, sinv, ALU.mult))
            ts(t1, lbr, -1.0, ALU.add)
            tt(t2, lr, lr, ALU.mult)
            step(tt(t3, li, li, ALU.mult))
            step(tt(t2, t2, t3, ALU.add))
            step(nc.vector.reciprocal(den, t2))
            tt(t2, t1, lr, ALU.mult)
            step(tt(t3, lbi, li, ALU.mult))
            step(tt(t2, t2, t3, ALU.add))
            tt(cor, t2, den, ALU.mult)
            tt(t3, lbi, lr, ALU.mult)
            step(tt(t4, t1, li, ALU.mult))
            step(tt(t3, t3, t4, ALU.subtract))
            step(tt(coi, t3, den, ALU.mult))

            def over_h(w):
                return w.unsqueeze(2).to_broadcast([128, PR, H])

            big = [scan_t[i] for i in range(8)]
            dve.wait_ge(S["b_in"], 32)
            dve.wait_ge(S["par_t_done"], 3)
            tv = [big[i][:, 0:PR * H].rearrange("p (r h) -> p r h", r=PR) for i in range(4)]
            cmul(Bbar, Braw, [over_h(cor), over_h(coi)], tv, lambda ins: ins.then_inc(S["Bbar_ready"], 1))
            dve.wait_ge(S["Bbar_ready"], 1)
            nc.vector.memset(PW[0][:, 0, :], 1.0)
            nc.vector.memset(PW[1][:, 0, :], 0.0)
            nc.vector.tensor_copy(PW[0][:, 1, :], lbr)
            step(nc.vector.tensor_copy(PW[1][:, 1, :], lbi))
            for have in (1, 2, 4):
                by = [PW[i][:, have:have + 1, :].to_broadcast([128, have, PR]) for i in range(2)]
                tw = [big[i][:, 0:have * PR].rearrange("p (k r) -> p k r", k=have) for i in range(4)]
                cmul([PW[i][:, have + 1:2 * have + 1, :] for i in range(2)],
                     [PW[i][:, 1:have + 1, :] for i in range(2)], by, tw)

            def products(outs, mats, ks, sign, turn):
                for j, k in enumerate(ks):
                    w = [over_h(PW[i][:, k, :]) for i in range(2)]
                    tmps = [big[4 * ((j + turn) % 2) + i][:, 0:256].rearrange("p (r h) -> p r h", r=PR) for i in range(4)]
                    ta, tb, tc, td = tmps
                    tt(ta, mats[0], w[0], ALU.mult)
                    tt(tb, mats[1], w[1], ALU.mult)
                    tt(tc, mats[0], w[1], ALU.mult)
                    step(tt(td, mats[1], w[0], ALU.mult))
                    last = tt(outs[0][:, :, j, :], ta, tb, ALU.subtract)
                    if sign > 0:
                        last = tt(outs[1][:, :, j, :], tc, td, ALU.add)
                    else:
                        last = stt(outs[1][:, :, j, :], tc, -1.0, td, ALU.mult, ALU.subtract)
                return last

            dve.wait_ge(S["ct_evac"], 4)
            products(GmV, Ct, list(range(L + 1)), -1, 0).then_inc(S["G_ready"], 1)
            products(EtV, Bbar, [L - 1 - j for j in range(L)], 1, 1).then_inc(S["Et_ready"], 1)
            dve.wait_ge(S["u_evac"], 2)
            nc.vector.transpose(U, uev).then_inc(S["U_ready"], 1)
            dve.wait_ge(S["qk_evac"], 4)
            for a in range(2):
                last = nc.vector.tensor_reduce(ssqk[:, 16 * a:16 * a + 16], sqtmp[:, 1024 * a:1024 * a + 1024].rearrange("p (h d) -> p h d", d=DH),
                                        AX.X, ALU.add)
            step(last)
            y = rsqrt_of_mean(ssqk, 32, DH)
            for a in range(2):
                q3 = qk[:, a, :].rearrange("p (h d) -> p h d", d=DH)
                tt(q3, q3, y[:, 16 * a:16 * a + 16].unsqueeze(2).to_broadcast([128, 16, DH]), ALU.mult).then_inc(S["qk_normed"], 1)
            dve.wait_ge(S["gains_in"], 16 * 8)
            ts(gq, gq, float(DH) ** -0.5, ALU.mult).then_inc(S["gq_ready"], 1)
            for n_ in range(1, 8, 2):
                dve.wait_ge(S["E_done"], n_ + 1)
                nc.vector.tensor_copy(Em[:, 512 * n_:512 * n_ + 512], ps[1][:, :]).then_inc(S["E_dve"], 1)
            dve.wait_ge(S["U_ready"], 1)
            cur, nxt = [cosv, sinv], [t1, t2]
            tq = [t3, t4, e8r, e8i]
            for _ in range(3):
                cmul(nxt, cur, cur, tq)
                cur, nxt = nxt, cur
            nc.vector.memset(rot[0][:, 0, :], 1.0)
            nc.vector.memset(rot[1][:, 0, :], 0.0)
            nc.vector.tensor_copy(rot[0][:, 1, :], cur[0])
            step(nc.vector.tensor_copy(rot[1][:, 1, :], cur[1]))
            for have in (1, 2, 4, 8, 16):
                by = [rot[i][:, have:have + 1, :].to_broadcast([128, have, PR]) for i in range(2)]
                tw = [rtmp[i][:, 0:have * PR].rearrange("p (k r) -> p k r", k=have) for i in range(4)]
                cmul([rot[i][:, have + 1:2 * have + 1, :] for i in range(2)],
                     [rot[i][:, 1:have + 1, :] for i in range(2)], by, tw)
            dve.wait_ge(S["ident_ready"], 1)
            step(tt(Kdiag, ident[0:H, 0:H].unsqueeze(1).to_broadcast([H, G, H]),
                    dT[0:H, :].unsqueeze(2).to_broadcast([H, G, H]), ALU.mult))
            dve.wait_ge(S["K_evac"], 8)
            tt(Kv[:, :, 0:H], Kv[:, :, 0:H], Kdiag, ALU.add).then_inc(S["diag_ready"], 1)
            dve.wait_ge(S["V_done"], 2)
            nc.vector.tensor_copy(Vs[:, 512:1024], ps[1][:, :]).then_inc(S["V_dve"], 1)
            s3 = [w.rearrange("p (r c) -> p r c", r=PR) for w in scan_t]
            s4 = [w.rearrange("p (q r c) -> p q r c", q=4, r=4) for w in scan_t]
            V4 = [ps[i][:, :].rearrange("p (r q c) -> p q r c", r=4, q=4) for i in range(2)]
            R1 = [w[:, 1:33, :].rearrange("p c r -> p r c") for w in rot]
            R4 = [w[:, 1:33, :].rearrange("p c (q r) -> p q r c", q=4) for w in rot]
            def scan_turn():
                dve.wait_ge(S["VT_done"], 2)
                tt(s4[0], V4[0], R4[0], ALU.mult)
                tt(s4[1], V4[1], R4[1], ALU.mult)
                tt(s4[2], V4[1], R4[0], ALU.mult)
                tt(s4[3], V4[0], R4[1], ALU.mult)
                step(nc.vector.tensor_copy(s3[6], rho.unsqueeze(2).to_broadcast([128, PR, C])))
                nc.vector.memset(s3[6][:, :, 0:1], 0.0)
                tt(s3[0], s3[0], s3[1], ALU.add)
                step(tt(s3[2], s3[2], s3[3], ALU.subtract))

            def scan_run():
                nc.vector.tensor_tensor_scan(scan_t[1], scan_t[6], scan_t[0], 0.0, ALU.mult, ALU.add)
                step(nc.vector.tensor_tensor_scan(scan_t[3], scan_t[6], scan_t[2], 0.0, ALU.mult, ALU.add))

            def scan_back():
                w = C - 1
                Rw = [x[:, :, 0:w] for x in R1]
                g_r, g_i = s3[1][:, :, 0:w], s3[3][:, :, 0:w]
                tt(s3[0][:, :, 0:w], g_r, Rw[0], ALU.mult)
                tt(s3[2][:, :, 0:w], g_i, Rw[1], ALU.mult)
                tt(s3[6][:, :, 0:w], g_r, Rw[1], ALU.mult)
                step(tt(s3[7][:, :, 0:w], g_i, Rw[0], ALU.mult))
                nc.vector.memset(s3[4][:, :, 0:1], 0.0)
                nc.vector.memset(s3[5][:, :, 0:1], 0.0)
                tt(s3[4][:, :, 1:C], s3[0][:, :, 0:w], s3[2][:, :, 0:w], ALU.subtract)
                tt(s3[5][:, :, 1:C], s3[6][:, :, 0:w], s3[7][:, :, 0:w], ALU.add).then_inc(S["S_ready"], 1)

            for n_ in (2, 3):
                dve.wait_ge(S["qkT_done"], n_ + 1)
                ts(kT[:, 2 * n_ - 4:2 * n_ - 2, :], ps[2 + n_][:, :].rearrange("p (m t) -> p m t", m=2), gk, ALU.mult).then_inc(S["qkT_dve"], 1)

            def clamp(h):
                dve.wait_ge(S["z_done"], h + 1)
                if h >= 2:
                    dve.wait_ge(S["sp_ready"], h - 1)
                ts(attE[h % 2], ps[2 + h % 4][:, 0:384], 80.0, ALU.min).then_inc(S["zc_ready"], 1)

            def softplus(h):
                dve.wait_ge(S["ln_ready"], h + 1)
                if h >= 2:
                    dve.wait_ge(S["zi_done"], h - 1)
                tt(attL[h % 2], attE[h % 2], ps[2 + h % 4][:, 0:384], ALU.max).then_inc(S["sp_ready"], 1)

            clamp(0)
            for h in range(NH):
                if h + 1 < NH:
                    clamp(h + 1)
                softplus(h)
                if h < 3:
                    (scan_turn, scan_run, scan_back)[h]()
            dve.wait_ge(S["sso_done"], 1)
            step(nc.vector.tensor_copy(sso[:, 2:4], ps[7][:, 2:4]))
            y = rsqrt_of_mean(sso[:, 2:4], 2, DS)
            step(nc.vector.tensor_copy(rso[:, 2:4], y))
            def add_projection(a, hf, bank, col):
                part = acc[:, D * a + 512 * hf:D * a + 512 * hf + 512]
                return stt(part, bank[:, :], rso[:, col + a:col + a + 1], part, ALU.mult, ALU.add)

            def add_attention(a):
                for hf in range(2):
                    dve.wait_ge(S["opa_done"], 2 * a + hf + 1)
                    last = add_projection(a, hf, ps[2 + 2 * a + hf], 2)
                last.then_inc(S["oa_added"], 1)

            add_attention(0)
            dve.wait_ge(S["yT_done"], 2)
            nc.vector.tensor_copy(mixV[:, 1], ps[1][:, :].rearrange("p (q m c) -> p q m c", q=4, m=4)).then_inc(S["yT_dve"], 1)
            dve.wait_ge(S["zg_done"], 4)
            for m in range(4):
                dve.wait_ge(S["sig_ready"], m + 1)
                last = tt(mixT[:, m, :], mixT[:, m, :], sigt[:, m, :], ALU.mult)
            step(last)
            for m in range(4):
                tt(sqs[:, m, :], mixT[:, m, :], mixT[:, m, :], ALU.mult).then_inc(S["sqs_ready"], 1)
            for m in range(4):
                ts(mixT[:, m, :], mixT[:, m, :], g_os[:, m:m + 1], ALU.mult).then_inc(S["ys_ready"], 1)
            add_attention(1)
            dve.wait_ge(S["sso_done"], 2)
            nc.vector.tensor_copy(sso[:, 0:2], ps[7][:, 0:2]).then_inc(S["sso_evac"], 1)
            dve.wait_ge(S["sso_evac"], 1)
            y = rsqrt_of_mean(sso[:, 0:2], 2, DS)
            step(nc.vector.tensor_copy(rso[:, 0:2], y))
            for a in range(2):
                dve.wait_ge(S["oa_added"], a + 1)
                for hf in range(2):
                    dve.wait_ge(S["ops_done"], 2 * a + hf + 1)
                    last = add_projection(a, hf, ps[(0, 1, 6, 7)[2 * a + hf]], 0)
                last.then_inc(S["h_ready"], 1)
            for k in (0, 1, 4, 5):
                dve.wait_ge(S["hT_done"], k // 2 + 1)
                last = ts(hT[:, k, :], ps[2 + k // 2][:, 256 * (k % 2):256 * (k % 2) + 256], g_ffn[:, k:k + 1], ALU.mult)
                if k % 2 == 1:
                    last.then_inc(S["hT_dve"], 1)
            dve.wait_ge(S["ssh_ready"], 2)
            y = rsqrt_of_mean(ssx, 2, D)
            nc.vector.tensor_copy(rsh, y).then_inc(S["rsh_ready"], 1)
            for a in range(2):
                ts(hs[:, a], acc[:, D * a:D * a + D].rearrange("p (m k) -> p k m", k=KT), y[:, a:a + 1], ALU.mult).then_inc(S["hs_ready"], 1)

            dve.wait_ge(S["scores_ready"], 1)
            dve.wait_ge(S["bias_in"], 16)
            step(tt(biased, scores, bias_bc.unsqueeze(1).to_broadcast([128, 2, E]), ALU.add))
            for a in range(2):
                for g in range(NG):
                    last = nc.vector.max(m8[:, a, g, :], biased[:, a, GE * g:GE * g + GE])
            step(last)
            step(tt(gs, m8[:, :, :, 0], m8[:, :, :, 1], ALU.add))
            gi = gs.unsqueeze(3).to_broadcast([128, 2, NG, NG])
            gj = gs.unsqueeze(2).to_broadcast([128, 2, NG, NG])
            tt(gt_c, gj, gi, ALU.is_gt)
            step(tt(eq_c, gj, gi, ALU.is_equal))
            dve.wait_ge(S["lower_ready"], 1)
            step(tt(eq_c, eq_c, lower.unsqueeze(1).to_broadcast([128, 2, NG, NG]), ALU.mult))
            step(tt(gt_c, gt_c, eq_c, ALU.add))
            step(nc.vector.tensor_reduce(rk1, gt_c, AX.X, ALU.add))
            step(ts(gmask, rk1, float(TOPG), ALU.is_lt))
            dve.wait_ge(S["p1_ready"], 1)
            tt(rest, hs, parts[0], ALU.subtract).then_inc(S["rest_ready"], 1)
            step(ts(rk1, gmask, -1.0, ALU.add, BIG, ALU.mult))
            b4 = biased.rearrange("p a (g x) -> p a g x", g=NG)
            s4 = sel.rearrange("p a (g x) -> p a g x", g=NG)
            step(tt(s4, b4, gmask.unsqueeze(3).to_broadcast([128, 2, NG, GE]), ALU.mult))
            step(tt(s4, s4, rk1.unsqueeze(3).to_broadcast([128, 2, NG, GE]), ALU.add))
            for a in range(2):
                step(nc.vector.max(top8[:, a, :], sel[:, a, :]))
                step(nc.vector.match_replace(out=repl[:, a, :], in_to_replace=top8[:, a, :], in_values=sel[:, a, :], imm_value=BIG))
            step(tt(mask, repl, sel, ALU.not_equal))
            nc.vector.tensor_copy(mask_b, mask).then_inc(S["mask_ready"], 1)
            step(tt(gate_r, scores, mask, ALU.mult))
            step(nc.vector.tensor_reduce(gsum, gate_r, AX.X, ALU.add))
            step(nc.vector.reciprocal(gsum, gsum))
            for a in range(2):
                ts(gate[:, a, 0:E], gate_r[:, a, :], gsum[:, a:a + 1], ALU.mult, ROUTED_SCALE, ALU.mult)
            for t in (pos, gate):
                nc.vector.memset(t[:, :, E + MAX_EXTRA:COLS], 0.0)
            dve.wait_ge(S["pos_done"], 1)
            tt_pos = stt(pos[:, :, 0:E], ps[6][:, 0:2 * E].rearrange("p (a e) -> p a e", a=2), 1.0, mask, ALU.add, ALU.mult)
            tt_pos.then_inc(S["slots_ready"], 1)
            dve.wait_ge(S["rx_ready"], 1)
            step(nc.vector.tensor_copy(cnt[0:E, :], ps[6][0:E, 2 * E:2 * E + 1]))
            step(ts(more[0:E, :], cnt[0:E, :], float(SLOTS), ALU.is_gt))
            for most in range(2 * SLOTS, T, SLOTS):
                step(stt(more[0:E, :], cnt[0:E, :], float(most), more[0:E, :], ALU.is_gt, ALU.add))
            nc.vector.tensor_copy(more_b[0:E, :], more[0:E, :]).then_inc(S["cnt_done"], 1)
            def place(g):
                nc.vector.tensor_copy(gate_b, gate[:, :, bass.ds(g * EB, EB)])
                nc.vector.tensor_copy(pos_b, pos[:, :, bass.ds(g * EB, EB)]).then_inc(S["slots_copied"], 1)
                dve.wait_ge(S["slots_copied"], g + 1)
                for a in range(2):
                    last = tt(Pm[:, a], iota.unsqueeze(1).to_broadcast([128, EB, SLOTS]),
                              pos_b[:, a].unsqueeze(2).to_broadcast([128, EB, SLOTS]), ALU.is_equal)
                last.then_inc(S["P_ready"], 1)

            def place_gates(g):
                dve.wait_ge(S["P_ready"], g + 1)
                for a in range(2):
                    last = tt(PG[:, a], Pm[:, a], gate_b[:, a].unsqueeze(2).to_broadcast([128, EB, SLOTS]), ALU.mult)
                last.then_inc(S["PG_ready"], 1)

            nc.vector.tensor_copy(ident_b, ident[:, :]).then_inc(S["identb_ready"], 1)
            dve.wait_ge(S["iota_ready"], 1)
            place(0)
            dve.wait_ge(S["first_done"], 1)
            nc.vector.tensor_copy(first[0:E, :], ps[6][0:E, 2 * E + 1:2 * E + 2])
            ts(n_full, ps[6][:, 2 * E + 2:2 * E + 3], 0.25, ALU.mult, 0.25 - 0.375, ALU.add)
            step(ts(n_rest, ps[6][:, 2 * E + 2:2 * E + 3], 0.5, ALU.mult, 0.5 - 0.25, ALU.add))
            ts(depth[0:E, :], iota_x[0:E, :], first[0:E, :], ALU.subtract)
            for count in (n_full, n_rest):
                step(ts(count, count, ROUND_MAGIC, ALU.add))
                step(ts(count, count, ROUND_MAGIC, ALU.subtract))
            step(stt(n_rest, n_full, -2.0, n_rest, ALU.mult, ALU.add))
            nc.vector.tensor_copy(n_tail, n_rest)
            ts(n_iter, n_full, float(NB), ALU.add)
            ts(n_last, n_full, float(NB - 1), ALU.add)
            step(ts(selx[0:E, :], depth[0:E, :], more[0:E, :], ALU.is_lt))
            step(stt(selx[0:E, :], depth[0:E, :], 0.0, selx[0:E, :], ALU.is_ge, ALU.mult))
            step(ts(depth[0:E, :], depth[0:E, :], -float(SLOTS), ALU.mult, -float(SLOTS), ALU.add))
            tt(offs[0:E, :], depth[0:E, :], selx[0:E, :], ALU.mult).then_inc(S["selx_ready"], 1)
            def gathered(g, n):
                dve.wait_ge(S["gath_done"], g * 4 + (2 * n + 2))
                for k in (4 * n + 2, 4 * n + 3):
                    last = ts(xTg[:, k, :], ps[7][:, 256 * (k % 2):256 * (k % 2) + 256], g_ffn[:, k:k + 1], ALU.mult)
                last.then_inc(S["xd"], 1)

            place_gates(0)
            dve.wait_ge(S["extra_done"], 1)
            X = MAX_EXTRA
            nc.vector.tensor_copy(pos[:, :, E:E + X], ps[6][:, 0:2 * X].rearrange("p (a k) -> p a k", a=2))
            nc.vector.tensor_copy(gate[:, :, E:E + X], ps[6][:, 2 * X:4 * X].rearrange("p (a k) -> p a k", a=2))
            nc.vector.tensor_copy(experts[0:1, 0:X], ps[6][0:1, 4 * X:5 * X]).then_inc(S["route_ready"], 1)
            for a in range(2):
                dve.wait_ge(S["sh_silu"], a + 1)
                stt(act_o[a], ps[a][:, 256:512], rsh[:, a:a + 1], silu_o[a], ALU.mult, ALU.mult).then_inc(S["sh_act"], 1)
            gathered(0, 0)
            gathered(0, 1)
            def activate(it, p):
                dve.wait_ge(S["silu_done"], it * NPAIR + (p + 1))
                stt(act_o[p], silu_o[p], gate_s[:, p:p + 1], ps[p][:, 256:512], ALU.mult, ALU.mult).then_inc(S["act_ready"], 1)

            def y_left(it, p):
                if p:
                    dve.wait_ge(S["y3_ready"], it * NPAIR + p)
                for hf in range(2):
                    dve.wait_ge(S["y1_ready"], it * (2 * NPAIR) + (2 * p + hf + 1))
                    tt(y_rest[:, 512 * hf:512 * hf + 512], ps[y_bank(p) + hf][:, :],
                       y_parts[0][:, p, 512 * hf:512 * hf + 512], ALU.subtract).then_inc(S["y_rest_ready"], 1)

            def y_third(it, p):
                dve.wait_ge(S["y2_ready"], it * NPAIR + (p + 1))
                tt(y_parts[2][:, p, :], y_rest, y_parts[1][:, p, :], ALU.subtract).then_inc(S["y3_ready"], 1)

            def slots_out(it, pairs):
                dve.wait_ge(S["gt_done"], it * 2 + 2)
                nc.vector.tensor_copy(gate_s[:, 0:pairs], ps[5][:, 0:pairs])
                nc.vector.tensor_copy(PT[:, 0:pairs, 1, :], ps[5][:, 256:256 + 128 * pairs].rearrange("p (n t) -> p n t", n=pairs)).then_inc(S["gm_dve"], 1)
                dve.wait_ge(S["gm_dve"], it + 1)

            def add_batch(it, sums):
                if sums is not None:
                    dve.wait_ge(S["acc_added"], sums)
                for c in range(4):
                    dve.wait_ge(S["comb_mm"], it * 4 + (c + 1))
                    part = acc[:, 512 * c:512 * c + 512]
                    tt(part, part, ps[sum_bank(c)][:, :], ALU.add).then_inc(S["acc_added"], 1)

            def add_shared():
                dve.wait_ge(S["acc_added"], n_it * 4)
                for a in range(2):
                    for hf in range(2):
                        dve.wait_ge(S["shd_done"], 2 * a + hf + 1)
                        part = acc[:, D * a + 512 * hf:D * a + 512 * hf + 512]
                        tt(part, part, ps[4 * a + hf][:, :], ALU.add).then_inc(S["acc_added"], 1)

            def batch(it, first=False):
                slots_out(it, NPAIR)
                dve.wait_ge(S["PG_ready"], it + 1)
                activate(it, 0)
                place(it + 1)
                place_gates(it + 1)
                activate(it, 1)
                gathered(it + 1, 0)
                y_left(it, 0)
                y_third(it, 0)
                y_left(it, 1)
                gathered(it + 1, 1)
                y_third(it, 1)
                add_batch(it, None if first else it * 4)

            dve.wait_ge(S["route_ready"], 1)
            n_it = dve.value_load(n_iter[0:1, :], min_val=NB, max_val=MAX_FULL)
            tail = dve.value_load(n_tail[0:1, :], min_val=0, max_val=1)
            dve.wait_ge(S["sh_T"], 2)
            batch(0, first=True)
            batch(1)
            with dve.Fori(2, n_it) as it:
                batch(it)
            with dve.If(tail > 0):
                slots_out(n_it, 1)
                activate(n_it, 0)
                y_left(n_it, 0)
                y_third(n_it, 0)
            add_shared()
            with dve.If(tail > 0):
                add_batch(n_it, n_it * 4 + 4)


_INS = ["x", "g_mix", "w_in", "lam_re", "lam_im", "b_re", "b_im", "c_re", "c_im", "d_skip", "log_step", "w_glu",
        "b_glu", "g_q", "g_k", "g_out_ssm", "g_out_att", "w_out", "g_ffn", "w_router", "router_bias", "e_w1", "e_w3",
        "e_w2", "s_w1", "s_w3", "s_w2"]


def kernel(**inputs):
    import numpy as _np
    import concourse.bacc as _bacc
    from concourse import mybir as _mybir
    from concourse.bass_utils import run_bass_kernel_spmd as _run

    nc = _bacc.Bacc("TRN2", target_bir_lowering=False, num_devices=1)
    arrays, args = {}, {}
    for name in _INS:
        a = _np.ascontiguousarray(inputs[name])
        arrays[f"in_{name}"] = a
        args[name] = nc.dram_tensor(f"in_{name}", a.shape, _mybir.dt.from_np(a.dtype), kind="ExternalInput").ap()
    out = nc.dram_tensor("out_h", (1, T, D), FP32, kind="ExternalOutput").ap()
    build(nc, args, out)
    r = _run(nc, [arrays], core_ids=[0])
    return r.results[0]["out_h"]
```
